# Optimizing a Trainium2 kernel written in Bass

```python
import math
import jax, jax.numpy as jnp
from jax import lax
import numpy as np

D_MODEL = 1024
BATCH = 1
SEQ = 1024
DEPTH = 1

PLE_DIM = 256
D_MIX_SSD = D_MODEL
D_MIX_CONV = D_MODEL
D_MIX = D_MIX_SSD + D_MIX_CONV
SSD_HEAD_DIM = 64
SSD_HEADS = D_MIX_SSD // SSD_HEAD_DIM
SSD_GROUPS = 2
HEADS_PER_GROUP = SSD_HEADS // SSD_GROUPS
D_STATE = 64
SSD_CONV_W = 4
CHUNK = 128
SSD_CONV_DIM = D_MIX_SSD + 2 * SSD_GROUPS * D_STATE
SC_CONV_W = 3
IN_SPLITS = [SSD_CONV_DIM, SSD_HEADS, D_MIX_SSD, D_MIX_CONV, D_MIX_CONV, D_MIX_CONV, D_MIX_CONV]
IN_COLS = sum(IN_SPLITS)
EPS = 1e-6


def rmsnorm(x, w):
    xf = x.astype(jnp.float32)
    xf = xf * lax.rsqrt(jnp.mean(xf * xf, axis=-1, keepdims=True) + EPS)
    return (xf * w.astype(jnp.float32)).astype(x.dtype)

def causal_dwconv(u, w, b=None):
    k_w = w.shape[0]
    length = u.shape[1]
    up = jnp.pad(u, ((0, 0), (k_w - 1, 0), (0, 0)))
    y = up[:, 0:length] * w[0]
    for k in range(1, k_w):
        y = y + up[:, k:k + length] * w[k]
    if b is not None:
        y = y + b
    return y

def segsum(a):
    t = a.shape[-1]
    cs = jnp.cumsum(a, axis=-1)
    diff = cs[..., :, None] - cs[..., None, :]
    mask = jnp.tril(jnp.ones((t, t), dtype=bool))
    return jnp.where(mask, diff, -jnp.inf)

def ssd_chunked(x, dt, a, b_mat, c_mat, d_skip):
    bsz, length, _, _ = x.shape
    nc = length // CHUNK
    g, r, p, n = SSD_GROUPS, HEADS_PER_GROUP, SSD_HEAD_DIM, D_STATE
    xd = (x * dt[..., None]).reshape(bsz, nc, CHUNK, g, r, p)
    bc = b_mat.reshape(bsz, nc, CHUNK, g, n)
    cc = c_mat.reshape(bsz, nc, CHUNK, g, n)
    adt = (dt * a).reshape(bsz, nc, CHUNK, g, r).transpose(0, 3, 4, 1, 2)
    a_cs = jnp.cumsum(adt, axis=-1)
    decay_in = jnp.exp(segsum(adt))
    cb = jnp.einsum("bclgn,bcsgn->bgcls", cc, bc)
    y_diag = jnp.einsum("bgrcls,bcsgrp->bclgrp", cb[:, :, None] * decay_in, xd)
    decay_states = jnp.exp(a_cs[..., -1:] - a_cs).transpose(0, 3, 4, 1, 2)
    states = jnp.einsum("bclgn,bclgrp->bcgrpn", bc, xd * decay_states[..., None])
    init = jnp.zeros_like(states[:, :1])
    states = jnp.concatenate([init, states], axis=1)
    totals = jnp.pad(a_cs[..., -1], ((0, 0), (0, 0), (0, 0), (1, 0)))
    decay_chunk = jnp.exp(segsum(totals))
    new_states = jnp.einsum("bgrzc,bcgrpn->bzgrpn", decay_chunk, states)
    prev_states = new_states[:, :-1]
    decay_out = jnp.exp(a_cs).transpose(0, 3, 4, 1, 2)
    y_off = jnp.einsum("bclgn,bcgrpn->bclgrp", cc, prev_states) * decay_out[..., None]
    y = (y_diag + y_off).reshape(bsz, length, SSD_HEADS, p)
    return y + d_skip[:, None] * x

def hybrid_layer(x, p_i, norm_pre, norm_post, w_in, ssd_conv_w, ssd_conv_b, dt_bias,
                 a_log, d_skip, ssd_norm, sc_conv_w, w_out, w_ple_gate, w_ple_proj):
    bsz, length, _ = x.shape
    h = rmsnorm(x, norm_pre)
    proj = h @ w_in
    idx = list(np.cumsum(IN_SPLITS)[:-1])
    xbc, dt_raw, z_ssd, sc_h, sc_b, sc_c, z_sc = jnp.split(proj, idx, axis=-1)

    xbc = jax.nn.silu(causal_dwconv(xbc, ssd_conv_w, ssd_conv_b))
    xs, bm, cm = jnp.split(xbc, [D_MIX_SSD, D_MIX_SSD + SSD_GROUPS * D_STATE], axis=-1)
    xs = xs.reshape(bsz, length, SSD_HEADS, SSD_HEAD_DIM)
    bm = bm.reshape(bsz, length, SSD_GROUPS, D_STATE)
    cm = cm.reshape(bsz, length, SSD_GROUPS, D_STATE)
    dt = jax.nn.softplus(dt_raw + dt_bias)
    a = -jnp.exp(a_log)
    y_ssd = ssd_chunked(xs, dt, a, bm, cm, d_skip).reshape(bsz, length, D_MIX_SSD)
    yz = (y_ssd * jax.nn.silu(z_ssd)).reshape(bsz, length, SSD_GROUPS, D_MIX_SSD // SSD_GROUPS)
    y_ssd = rmsnorm(yz, ssd_norm.reshape(SSD_GROUPS, -1)).reshape(bsz, length, D_MIX_SSD)

    v = causal_dwconv(sc_c * sc_h, sc_conv_w)
    y_sc = sc_b * v * jax.nn.silu(z_sc)

    mix = jnp.concatenate([y_ssd, y_sc], axis=-1) @ w_out
    x = x + rmsnorm(mix, norm_post)

    gate = jax.nn.sigmoid(x @ w_ple_gate)
    return x + gate * (p_i @ w_ple_proj)

def first_inputs(seed: int = 0) -> dict:
    key = jax.random.key(seed)
    ks = jax.random.split(key, 16)
    f32 = jnp.float32
    x = jax.random.normal(ks[0], (BATCH, SEQ, D_MODEL), f32)
    p = jax.random.normal(ks[1], (DEPTH, BATCH, SEQ, PLE_DIM), f32)
    norm_pre = 1.0 + 0.05 * jax.random.normal(ks[2], (DEPTH, D_MODEL), f32)
    norm_post = 1.0 + 0.05 * jax.random.normal(ks[3], (DEPTH, D_MODEL), f32)
    w_in = jax.random.normal(ks[4], (DEPTH, D_MODEL, IN_COLS), f32) * D_MODEL ** -0.5
    ssd_conv_w = jax.random.normal(ks[5], (DEPTH, SSD_CONV_W, SSD_CONV_DIM), f32) * SSD_CONV_W ** -0.5
    ssd_conv_b = 0.02 * jax.random.normal(ks[6], (DEPTH, SSD_CONV_DIM), f32)
    dt0 = jnp.exp(jax.random.uniform(ks[7], (DEPTH, SSD_HEADS), f32,
                                     math.log(1e-3), math.log(1e-1)))
    dt_bias = dt0 + jnp.log(-jnp.expm1(-dt0))
    a_log = jnp.log(jax.random.uniform(ks[8], (DEPTH, SSD_HEADS), f32, 1.0, 16.0))
    d_skip = 1.0 + 0.05 * jax.random.normal(ks[9], (DEPTH, SSD_HEADS), f32)
    ssd_norm = 1.0 + 0.05 * jax.random.normal(ks[10], (DEPTH, D_MIX_SSD), f32)
    sc_conv_w = jax.random.normal(ks[11], (DEPTH, SC_CONV_W, D_MIX_CONV), f32) * SC_CONV_W ** -0.5
    w_out = jax.random.normal(ks[12], (DEPTH, D_MIX, D_MODEL), f32) * D_MIX ** -0.5
    w_ple_gate = jax.random.normal(ks[13], (DEPTH, D_MODEL, D_MODEL), f32) * D_MODEL ** -0.5
    w_ple_proj = jax.random.normal(ks[14], (DEPTH, PLE_DIM, D_MODEL), f32) * (0.5 * PLE_DIM ** -0.5)
    return {"x": x, "p": p, "norm_pre": norm_pre, "norm_post": norm_post, "w_in": w_in,
            "ssd_conv_w": ssd_conv_w, "ssd_conv_b": ssd_conv_b, "dt_bias": dt_bias,
            "a_log": a_log, "d_skip": d_skip, "ssd_norm": ssd_norm, "sc_conv_w": sc_conv_w,
            "w_out": w_out, "w_ple_gate": w_ple_gate, "w_ple_proj": w_ple_proj}

def first_block(x, p, norm_pre, norm_post, w_in, ssd_conv_w, ssd_conv_b, dt_bias, a_log,
              d_skip, ssd_norm, sc_conv_w, w_out, w_ple_gate, w_ple_proj):
    for i in range(DEPTH):
        x = hybrid_layer(x, p[i], norm_pre[i], norm_post[i], w_in[i], ssd_conv_w[i],
                         ssd_conv_b[i], dt_bias[i], a_log[i], d_skip[i], ssd_norm[i],
                         sc_conv_w[i], w_out[i], w_ple_gate[i], w_ple_proj[i])
    return x


SG_CHUNK = 128
SG_WIDTH = D_MODEL
SG_GROUPS = 8
SG_GROUP_DIM = SG_WIDTH // SG_GROUPS
GLA_HEADS = 4
GLA_KEY_DIM = D_MODEL // 2
GLA_VAL_DIM = D_MODEL
GLA_HEAD_K = GLA_KEY_DIM // GLA_HEADS
GLA_HEAD_V = GLA_VAL_DIM // GLA_HEADS
GLA_GATE_RANK = 16
GLA_GATE_TEMP = 16.0
GLA_CHUNK = 64
D_FF = 4 * D_MODEL
LN_EPS = 1e-5
DEEPNORM_ALPHA = (2.0 * DEPTH) ** 0.25
DEEPNORM_BETA = (8.0 * DEPTH) ** -0.25
SPLITS = (SG_WIDTH, SG_WIDTH, GLA_KEY_DIM, GLA_KEY_DIM, GLA_VAL_DIM, GLA_VAL_DIM,
          GLA_GATE_RANK, D_MODEL, D_MODEL)
D_IN = sum(SPLITS)
SPLIT_POINTS = [int(s) for s in np.cumsum(SPLITS)[:-1]]


def layer_norm(x, g, b):
    xf = x.astype(jnp.float32)
    mu = jnp.mean(xf, axis=-1, keepdims=True)
    var = jnp.mean(jnp.square(xf - mu), axis=-1, keepdims=True)
    y = (xf - mu) * lax.rsqrt(var + LN_EPS) * g.astype(jnp.float32) + b.astype(jnp.float32)
    return y.astype(x.dtype)

def spatial_gating(u, v, ln_g, ln_b, w_s, b_s):
    bsz, t, _ = v.shape
    n = t // SG_CHUNK
    u = jax.nn.gelu(u)
    v = layer_norm(jax.nn.gelu(v), ln_g, ln_b)
    vc = v.reshape(bsz, n, SG_CHUNK, SG_GROUPS, SG_GROUP_DIM)
    causal = jnp.tril(jnp.ones((SG_CHUNK, SG_CHUNK), dtype=bool))
    ws = jnp.where(causal[None], w_s, jnp.zeros_like(w_s))
    mixed = jnp.einsum('gts,bnsgd->bntgd', ws, vc) + jnp.transpose(b_s)[:, :, None]
    return u * mixed.reshape(bsz, t, SG_WIDTH)

def gla_chunked(q, k, v, log_f):
    bsz, t, h, dk = q.shape
    dv = v.shape[-1]
    n = t // GLA_CHUNK

    def to_chunks(a):
        return a.astype(jnp.float32).reshape(bsz, n, GLA_CHUNK, h, a.shape[-1]).transpose(1, 0, 3, 2, 4)

    qc, kc, vc, gc = to_chunks(q * (GLA_HEAD_K ** -0.5)), to_chunks(k), to_chunks(v), to_chunks(log_f)
    causal = jnp.tril(jnp.ones((GLA_CHUNK, GLA_CHUNK), dtype=bool))[:, :, None]

    def step(state, inp):
        qb, kb, vb, gb = inp
        cum = jnp.cumsum(gb, axis=-2)
        diff = cum[..., :, None, :] - cum[..., None, :, :]
        decay = jnp.exp(jnp.where(causal, diff, -jnp.inf))
        scores = jnp.einsum('bhtd,bhsd,bhtsd->bhts', qb, kb, decay)
        o_intra = jnp.einsum('bhts,bhsv->bhtv', scores, vb)
        o_inter = jnp.einsum('bhtd,bhdv->bhtv', qb * jnp.exp(cum), state)
        total = cum[..., -1, :]
        k_dec = kb * jnp.exp(total[..., None, :] - cum)
        new_state = jnp.exp(total)[..., None] * state + jnp.einsum('bhsd,bhsv->bhdv', k_dec, vb)
        return new_state, o_intra + o_inter

    s0 = jnp.zeros((bsz, h, dk, dv), dtype=jnp.float32)
    _, out = lax.scan(step, s0, (qc, kc, vc, gc))
    return out.transpose(1, 0, 3, 2, 4).reshape(bsz, t, h, dv)

def second_inputs(seed: int = 0) -> dict:
    key = jax.random.key(seed)
    ks = jax.random.split(key, 20)
    f32 = jnp.float32
    x = jax.random.normal(ks[0], (BATCH, SEQ, D_MODEL), f32)
    w_in = jax.random.normal(ks[1], (DEPTH, D_MODEL, D_IN), f32) * D_MODEL ** -0.5
    col_scale = np.ones((D_IN,), np.float32)
    col_scale[:2 * SG_WIDTH] = DEEPNORM_BETA
    v0 = 2 * SG_WIDTH + 2 * GLA_KEY_DIM
    col_scale[v0:v0 + GLA_VAL_DIM] = DEEPNORM_BETA
    w_in = w_in * jnp.asarray(col_scale)
    b_in = 0.02 * jax.random.normal(ks[2], (DEPTH, D_IN), f32)
    sg_ln_g = 1.0 + 0.05 * jax.random.normal(ks[3], (DEPTH, SG_WIDTH), f32)
    sg_ln_b = 0.02 * jax.random.normal(ks[4], (DEPTH, SG_WIDTH), f32)
    sg_w_s = 0.5 * jax.random.normal(ks[5], (DEPTH, SG_GROUPS, SG_CHUNK, SG_CHUNK), f32) * SG_CHUNK ** -0.5
    sg_b_s = 1.0 + 0.1 * jax.random.normal(ks[6], (DEPTH, SG_GROUPS, SG_CHUNK), f32)
    gla_w_gate2 = jax.random.normal(ks[7], (DEPTH, GLA_GATE_RANK, GLA_KEY_DIM), f32) * GLA_GATE_RANK ** -0.5
    gla_b_gate = 0.1 * jax.random.normal(ks[8], (DEPTH, GLA_KEY_DIM), f32)
    gla_norm_g = 1.0 + 0.05 * jax.random.normal(ks[9], (DEPTH, GLA_VAL_DIM), f32)
    w_out = jax.random.normal(ks[10], (DEPTH, D_MODEL, D_MODEL), f32) * (D_MODEL ** -0.5 * DEEPNORM_BETA)
    ln1_g = 1.0 + 0.05 * jax.random.normal(ks[11], (DEPTH, D_MODEL), f32)
    ln1_b = 0.02 * jax.random.normal(ks[12], (DEPTH, D_MODEL), f32)
    w_ff1 = jax.random.normal(ks[13], (DEPTH, D_MODEL, D_FF), f32) * (D_MODEL ** -0.5 * DEEPNORM_BETA)
    w_ff2 = jax.random.normal(ks[14], (DEPTH, D_FF, D_MODEL), f32) * (D_FF ** -0.5 * DEEPNORM_BETA)
    ln2_g = 1.0 + 0.05 * jax.random.normal(ks[15], (DEPTH, D_MODEL), f32)
    ln2_b = 0.02 * jax.random.normal(ks[16], (DEPTH, D_MODEL), f32)
    return {'x': x, 'w_in': w_in, 'b_in': b_in, 'sg_ln_g': sg_ln_g, 'sg_ln_b': sg_ln_b,
            'sg_w_s': sg_w_s, 'sg_b_s': sg_b_s, 'gla_w_gate2': gla_w_gate2, 'gla_b_gate': gla_b_gate,
            'gla_norm_g': gla_norm_g, 'w_out': w_out, 'ln1_g': ln1_g, 'ln1_b': ln1_b,
            'w_ff1': w_ff1, 'w_ff2': w_ff2, 'ln2_g': ln2_g, 'ln2_b': ln2_b}

def second_block(x, w_in, b_in, sg_ln_g, sg_ln_b, sg_w_s, sg_b_s, gla_w_gate2, gla_b_gate,
              gla_norm_g, w_out, ln1_g, ln1_b, w_ff1, w_ff2, ln2_g, ln2_b):
    bsz, t, _ = x.shape
    h = x
    for l in range(DEPTH):
        p = jnp.einsum('btd,de->bte', h, w_in[l]) + b_in[l]
        a_u, a_v, q, k, v, r, a_low, g_a, g_b = jnp.split(p, SPLIT_POINTS, axis=-1)
        y_a = spatial_gating(a_u, a_v, sg_ln_g[l], sg_ln_b[l], sg_w_s[l], sg_b_s[l])
        log_f = jax.nn.log_sigmoid((a_low @ gla_w_gate2[l] + gla_b_gate[l]).astype(jnp.float32)) / GLA_GATE_TEMP
        o = gla_chunked(q.reshape(bsz, t, GLA_HEADS, GLA_HEAD_K),
                        k.reshape(bsz, t, GLA_HEADS, GLA_HEAD_K),
                        v.reshape(bsz, t, GLA_HEADS, GLA_HEAD_V),
                        log_f.reshape(bsz, t, GLA_HEADS, GLA_HEAD_K))
        o = o * lax.rsqrt(jnp.mean(jnp.square(o), axis=-1, keepdims=True) + LN_EPS)
        y_b = (o.reshape(bsz, t, GLA_VAL_DIM) * gla_norm_g[l].astype(jnp.float32)).astype(h.dtype) * jax.nn.silu(r)
        m = jax.nn.sigmoid(g_a) * y_a + jax.nn.sigmoid(g_b) * y_b
        h = layer_norm(DEEPNORM_ALPHA * h + m @ w_out[l], ln1_g[l], ln1_b[l])
        f = jnp.square(jax.nn.relu(h @ w_ff1[l])) @ w_ff2[l]
        h = layer_norm(DEEPNORM_ALPHA * h + f, ln2_g[l], ln2_b[l])
    return h


def setup_inputs(seed=0):
    out = dict(first_inputs(seed))
    for name, value in second_inputs(seed + 1).items():
        if name != "x":
            out[name + "_2"] = value
    return out


def reference(
    x, p, norm_pre, norm_post, w_in, ssd_conv_w, ssd_conv_b, dt_bias, a_log, d_skip, ssd_norm,
    sc_conv_w, w_out, w_ple_gate, w_ple_proj, w_in_2, b_in_2, sg_ln_g_2, sg_ln_b_2, sg_w_s_2,
    sg_b_s_2, gla_w_gate2_2, gla_b_gate_2, gla_norm_g_2, w_out_2, ln1_g_2, ln1_b_2, w_ff1_2,
    w_ff2_2, ln2_g_2, ln2_b_2,
):
    x = first_block(
        x, p, norm_pre, norm_post, w_in, ssd_conv_w, ssd_conv_b, dt_bias, a_log, d_skip,
        ssd_norm, sc_conv_w, w_out, w_ple_gate, w_ple_proj,
    )
    return second_block(
        x, w_in_2, b_in_2, sg_ln_g_2, sg_ln_b_2, sg_w_s_2, sg_b_s_2, gla_w_gate2_2,
        gla_b_gate_2, gla_norm_g_2, w_out_2, ln1_g_2, ln1_b_2, w_ff1_2, w_ff2_2, ln2_g_2,
        ln2_b_2,
    )


_drawn_inputs = setup_inputs


def setup_inputs(seed=0):
    import zlib

    import numpy as np

    out = dict(_drawn_inputs(seed))
    spreads = {}
    factors = {'ssd_conv_b': 3.281,
     'b_in_2': 7.511,
     'sg_ln_g_2': 48.299,
     'sg_ln_b_2': 190.047,
     'sg_b_s_2': 5.615,
     'gla_b_gate_2': 7.908,
     'gla_norm_g_2': 6.191,
     'ln1_b_2': 2.819,
     'ln2_b_2': 2.738}
    for name, (base, spread) in spreads.items():
        noise = np.random.default_rng([zlib.crc32(name.encode()), seed]).standard_normal(out[name].shape)
        drawn = base * np.exp(spread * noise) if base else spread * noise
        out[name] = __import__('jax').numpy.asarray(drawn.astype(out[name].dtype))
    for name, factor in factors.items():
        out[name] = (out[name] * factor).astype(out[name].dtype)
    return out
```

```python
import math
from contextlib import ExitStack

import numpy as np

import concourse.bass as bass
from concourse import mybir

P = 128
T = 1024
D = 1024
KT = D // P
C = T // P
HALF = 512
HEADS, HP, GROUPS, NS = 16, 64, 2, 64
HG = HEADS // GROUPS
XBC_T = (D + 2 * GROUPS * NS) // P
CW, SW = 4, 3
GH, GK, GV = 4, 128, 256
RANK = 16
FF_BLOCKS = 4
EPS1, EPS2 = 1e-6, 1e-5
ALPHA = 2.0 ** 0.25
Q_SCALE = GK ** -0.5
TEMP = 16.0
LEVELS = [64, 32, 16, 8, 4, 2, 1]

VCOLS = [("norm_pre", 8), ("norm_post", 8), ("conv_w", CW * XBC_T), ("conv_b", XBC_T), ("d_skip", 8),
         ("ssd_norm", 8), ("sc_w", SW * 8), ("b_u", 8), ("b_v", 8), ("b_qk", 8), ("b_val", 8), ("b_r", 8),
         ("b_ga", 8), ("b_gb", 8), ("sg_g", 8), ("sg_b", 8), ("gn", 8), ("ln1_g", 8), ("ln1_b", 8),
         ("ln2_g", 8), ("ln2_b", 8)]
VOFF, _n = {}, 0
for _name, _w in VCOLS:
    VOFF[_name] = _n
    _n += _w
NV = _n
HOFF = {}
for _name in ("half_ga", "half_r", "half_gb", "half_gn", "half_rgn", "qk_s", "qk_b"):
    HOFF[_name] = _n
    _n += 8
NVH = _n

S_PLE, N_PLE = 0, 0
S_XBC, N_XBC = 2, 8
S_SC, N_SC = 12, 18
S_SB, N_SB = 44, 50
S_OUT, N_OUT = 52, 58
S_GATE, N_GATE = 68, 66
S_AV, N_AV = 76, 74
S_QK, N_QK = 84, 82
S_VAL, N_VAL = 92, 90
S_G, N_G = 100, 98
S_U, N_U = 124, 122
S_OUT2, N_OUT2 = 132, 130
S_FF, N_FF = 140, 138
S_ALL = S_FF + FF_BLOCKS * 16


class Chain:

    def __init__(self, eng, sem):
        self.eng, self.sem, self.base, self.n = eng, sem, 0, 0

    def __call__(self, ins):
        self.n += 1
        ins.then_inc(self.sem, 1)
        self.eng.wait_ge(self.sem, self.base + self.n)

    def enter(self, i, per):
        self.start, self.per = self.base + self.n, per
        self.base, self.n = self.start + i * per, 0

    def leave(self, times):
        assert self.n == self.per, (self.n, self.per)
        self.base, self.n = self.start + times * self.per, 0


def two_blocks_kernel(nc, xT, pT, ws, w_dt, w_low, vecs, dt_bias, a_log, b_low, w_gate2, b_gate,
                      sg_w, sg_bs, outT):
    f32, f32r = mybir.dt.float32, mybir.dt.float32r
    u32, i32 = mybir.dt.uint32, mybir.dt.int32
    ALU, ACT = mybir.AluOpType, mybir.ActivationFunctionType
    ds = bass.ds
    ctx = ExitStack()

    BASE = 16512
    W0 = BASE
    A0, A1 = W0 + 24576, W0 + 24576 + 32768
    R2 = A1 + 32768
    R3 = R2 + 32768
    R1 = R3 + 32768
    BC = R1 + 32768
    EAo, EBo, ECo = BC + 8192, BC + 12288, BC + 16384
    K0 = ECo + 4128
    assert K0 + 3904 <= 229344

    def at(name, shape, off, dt=f32):
        return nc.alloc_sbuf_tensor_at(name, [P] + shape, dt, offset=off)

    w_raw = at("w_raw", [2, 1024], W0)
    w_hi = at("w_hi", [2, 1024], W0 + 8192, f32r)
    w_lo = at("w_lo", [2, 1024], W0 + 16384, f32r)
    ea, eb, ec = at("ea", [1024], EAo), at("eb", [1024], EBo), at("ec", [1024], ECo)
    ebuf = at("ebuf", [2, 1024], EAo)
    tri = at("tri", [P], K0)
    ident = at("ident", [P], K0 + 512)
    vec = at("vec", [NVH], K0 + 1024)
    sm = at("sm", [64], K0 + 2240)
    ones = at("ones", [2], K0 + 2496)
    dec = at("dec", [P], K0 + 2560)
    assert 1024 + NVH * 4 <= 2240
    xh, xl = at("xh", [KT, T], A0, f32r), at("xl", [KT, T], A1, f32r)
    x_raw = at("x_raw", [KT, T], R1)
    p_raw, p_hi, p_lo = at("p_raw", [2, T], R2), at("p_hi", [2, T], R3, f32r), at("p_lo", [2, T], R3 + 8192, f32r)
    acc_a, acc_b = at("acc_a", [1024], BC), at("acc_b", [1024], BC + 4096)
    acc_g = at("acc_g", [2, 1024], R3 + 24576)
    raw_p = at("raw_p", [2, T + CW], R2 + 8192)
    conv_o = at("conv_o", [2, T], R2 + 16448)
    wdt_raw, wdt_hi, wdt_lo = (at("wdt_raw", [KT, HEADS], R2 + 24640),
                               at("wdt_hi", [KT, HEADS], R2 + 25152, f32r), at("wdt_lo", [KT, HEADS], R2 + 25664, f32r))
    dtb, alr = at("dtb", [HEADS], R2 + 26176), at("alr", [HEADS], R2 + 26240)
    tmps = [at(f"tmp{i}", [P], R2 + 26304 + 512 * i) for i in range(8)]
    adt = at("adt", [C, HEADS], R2 + 30400)
    dtf = at("dtf", [T], R2)
    acs_row = at("acs_row", [P], R2 + 30912)
    xbc = at("xbc", [XBC_T, T], R1)
    rowb = at("rowb", [HEADS, P], R3)
    st = at("st", [XBC_T, P], R3 + 8192)
    xd = at("xd", [HEADS, HP], R3 + 13312)
    xdd = at("xdd", [HEADS, HP], R3 + 17408)
    ce = at("ce", [HG, P], R3 + 21504)
    bt = at("bt", [P], R3 + 25600)
    cbm = at("cbm", [GROUPS, P], R3 + 26112)
    state = at("state", [HEADS, HP], R3 + 27136)
    dtt = at("dtt", [C, HEADS], R3 + 31232)
    acs = at("acs", [C, HEADS], R3 + 31744)
    et2 = at("et2", [C, HG], K0 + 3072)
    vbuf = at("vbuf", [KT, T], R2)
    ecp = at("ecp", [T + SW - 1], ECo)
    sh, sl = at("sh", [KT, T], R3, f32r), at("sl", [KT, T], R2, f32r)
    yh, yl = at("yh", [KT, T], A0, f32r), at("yl", [KT, T], R1, f32r)
    mm = at("mm", [KT, T], A1)
    xres = x_raw
    h2, l2 = at("h2", [KT, T], R2, f32r), at("l2", [KT, T], R3, f32r)
    av = at("av", [C, D], A0)
    mix = at("mix", [KT, T], A1)
    wl_raw, wl_hi, wl_lo = (at("wl_raw", [KT, RANK], R1), at("wl_hi", [KT, RANK], R1 + 512, f32r),
                            at("wl_lo", [KT, RANK], R1 + 1024, f32r))
    blow = at("blow", [1], R1 + 1536)
    wg2 = at("wg2", [GH * GK], R1 + 2048)
    alow = at("alow", [T], R1 + 4096)
    alc = at("alc", [2, P], R1 + 8192)
    wst = at("wst", [KT, P], R1 + 9216)
    rg = at("rg", [KT, P], R1 + 13312)
    ga_, ge_, gl_, gm_ = (at(f"gz{i}", [512], R1 + 17408 + 2048 * i) for i in range(4))
    cu_o = at("cu_o", [512], R1 + 25600)
    bnst, bnag = at("bnst", [2 * C, 6], R1 + 27648), at("bnag", [C, 2], R1 + 28160)
    vb = at("vb", [2, C, P], BC)
    G = A0
    qkc = at("qkc", [3, GH, P], G)
    vc = at("vc", [D], G + 6144)
    darg = at("darg", [2, 2, 256], G + 10240)
    kp = at("kp", [2, GH, P], G + 14336)
    qc = at("qc", [2, GH, 64], G + 18432)
    sc = at("sc", [GH, P], G + 20480)
    kd = at("kd", [GH, P], G + 22528)
    qe = at("qe", [GH, P], G + 24576)
    kdt = at("kdt", [GH, P], G + 26624)
    gst = at("gst", [GH, GV], G + 28672)
    oc = at("oc", [8, P], BC)
    osq = at("osq", [8, P], BC + 4096)
    lmask_f = at("lmask_f", [7, 64], R3 + 16384)
    lmask = at("lmask", [7, 64], K0 + 3328, mybir.dt.uint8)
    etot = at("etot", [GH], K0 + 2528)
    gbuf = at("gbuf", [KT, T], R1)
    mh, ml = at("mh", [KT, T], A0, f32r), at("ml", [KT, T], A1, f32r)
    yr = at("yr", [KT, T], R1)
    fh, fl = at("fh", [KT, T], A0, f32r), at("fl", [KT, T], A1, f32r)

    pt = ctx.enter_context(nc.psum_tensor("pt", [P, 2, 1024], f32))
    wk = ctx.enter_context(nc.psum_tensor("wk", [P, 4, HALF], f32))
    wka = wk[:, 0:2, :].rearrange("p b n -> p (b n)")
    wkb = wk[:, 2:4, :].rearrange("p b n -> p (b n)")

    pp_d = nc.dram_tensor("pp_d", [KT, P, T], f32, kind="Internal").ap()
    sz_d = nc.dram_tensor("sz_d", [KT, P, T], f32, kind="Internal").ap()
    acs_d = nc.dram_tensor("acs_d", [C, HEADS * P], f32, kind="Internal").ap()
    qk_d = nc.dram_tensor("qk_d", [KT, P, T], f32, kind="Internal").ap()
    cu_d = nc.dram_tensor("cu_d", [C, P, GH * P], f32, kind="Internal").ap()
    v_d = nc.dram_tensor("v_d", [C, P, D], f32, kind="Internal").ap()
    o_d = nc.dram_tensor("o_d", [KT, P, T], f32, kind="Internal").ap()

    def tile_of(dram, i):
        return dram[ds(i, 1), :, :].rearrange("a p n -> (a p) n")

    def row(t, i):
        return t[:, ds(i, 1), :].rearrange("p a t -> p (a t)")

    def sem(name):
        return ctx.enter_context(nc.semaphore(name))

    def V(name, i=0, n=1):
        off = VOFF[name] if name in VOFF else HOFF[name]
        return vec[:, ds(off + i, n)]

    w_loaded = [sem("w_loaded0"), sem("w_loaded1")]
    w_hi_done, w_split = sem("w_hi_done"), sem("w_split")
    mm_done = sem("mm_done")
    ple_done = sem("ple_done")
    evac_done = sem("evac_done")
    cst = sem("cst")
    x_in = [sem(f"x_in{k}") for k in range(KT)]
    p_in, vec_in, sml_in = sem("p_in"), sem("vec_in"), sem("sml_in")
    p_hi_done, p_lo_done = sem("p_hi_done"), sem("p_lo_done")
    pp_put = [sem("pp_put0"), sem("pp_put1")]
    sq_done, sq_used = sem("sq_done"), sem("sq_used")
    stat_done = sem("stat_done")
    rstd_done = sem("rstd_done")
    spread_done = sem("spread_done")
    val_done = sem("val_done")
    hi_done = sem("hi_done")
    lo_done = sem("lo_done")
    wdt_done = sem("wdt_done")
    dt_mm, dt_sb, dt_a, dt_b = sem("dt_mm"), sem("dt_sb"), sem("dt_a"), sem("dt_b")
    adt_done, acs_mm, acs_put = sem("adt_done"), sem("acs_mm"), sem("acs_put")
    acs_sb, dec_arg, dec_done = sem("acs_sb"), sem("dec_arg"), sem("dec_done")
    conv_done, silu_done = sem("conv_done"), sem("silu_done")
    stage_done, ssd_a, ssd_b = sem("stage_done"), sem("ssd_a"), sem("ssd_b")
    bt_done, row_in, ce_exp, e_arg, e_exp = sem("bt_done"), sem("row_in"), sem("ce_exp"), sem("e_arg"), sem("e_exp")
    ce_done, xdd_done, m_ready, y_evac, s_ready = sem("ce_done"), sem("xdd_done"), sem("m_ready"), sem("y_evac"), sem("s_ready")
    sz_done, sz_put, u_done, v_done = sem("sz_done"), sem("sz_put"), sem("u_done"), sem("v_done")
    sz_in, yz_done = [sem("sz_in0"), sem("sz_in1")], sem("yz_done")
    ys_done = sem("ys_done")
    pp_in = [sem("pp_in0"), sem("pp_in1")]
    b2_in = sem("b2_in")
    tr_done, tr_used = sem("tr_done"), sem("tr_used")
    wl_done = sem("wl_done")
    low_mm, low_done = sem("low_mm"), sem("low_done")
    alc_done, z_mm, z_act, z_dve, z_min = sem("alc_done"), sem("z_mm"), sem("z_act"), sem("z_dve"), sem("z_min")
    cu_mm, cu_done, cu_put = sem("cu_mm"), sem("cu_done"), sem("cu_put")
    qk_put = [sem("qk_put0"), sem("qk_put1")]
    v_put = [sem("v_put0"), sem("v_put1")]
    bn_done, av_done = sem("bn_done"), sem("av_done")
    ws_done, row_mm, rg_done, mix_mm, mix_done = sem("ws_done"), sem("row_mm"), sem("rg_done"), sem("mix_mm"), sem("mix_done")
    ch_in = sem("ch_in")
    arg_done, lev_exp, lev_ready, lev_mm, lev_used = sem("arg_done"), sem("lev_exp"), sem("lev_ready"), sem("lev_mm"), sem("lev_used")
    dg_mm, sc_done, end_exp, end_arg, kd_done = (sem("dg_mm"), sem("sc_done"), sem("end_exp"), sem("end_arg"),
                                                 sem("kd_done"))
    kdt_mm, kdt_done, o_mm, su_mm, gst_done = sem("kdt_mm"), sem("kdt_done"), sem("o_mm"), sem("su_mm"), sem("gst_done")
    o_act, o_stat, o_rstd, o_spread, on_done, o_put = (sem("o_act"), sem("o_stat"), sem("o_rstd"), sem("o_spread"),
                                                      sem("on_done"), sem("o_put"))
    ga_done, r_done, gb_done = sem("ga_done"), sem("r_done"), sem("gb_done")
    o_in, m_done = sem("o_in"), sem("m_done")
    y_done, a_used = sem("y_done"), sem("a_used")
    ln_done, h_done = sem("ln_done"), sem("h_done")
    f_sq, f_hi, f_lo, f_acc, f_zero = sem("f_sq"), sem("f_hi"), sem("f_lo"), sem("f_acc"), sem("f_zero")
    out_ready, out_put = sem("out_ready"), sem("out_put")
    d_chain, a_chain, p_chain = sem("d_chain"), sem("a_chain"), sem("p_chain")

    block = ctx.enter_context(nc.Block())

    @block.sync
    def _(sp):
        for u in range(2):
            sp.dma_start(w_raw[:, u, :], ws[u, :, :]).then_inc(w_loaded[u], 16)
        with sp.Fori(1, S_ALL // 2) as j:
            for u in range(2):
                tile = sp.snap(j * 2 + u)
                sp.wait_ge(w_split, j * 2 + u - 1)
                sp.dma_start(w_raw[:, u, :], tile_of(ws, tile)).then_inc(w_loaded[u], 16)

    @block.gpsimd
    def _(pool):
        link = Chain(pool, p_chain)
        link(nc.gpsimd.memset(ones[:, 0:1], 1.0))
        link(nc.gpsimd.memset(ones[:, 1:2], 0.0))
        link(nc.gpsimd.memset(ident[:], 0.0))
        link(nc.gpsimd.memset(tri[:], 1.0))
        link(nc.gpsimd.affine_select(out=ident[:], in_=ident[:], compare_op=ALU.not_equal, fill=1.0, base=0,
                                     pattern=[[-1, P]], channel_multiplier=1))
        nc.gpsimd.affine_select(out=tri[:], in_=tri[:], compare_op=ALU.is_ge, fill=0.0, base=0,
                                pattern=[[1, P]], channel_multiplier=-1).then_inc(cst, 1)

        def split(u, loaded):
            pool.wait_ge(w_loaded[u], loaded)
            zeros = ones[:, 1:2].to_broadcast([P, 1024])
            nc.gpsimd.tensor_tensor(out=w_hi[:, u, :], in0=w_raw[:, u, :], in1=zeros, op=ALU.add).then_inc(w_hi_done, 1)

        def rest(u, n):
            pool.wait_ge(w_hi_done, n)
            nc.gpsimd.tensor_tensor(out=w_lo[:, u, :], in0=w_raw[:, u, :], in1=w_hi[:, u, :].bitcast(f32),
                                    op=ALU.subtract).then_inc(w_split, 1)

        for u in range(2):
            split(u, 16)
            rest(u, u + 1)
        for n, m in enumerate(LEVELS):
            v = lmask_f[:, n, :].rearrange("p (b r) -> p b r", r=m)
            link(nc.gpsimd.memset(lmask_f[:, n, :], 1.0))
            link(nc.gpsimd.affine_select(out=v, in_=v, compare_op=ALU.is_ge, fill=0.0, base=0,
                                         pattern=[[-2 * m, 64 // m], [0, m]], channel_multiplier=1))
            nc.gpsimd.affine_select(out=v, in_=v, compare_op=ALU.is_ge, fill=0.0, base=m - 1,
                                    pattern=[[2 * m, 64 // m], [0, m]], channel_multiplier=-1).then_inc(cst, 1)
        with pool.Fori(1, S_ALL // 2) as j:
            for u in range(2):
                pool.wait_ge(mm_done, j * 2 + u - 1)
                split(u, j * 16 + 16)
                rest(u, j * 2 + u + 1)

    @block.scalar
    def _(act):
        A = nc.scalar.activation
        link = Chain(act, a_chain)
        act.dma_start(p_raw[:], pT.rearrange("(k p) t -> p k t", p=P)).then_inc(p_in, 16)
        act.dma_start(vec[:, 0:NV], vecs).then_inc(vec_in, 16)
        for k in range(KT):
            act.dma_start(x_raw[:, k, :], xT[k * P:(k + 1) * P, :]).then_inc(x_in[k], 16)
        act.dma_start(wdt_raw[:], w_dt.rearrange("(k p) h -> p k h", p=P)).then_inc(sml_in, 16)
        act.dma_start(dtb[:], dt_bias.to_broadcast([P, HEADS])).then_inc(sml_in, 16)
        act.dma_start(alr[:], a_log.to_broadcast([P, HEADS])).then_inc(sml_in, 16)

        act.wait_ge(p_in, 16)
        for k in range(2):
            A(p_hi[:, k, :], p_raw[:, k, :], ACT.Copy).then_inc(p_hi_done, 1)

        for k in range(KT):
            act.wait_ge(x_in[k], 16)
            if k:
                act.wait_ge(sq_used, k)
            A(ec[:], x_raw[:, k, :], ACT.Square).then_inc(sq_done, 1)
            act.wait_ge(ple_done, k + 1)
            if k >= 2:
                act.wait_ge(pp_put[k % 2], 16 * (k // 2))
            A(ebuf[:, k % 2, :], pt[:, k % 2, :], ACT.Copy, scale=0.5).then_inc(evac_done, 1)
            act.wait_ge(evac_done, k + 1)
            act.dma_start(pp_d[k, :, :], ebuf[:, k % 2, :]).then_inc(pp_put[k % 2], 16)
        act.wait_ge(sml_in, 48)
        A(wdt_hi[:], wdt_raw[:], ACT.Copy).then_inc(wdt_done, 1)
        for k in range(KT):
            act.wait_ge(val_done, k + 1)
            A(xh[:, k, :], x_raw[:, k, :], ACT.Copy).then_inc(hi_done, 1)

        def xbc_pair(j):
            for u in range(2):
                act.wait_ge(mm_done, j * 2 + (S_XBC + u + 1))
                act.wait_ge(conv_done, j * 2)
                A(raw_p[:, u, CW - 1:CW - 1 + T], pt[:, u, :], ACT.Copy).then_inc(evac_done, 1)
            for u in range(2):
                act.wait_ge(conv_done, j * 2 + (u + 1))
                A(row(xbc, j * 2 + u), conv_o[:, u, :], ACT.Silu).then_inc(silu_done, 1)

        act.wait_ge(lo_done, KT)
        xbc_pair(0)
        act.wait_ge(dt_mm, 1)
        A(dtf[0:HEADS, :], wka[0:HEADS, :], ACT.Copy).then_inc(dt_sb, 1)
        xbc_pair(1)
        v, r_, e_, u_, l_ = tmps[0], tmps[1], tmps[2], tmps[3], tmps[4]
        act.wait_ge(dt_a, 1)
        link(A(l_[:], v[:], ACT.Abs))
        A(e_[:], l_[:], ACT.Exp, scale=-1.0).then_inc(dt_b, 1)
        A(alr[:], alr[:], ACT.Exp).then_inc(dt_b, 1)
        act.wait_ge(dt_a, 2)
        A(l_[:], u_[:], ACT.Ln).then_inc(dt_b, 1)

        with act.Fori(2, XBC_T // 2 - 1) as j:
            xbc_pair(j)

        act.wait_ge(acs_mm, 1)
        A(acs[:], wk[:, 3, 0:P].rearrange("p (c h) -> p c h", c=C), ACT.Copy).then_inc(acs_sb, 1)
        A(acs_row[:], wk[:, 3, 2 * P:3 * P], ACT.Copy).then_inc(acs_sb, 1)
        act.wait_ge(acs_sb, 2)
        act.dma_start(acs_d.rearrange("c (h l) -> (c h) l", h=HEADS), acs_row[:]).then_inc(acs_put, 16)
        tot = wk[:, 3, P:2 * P].rearrange("p (c h) -> p c h", c=C)
        A(et2[0:64], tot[0:64, :, 0:HG], ACT.Exp).then_inc(dec_done, 1)
        A(et2[64:128], tot[64:128, :, HG:HEADS], ACT.Exp).then_inc(dec_done, 1)
        act.wait_ge(dec_arg, 1)
        A(dec[:], dec[:], ACT.Exp).then_inc(dec_done, 1)
        act.wait_ge(acs_put, 16)
        xbc_pair(XBC_T // 2 - 1)
        act.wait_ge(silu_done, XBC_T)

        act.wait_ge(pp_put[0], 64)
        act.wait_ge(pp_put[1], 64)
        with act.Fori(0, C) as j:
            S, N = S_SC + j * 4, N_SC + j * 4
            row_src = acs_d[ds(j, 1), :].to_broadcast([P, HEADS * P])
            act.wait_ge(ssd_b, j)
            act.dma_start(rowb[:].rearrange("p h l -> p (h l)"), row_src).then_inc(row_in, 16)
            act.wait_ge(y_evac, j)
            A(st[:], xbc[:, :, ds(j * P, P)], ACT.Copy).then_inc(stage_done, 1)
            act.wait_ge(row_in, j * 16 + 16)
            A(ce[0:64], rowb[0:64, 0:HG, :], ACT.Exp).then_inc(ce_exp, 1)
            A(ce[64:128], rowb[64:128, HG:HEADS, :], ACT.Exp).then_inc(ce_exp, 1)
            act.wait_ge(e_arg, j + 1)
            A(rowb[:], rowb[:], ACT.Exp).then_inc(e_exp, 1)
            act.wait_ge(mm_done, S + 1)
            act.wait_ge(v_done, j)
            A(ea[:], pt[:, 0, :], ACT.Copy, scale=0.5)
            A(eb[:], pt[:, 0, :], ACT.Tanh, scale=0.5).then_inc(evac_done, 1)
            act.wait_ge(ssd_a, j + 1)
            A(bt[:], wk[:, 2, 0:P], ACT.Copy).then_inc(bt_done, 1)
            act.wait_ge(mm_done, S + 2)
            act.wait_ge(sz_done, j + 1)
            act.dma_start(tile_of(sz_d, j), eb[:]).then_inc(sz_put, 16)
            A(ea[:], pt[:, 1, :], ACT.Copy).then_inc(evac_done, 1)
            act.wait_ge(mm_done, S + 3)
            act.wait_ge(sz_put, j * 16 + 16)
            A(eb[:], pt[:, 0, :], ACT.Copy).then_inc(evac_done, 1)
            act.wait_ge(mm_done, S + 4)
            act.wait_ge(u_done, j + 1)
            A(ea[:], pt[:, 1, :], ACT.Copy, scale=0.5)
            A(eb[:], pt[:, 1, :], ACT.Tanh, scale=0.5).then_inc(evac_done, 1)

        act.wait_ge(v_done, C)
        act.dma_start(eb[:], sz_d[0, :, :]).then_inc(sz_in[0], 16)

        def gated(i):
            if i + 1 < KT:
                if i:
                    act.wait_ge(yz_done, i)
                act.dma_start((ec if i % 2 == 0 else eb)[:], sz_d[i + 1, :, :]).then_inc(sz_in[(i + 1) % 2], 16)
            act.wait_ge(yz_done, i + 1)
            act.wait_ge(sq_used, KT + i)
            A(acc_b[:], xbc[:, i, :], ACT.Square).then_inc(sq_done, 1)

        def branch_high(i):
            act.wait_ge(mm_done, S_SB + i + 1)
            act.wait_ge(ys_done, i)
            A(ea[:], pt[:, i % 2, :], ACT.Copy).then_inc(evac_done, 1)
            act.wait_ge(ys_done, i + 1)
            A(sh[:, i, :], vbuf[:, i, :], ACT.Copy).then_inc(hi_done, 1)

        for i in range(KT):
            gated(i)
            if i in (3, 5):
                branch_high((i - 3) // 2)
        for i in range(2, KT):
            branch_high(i)

        act.wait_ge(mm_done, S_OUT)
        for i in range(KT):
            act.wait_ge(val_done, KT + i + 1)
            A(yh[:, i, :], xbc[:, i, :], ACT.Copy).then_inc(hi_done, 1)
        with act.Fori(0, KT // 2) as j:
            for u in range(2):
                n = j * 2 + u
                act.wait_ge(mm_done, S_OUT + 2 * n + 2)
                A(mm[:, ds(n, 1), :].rearrange("p a t -> p (a t)"), pt[:, u, :], ACT.Copy)
                act.wait_ge(sq_used, 2 * KT + n)
                A(eb[:], pt[:, u, :], ACT.Square).then_inc(evac_done, 1)
        for k in range(KT):
            act.dma_start(x_raw[:, k, :], xT[k * P:(k + 1) * P, :]).then_inc(x_in[k], 16)
        for k in range(KT):
            act.wait_ge(val_done, 2 * KT + k + 1)
            A(xh[:, k, :], xres[:, k, :], ACT.Copy).then_inc(hi_done, 1)

        with act.Fori(0, KT // 2) as j:
            for u in range(2):
                i = j * 2 + u
                act.wait_ge(val_done, 3 * KT + i)
                act.dma_start(eb[:], tile_of(pp_d, i)).then_inc(pp_in[u], 16)
                act.wait_ge(mm_done, S_GATE + i + 1)
                A(ea[:], pt[:, u, :], ACT.Tanh, scale=0.5).then_inc(evac_done, 1)
                act.wait_ge(val_done, 3 * KT + i + 1)
                A(h2[:, ds(i, 1), :], xres[:, ds(i, 1), :], ACT.Copy).then_inc(hi_done, 1)

        act.wait_ge(lo_done, 5 * KT)
        act.dma_start(wl_raw[:], w_low.rearrange("(k p) h -> p k h", p=P)).then_inc(b2_in, 16)
        act.dma_start(blow[0:RANK, :], b_low).then_inc(b2_in, 16)
        act.dma_start(wg2[0:RANK, :], w_gate2).then_inc(b2_in, 16)
        act.dma_start(wg2[RANK:RANK + 1, :], b_gate).then_inc(b2_in, 16)
        act.dma_start(wst[:], sg_w).then_inc(b2_in, 16)
        act.dma_start(rg[:].rearrange("p g t -> p (g t)"), sg_bs.to_broadcast([P, D])).then_inc(b2_in, 16)
        act.wait_ge(b2_in, 96)
        A(wl_hi[:], wl_raw[:], ACT.Copy).then_inc(wl_done, 1)
        with act.Fori(0, KT // 2) as j:
            for u in range(2):
                i = j * 2 + u
                act.wait_ge(mm_done, S_AV + i + 1)
                act.wait_ge(tr_done, j * 2)
                A(ebuf[:, u, :], pt[:, u, :], ACT.Gelu_apprx_tanh, bias=V("b_v", i)).then_inc(evac_done, 1)
        act.wait_ge(low_mm, 1)
        act.wait_ge(wl_done, 3)
        A(alow[0:RANK, :], wkb[0:RANK, :], ACT.Identity, bias=blow[0:RANK, :]).then_inc(low_done, 1)
        act.wait_ge(low_done, 1)
        act.wait_ge(tr_done, KT)
        A(alc[0:RANK + 1, 0, :], alow[0:RANK + 1, 0:P], ACT.Copy).then_inc(alc_done, 1)
        with act.Fori(0, KT // 2) as j:
            for u in range(2):
                i = j * 2 + u
                act.wait_ge(z_mm, i + 1)
                act.wait_ge(z_dve, i)
                A(ga_[:], wk[:, 0, :], ACT.Abs).then_inc(z_act, 1)
                act.wait_ge(z_act, i * 3 + 1)
                A(ge_[:], ga_[:], ACT.Exp, scale=-1.0).then_inc(z_act, 1)
                act.wait_ge(z_act, i * 3 + 2)
                A(gl_[:], ge_[:], ACT.Ln, bias=ones[:, 0:1]).then_inc(z_act, 1)
                A(alc[0:RANK + 1, 1 - u, :], alow[0:RANK + 1, ds((i + 1) % C * P, P)], ACT.Copy).then_inc(alc_done, 1)
                act.wait_ge(mm_done, S_QK + i + 1)
                act.wait_ge(qk_put[u], j * 16)
                A(ebuf[:, u, :], pt[:, u, :], ACT.Identity, scale=V("qk_s", i), bias=V("qk_b", i)).then_inc(evac_done, 1)
                act.wait_ge(evac_done, N_QK + i + 1)
                act.dma_start(tile_of(qk_d, i), ebuf[:, u, :]).then_inc(qk_put[u], 16)
                act.wait_ge(cu_mm, i + 1)
                act.wait_ge(cu_put, i * 16)
                A(cu_o[:], wk[:, 1, :], ACT.Copy, scale=1.0 / TEMP).then_inc(cu_done, 1)
                act.wait_ge(cu_done, i + 1)
                act.dma_start(tile_of(cu_d, i), cu_o[:]).then_inc(cu_put, 16)
        act.wait_ge(qk_put[0], 64)
        act.wait_ge(qk_put[1], 64)
        act.wait_ge(cu_put, 128)
        with act.Fori(0, KT // 2) as j:
            for u in range(2):
                i = j * 2 + u
                act.wait_ge(mm_done, S_VAL + i + 1)
                act.wait_ge(tr_done, j * 2 + KT)
                A(ebuf[:, u, :], pt[:, u, :], ACT.Identity, bias=V("b_val", i)).then_inc(evac_done, 1)
            for u in range(2):
                i = j * 2 + u
                act.wait_ge(tr_used, KT + i + 1)
                act.dma_start(v_d.rearrange("c p f -> p c f")[:, :, ds(i * P, P)], vb[:, u, :, :]).then_inc(v_put[u], 16)
        act.wait_ge(v_put[0], 64)
        act.wait_ge(v_put[1], 64)
        act.wait_ge(mix_mm, KT)

        def load_chunk(i):
            act.dma_start(qkc[:, 0:2, :, :].rearrange("p a h t -> p (a h) t"),
                          qk_d.rearrange("i p t -> p i t")[:, :, ds(i * P, P)]).then_inc(ch_in, 16)
            act.dma_start(qkc[:, 2, :, :].rearrange("p h t -> p (h t)"), tile_of(cu_d, i)).then_inc(ch_in, 16)
            act.dma_start(vc[:], tile_of(v_d, i)).then_inc(ch_in, 16)

        load_chunk(0)
        act.wait_ge(gst_done, 1)
        with act.Fori(0, C // 2) as j:
            for u in range(2):
                i = j * 2 + u
                S = S_G + j * 6 + 3 * u
                if_slot = [(u + n) % 2 for n in range(3)]
                act.wait_ge(ch_in, i * 48 + 48)
                act.wait_ge(gst_done, i + 1)
                A(qe[:], qkc[:, 2, :, :], ACT.Exp).then_inc(end_exp, 1)
                A(etot[:], qkc[:, 2, :, P - 1], ACT.Exp).then_inc(end_exp, 1)
                for n in range(7):
                    act.wait_ge(arg_done, i * 7 + n + 1)
                    A(darg[:, n % 2, :, :], darg[:, n % 2, :, :], ACT.Exp).then_inc(lev_exp, 1)
                    if n == 2:
                        act.wait_ge(end_arg, i + 1)
                        A(kd[:], kd[:], ACT.Exp).then_inc(end_exp, 1)
                    if n == 5:
                        act.wait_ge(mm_done, S + 1)
                        act.wait_ge(gb_done, i)
                        A(ea[:], pt[:, if_slot[0], :], ACT.Tanh, scale=0.5, bias=V("half_ga", i)).then_inc(evac_done, 1)
                act.wait_ge(mm_done, S + 2)
                A(eb[:], pt[:, if_slot[1], :], ACT.Identity, scale=V("half_gn", i), bias=V("half_rgn", i))
                A(ec[:], pt[:, if_slot[1], :], ACT.Tanh, scale=0.5, bias=V("half_r", i)).then_inc(evac_done, 1)
                act.wait_ge(kdt_mm, i + 1)
                A(kdt[:], wk[:, 3, :].rearrange("p (h t) -> p h t", h=GH), ACT.Copy).then_inc(kdt_done, 1)
                act.wait_ge(o_mm, i + 1)
                act.wait_ge(o_put, i * 16)
                A(oc[:], wka.rearrange("p (i t) -> p i t", i=8), ACT.Copy)
                A(osq[:], wka.rearrange("p (i t) -> p i t", i=8), ACT.Square).then_inc(o_act, 1)
                act.wait_ge(su_mm, i + 1)
                load_chunk((i + 1) % C)
                act.wait_ge(mm_done, S + 3)
                act.wait_ge(ga_done, i + 1)
                A(ea[:], pt[:, if_slot[2], :], ACT.Tanh, scale=0.5, bias=V("half_gb", i)).then_inc(evac_done, 1)
                act.wait_ge(on_done, i + 1)
                act.dma_start(o_d.rearrange("i p t -> p i t")[:, :, ds(i * P, P)], oc[:]).then_inc(o_put, 16)
        act.wait_ge(o_put, 128)
        act.wait_ge(gb_done, C)
        act.wait_ge(ch_in, (C + 1) * 48)

        with act.Fori(0, KT // 2) as j:
            for u in range(2):
                i = j * 2 + u
                act.wait_ge(lo_done, 5 * KT + i)
                act.dma_start(eb[:], tile_of(o_d, i)).then_inc(o_in, 16)
                act.wait_ge(mm_done, S_U + i + 1)
                A(ea[:], pt[:, u, :], ACT.Gelu_apprx_tanh, bias=V("b_u", i)).then_inc(evac_done, 1)
                act.wait_ge(m_done, i + 1)
                A(mh[:, ds(i, 1), :].rearrange("p a t -> p (a t)"), ea[:], ACT.Copy, scale=0.5).then_inc(hi_done, 1)
        act.wait_ge(lo_done, 6 * KT)
        with act.Fori(0, KT // 2) as j:
            for u in range(2):
                n = j * 2 + u
                act.wait_ge(mm_done, S_OUT2 + n + 1)
                act.wait_ge(y_done, n)
                A(ea[:], pt[:, u, :], ACT.Copy).then_inc(evac_done, 1)
                act.wait_ge(y_done, n + 1)
                act.wait_ge(a_used, n)
                A(eb[:], yr[:, ds(n, 1), :].rearrange("p a t -> p (a t)"), ACT.Square).then_inc(sq_done, 1)
        for k in range(KT):
            act.wait_ge(ln_done, k + 1)
            A(yr[:, k, :], ebuf[:, k % 2, :], ACT.Identity, scale=V("ln1_g", k), bias=V("ln1_b", k)).then_inc(h_done, 1)
            act.wait_ge(h_done, k + 1)
            A(h2[:, k, :], yr[:, k, :], ACT.Copy).then_inc(hi_done, 1)
        with act.Fori(0, FF_BLOCKS) as b:
            with act.Fori(0, KT // 2) as j:
                for u in range(2):
                    i = b * KT + j * 2 + u
                    act.wait_ge(mm_done, S_FF + b * 16 + j * 2 + u + 1)
                    act.wait_ge(f_lo, b * KT + j * 2)
                    A(ebuf[:, u, :], pt[:, u, :], ACT.Relu).then_inc(evac_done, 1)
                    act.wait_ge(f_sq, i + 1)
                    A(fh[:, ds(j * 2 + u, 1), :].rearrange("p a t -> p (a t)"), ebuf[:, u, :], ACT.Copy).then_inc(f_hi, 1)
            with act.Fori(0, KT // 2) as j:
                for u in range(2):
                    i = b * KT + j * 2 + u
                    act.wait_ge(mm_done, S_FF + b * 16 + 8 + j * 2 + u + 1)
                    act.wait_ge(f_lo, b * KT + KT)
                    act.wait_ge(f_acc, b * KT + j * 2 + KT)
                    A(ebuf[:, u, :], pt[:, u, :], ACT.Copy).then_inc(evac_done, 1)
                    act.wait_ge(f_acc, i + (KT + 1))
                    act.wait_ge(a_used, KT + i)
                    A(ec[:], yr[:, ds(j * 2 + u, 1), :].rearrange("p a t -> p (a t)"), ACT.Square).then_inc(sq_done, 1)
        for k in range(KT):
            act.wait_ge(ln_done, KT + k + 1)
            A(yr[:, k, :], ebuf[:, k % 2, :], ACT.Identity, scale=V("ln2_g", k), bias=V("ln2_b", k)).then_inc(h_done, 1)
            act.wait_ge(h_done, KT + k + 1)
            act.dma_start(outT[k * P:(k + 1) * P, :], yr[:, k, :]).then_inc(out_put, 16)
        act.wait_ge(out_put, KT * 16)

    @block.vector
    def _(dve):
        link = Chain(dve, d_chain)
        TT, TS, STT = nc.vector.tensor_tensor, nc.vector.tensor_scalar, nc.vector.scalar_tensor_tensor

        def rsqrt(y, v, t, done=None):
            link(TS(t.bitcast(i32), v.bitcast(i32), 1, None, ALU.arith_shift_right))
            link(TS(y.bitcast(i32), t.bitcast(i32), -1, 0x5f3759df, ALU.mult, ALU.add))
            for n in range(3):
                link(STT(out=t, in0=y, scalar=-0.5, in1=y, op0=ALU.mult, op1=ALU.mult))
                link(TT(out=t, in0=t, in1=v, op=ALU.mult))
                ins = STT(out=y, in0=t, scalar=1.5, in1=y, op0=ALU.add, op1=ALU.mult)
                if n < 2 or done is None:
                    link(ins)
                else:
                    ins.then_inc(done, 1)

        GLA_LINKS = 11

        link(nc.vector.memset(raw_p[:, :, 0:CW - 1], 0.0))
        dve.wait_ge(vec_in, 16)
        for k in range(2):
            dve.wait_ge(p_hi_done, k + 1)
            TT(out=p_lo[:, k, :], in0=p_raw[:, k, :], in1=p_hi[:, k, :].bitcast(f32), op=ALU.subtract).then_inc(p_lo_done, 1)
        dve.wait_ge(cst, 1 + len(LEVELS))
        link(nc.vector.tensor_copy(lmask[:], lmask_f[:]))
        for new, old in (("half_ga", "b_ga"), ("half_r", "b_r"), ("half_gb", "b_gb"), ("half_gn", "gn")):
            link(TS(V(new, 0, 8), V(old, 0, 8), 0.5, None, ALU.mult))
        link(TT(out=V("half_rgn", 0, 8), in0=V("half_gn", 0, 8), in1=V("b_r", 0, 8), op=ALU.mult))
        link(nc.vector.memset(V("qk_s", 0, 4), Q_SCALE))
        link(nc.vector.memset(V("qk_s", 4, 4), 1.0))
        link(TT(out=V("qk_b", 0, 8), in0=V("qk_s", 0, 8), in1=V("b_qk", 0, 8), op=ALU.mult))

        for k in range(KT):
            dve.wait_ge(sq_done, k + 1)
            if k == 0:
                nc.vector.tensor_copy(acc_a[:], ec[:]).then_inc(sq_used, 1)
            else:
                dve.wait_ge(sq_used, k)
                TT(out=acc_a[:], in0=acc_a[:], in1=ec[:], op=ALU.add).then_inc(sq_used, 1)

        def scale_of(eps, width):
            link(TS(sm[:, 8:16], wk[:, 3, 0:8], 1.0 / width, eps, ALU.mult, ALU.add))
            rsqrt(sm[:, 0:8], sm[:, 8:16], sm[:, 16:24], rstd_done)

        dve.wait_ge(stat_done, 1)
        scale_of(EPS1, D)
        dve.wait_ge(wdt_done, 1)
        TT(out=wdt_lo[:], in0=wdt_raw[:], in1=wdt_hi[:].bitcast(f32), op=ALU.subtract).then_inc(wdt_done, 1)
        dve.wait_ge(spread_done, 1)
        for k in range(KT):
            STT(out=x_raw[:, k, :], in0=x_raw[:, k, :], scalar=V("norm_pre", k), in1=wka, op0=ALU.mult,
                op1=ALU.mult).then_inc(val_done, 1)
            dve.wait_ge(hi_done, k + 1)
            TT(out=xl[:, k, :], in0=x_raw[:, k, :], in1=xh[:, k, :].bitcast(f32), op=ALU.subtract).then_inc(lo_done, 1)

        def conv_pair(j):
            for u in range(2):
                dve.wait_ge(evac_done, j * 2 + (N_XBC + u + 1))
                dve.wait_ge(silu_done, j * 2)
                link(TS(conv_o[:, u, :], raw_p[:, u, 0:T], V("conv_w", j * 2 + u), V("conv_b", j * 2 + u), ALU.mult, ALU.add))
                for k in range(1, CW):
                    ins = STT(out=conv_o[:, u, :], in0=raw_p[:, u, k:k + T], scalar=V("conv_w", j * 2 + (u + k * XBC_T)),
                              in1=conv_o[:, u, :], op0=ALU.mult, op1=ALU.add)
                    if k < CW - 1:
                        link(ins)
                    else:
                        ins.then_inc(conv_done, 1)

        conv_pair(0)
        conv_pair(1)
        v, r_, e_, u_, l_, z_, q_, g_ = tmps
        ch = lambda t: t[:].rearrange("p (c h) -> p c h", c=C)
        dve.wait_ge(dt_mm, 2)
        TT(out=ch(v), in0=wk[:, 3, 0:P].rearrange("p (c h) -> p c h", c=C),
           in1=dtb[:].unsqueeze(1).to_broadcast([P, C, HEADS]), op=ALU.add).then_inc(dt_a, 1)
        dve.wait_ge(dt_a, 1)
        link(TS(r_[:], v[:], 0.0, None, ALU.max))
        dve.wait_ge(dt_b, 1)
        TS(u_[:], e_[:], 1.0, None, ALU.add).then_inc(dt_a, 1)
        dve.wait_ge(dt_a, 2)
        link(TS(q_[:], u_[:], -1.0, None, ALU.add))
        link(TS(z_[:], q_[:], 0.0, None, ALU.is_equal))
        link(TT(out=q_[:], in0=q_[:], in1=z_[:], op=ALU.add))
        link(nc.vector.reciprocal(g_[:], q_[:]))
        link(TT(out=q_[:], in0=g_[:], in1=e_[:], op=ALU.mult))
        dve.wait_ge(dt_b, 3)
        link(TT(out=q_[:], in0=q_[:], in1=l_[:], op=ALU.mult))
        link(TT(out=z_[:], in0=z_[:], in1=e_[:], op=ALU.mult))
        link(TT(out=q_[:], in0=q_[:], in1=z_[:], op=ALU.add))
        link(TT(out=dtt[:], in0=ch(q_), in1=ch(r_), op=ALU.add))
        link(TS(alr[:], alr[:], -1.0, None, ALU.mult))
        TT(out=adt[:], in0=dtt[:], in1=alr[:].unsqueeze(1).to_broadcast([P, C, HEADS]), op=ALU.mult).then_inc(adt_done, 1)

        with dve.Fori(2, XBC_T // 2 - 1) as j:
            link.enter(j - 2, 2 * (CW - 1))
            conv_pair(j)
        link.leave(XBC_T // 2 - 3)

        dve.wait_ge(dec_done, 2)
        TT(out=dec[:], in0=wk[:, 3, P:2 * P], in1=acs[:].rearrange("p c h -> p (c h)"), op=ALU.subtract).then_inc(dec_arg, 1)
        conv_pair(XBC_T // 2 - 1)
        nc.vector.memset(state[:], 0.0)
        link(nc.vector.memset(ecp[:, 0:SW - 1], 0.0))
        dve.wait_ge(dec_done, 3)

        SC_LINKS = 7
        with dve.Fori(0, C) as j:
            link.enter(j, SC_LINKS)
            N = N_SC + j * 4
            dve.wait_ge(row_in, j * 16 + 16)
            dve.wait_ge(ce_exp, j * 2 + 2)
            for h in range(HEADS):
                ins = TS(rowb[:, h, :], rowb[:, h, :], acs[:].rearrange("p c h -> p (c h)")[:, ds(j * HEADS + h, 1)],
                         0.0, ALU.subtract, ALU.min)
            ins.then_inc(e_arg, 1)
            dve.wait_ge(ssd_a, j + 1)
            dts = dtt[:, ds(j, 1), :].rearrange("p a h -> p (a h)").unsqueeze(2).to_broadcast([P, HEADS, HP])
            link(TT(out=xd[:], in0=wka.rearrange("p (h q) -> p h q", h=HEADS), in1=dts, op=ALU.mult))
            decs = dec[:, ds(j * HEADS, HEADS)].unsqueeze(2).to_broadcast([P, HEADS, HP])
            TT(out=xdd[:], in0=xd[:], in1=decs, op=ALU.mult).then_inc(xdd_done, 1)
            dve.wait_ge(bt_done, j + 1)
            for g in range(GROUPS):
                cb_src = wk[:, 2, P:2 * P] if g == 0 else wk[:, 3, 0:P]
                ins = TT(out=cbm[:, g, :], in0=cb_src, in1=tri[:], op=ALU.mult)
            link(ins)
            TT(out=ce[:], in0=ce[:], in1=st[:, XBC_T - 1, :].unsqueeze(1).to_broadcast([P, HG, P]),
               op=ALU.mult).then_inc(ce_done, 1)
            dve.wait_ge(e_exp, j + 1)
            for g in range(GROUPS):
                ins = TT(out=rowb[:, g * HG:(g + 1) * HG, :], in0=rowb[:, g * HG:(g + 1) * HG, :],
                         in1=cbm[:, g, :].unsqueeze(1).to_broadcast([P, HG, P]), op=ALU.mult)
            ins.then_inc(m_ready, 1)
            dve.wait_ge(evac_done, N + 1)
            STT(out=eb[:], in0=eb[:], scalar=1.0, in1=ea[:], op0=ALU.add, op1=ALU.mult).then_inc(sz_done, 1)
            dve.wait_ge(ssd_b, j + 1)
            for i in range(KT):
                ins = STT(out=xbc[:, i, ds(j * P, P)], in0=st[:, i, :], scalar=V("d_skip", i),
                          in1=wka[:, i * P:(i + 1) * P], op0=ALU.mult, op1=ALU.add)
            ins.then_inc(y_evac, 1)
            for g in range(GROUPS):
                rows, hs = slice(g * 64, g * 64 + 64), slice(g * HG, (g + 1) * HG)
                ins = TT(out=state[rows, hs, :], in0=state[rows, hs, :],
                         in1=et2[rows, ds(j, 1), :].rearrange("p a h -> p (a h)").unsqueeze(2).to_broadcast([64, HG, HP]),
                         op=ALU.mult)
            link(ins)
            for g in range(GROUPS):
                rows, hs = slice(g * 64, g * 64 + 64), slice(g * HG, (g + 1) * HG)
                ins = TT(out=state[rows, hs, :], in0=state[rows, hs, :],
                         in1=wk[rows, 3, :].rearrange("p (h q) -> p h q", h=HG), op=ALU.add)
            ins.then_inc(s_ready, 1)
            dve.wait_ge(evac_done, N + 3)
            TT(out=ecp[:, SW - 1:SW - 1 + T], in0=ea[:], in1=eb[:], op=ALU.mult).then_inc(u_done, 1)
            dve.wait_ge(u_done, j + 1)
            vj = row(vbuf, j)
            link(TS(vj, ecp[:, 0:T], V("sc_w", j), None, ALU.mult))
            for k in range(1, SW):
                link(STT(out=vj, in0=ecp[:, k:k + T], scalar=V("sc_w", j + 8 * k), in1=vj, op0=ALU.mult, op1=ALU.add))
            dve.wait_ge(evac_done, N + 4)
            link(STT(out=ea[:], in0=eb[:], scalar=1.0, in1=ea[:], op0=ALU.add, op1=ALU.mult))
            TT(out=vj, in0=vj, in1=ea[:], op=ALU.mult).then_inc(v_done, 1)
        link.leave(C)

        dve.wait_ge(y_evac, C)
        def gated(i):
            acc = acc_g[:, i // 4, :]
            buf = eb if i % 2 == 0 else ec
            dve.wait_ge(sz_in[i % 2], 16 * (i // 2 + 1))
            TT(out=xbc[:, i, :], in0=xbc[:, i, :], in1=buf[:], op=ALU.mult).then_inc(yz_done, 1)
            if i:
                dve.wait_ge(sq_used, KT + i)
            dve.wait_ge(sq_done, KT + i + 1)
            if i % 4 == 0:
                nc.vector.tensor_copy(acc, acc_b[:]).then_inc(sq_used, 1)
            else:
                TT(out=acc, in0=acc, in1=acc_b[:], op=ALU.add).then_inc(sq_used, 1)

        def branch(i):
            dve.wait_ge(evac_done, N_SB + i + 1)
            TT(out=vbuf[:, i, :], in0=vbuf[:, i, :], in1=ea[:], op=ALU.mult).then_inc(ys_done, 1)
            dve.wait_ge(hi_done, KT + i + 1)
            TT(out=sl[:, i, :], in0=vbuf[:, i, :], in1=sh[:, i, :].bitcast(f32), op=ALU.subtract).then_inc(lo_done, 1)

        for i in range(KT):
            gated(i)
            if i in (3, 5):
                branch((i - 3) // 2)
        for i in range(2, 4):
            branch(i)
        dve.wait_ge(stat_done, 2)
        link(TS(sm[:, 16:32], wk[:, 3, 0:16], 2.0 / D, EPS1, ALU.mult, ALU.add))
        rsqrt(sm[:, 0:16], sm[:, 16:32], sm[:, 32:48], rstd_done)
        for i in range(4, 6):
            branch(i)
        dve.wait_ge(spread_done, 2)
        for i in range(KT):
            STT(out=xbc[:, i, :], in0=xbc[:, i, :], scalar=V("ssd_norm", i), in1=wka if i < 4 else wkb, op0=ALU.mult,
                op1=ALU.mult).then_inc(val_done, 1)
        for i in range(6, KT):
            branch(i)
        for i in range(KT):
            dve.wait_ge(hi_done, 2 * KT + i + 1)
            TT(out=yl[:, i, :], in0=xbc[:, i, :], in1=yh[:, i, :].bitcast(f32), op=ALU.subtract).then_inc(lo_done, 1)

        link(nc.vector.memset(acc_a[:], 0.0))
        with dve.Fori(0, KT // 2) as j:
            for u in range(2):
                n = j * 2 + u
                dve.wait_ge(evac_done, N_OUT + n + 1)
                dve.wait_ge(sq_used, 2 * KT + n)
                TT(out=acc_a[:], in0=acc_a[:], in1=eb[:], op=ALU.add).then_inc(sq_used, 1)
        dve.wait_ge(stat_done, 3)
        scale_of(EPS1, D)
        dve.wait_ge(spread_done, 3)
        for k in range(KT):
            link(STT(out=ebuf[:, k % 2, :], in0=mm[:, k, :], scalar=V("norm_post", k), in1=wka, op0=ALU.mult, op1=ALU.mult))
            dve.wait_ge(x_in[k], 32)
            TT(out=xres[:, k, :], in0=xres[:, k, :], in1=ebuf[:, k % 2, :], op=ALU.add).then_inc(val_done, 1)
            dve.wait_ge(hi_done, 3 * KT + k + 1)
            TT(out=xl[:, k, :], in0=xres[:, k, :], in1=xh[:, k, :].bitcast(f32), op=ALU.subtract).then_inc(lo_done, 1)
        with dve.Fori(0, KT // 2) as j:
            link.enter(j, 2)
            for u in range(2):
                i = j * 2 + u
                dve.wait_ge(evac_done, N_GATE + i + 1)
                dve.wait_ge(pp_in[u], j * 16 + 16)
                link(STT(out=ea[:], in0=ea[:], scalar=1.0, in1=eb[:], op0=ALU.add, op1=ALU.mult))
                TT(out=row(xres, i), in0=row(xres, i), in1=ea[:], op=ALU.add).then_inc(val_done, 1)
                dve.wait_ge(val_done, 3 * KT + i + 1)
                dve.wait_ge(hi_done, 4 * KT + i + 1)
                TT(out=row(l2, i), in0=row(xres, i), in1=row(h2, i).bitcast(f32), op=ALU.subtract).then_inc(lo_done, 1)
        link.leave(KT // 2)

        dve.wait_ge(b2_in, 96)
        dve.wait_ge(wl_done, 1)
        TT(out=wl_lo[:], in0=wl_raw[:], in1=wl_hi[:].bitcast(f32), op=ALU.subtract).then_inc(wl_done, 1)
        nc.vector.memset(alow[0:RANK + 1, :], 1.0).then_inc(wl_done, 1)
        TT(out=wst[:], in0=wst[:], in1=tri[:].unsqueeze(1).to_broadcast([P, KT, P]), op=ALU.mult).then_inc(ws_done, 1)
        with dve.Fori(0, KT // 2) as j:
            for u in range(2):
                i = j * 2 + u
                dve.wait_ge(tr_done, i + 1)
                nc.vector.tensor_copy(av[:, :, ds(i * P, P)], wka.rearrange("p (c f) -> p c f", c=C)).then_inc(tr_used, 1)
        dve.wait_ge(tr_used, KT)
        dve.wait_ge(row_mm, 1)
        for g in range(KT):
            ins = STT(out=rg[:, g, :], in0=wka[:, g * P:(g + 1) * P], scalar=V("sg_b", g), in1=rg[:, g, :],
                      op0=ALU.mult, op1=ALU.add)
        ins.then_inc(rg_done, 1)
        with dve.Fori(0, KT // 2) as j:
            link.enter(j, 2)
            for u in range(2):
                i = j * 2 + u
                dve.wait_ge(z_mm, i + 1)
                dve.wait_ge(z_dve, i)
                dve.wait_ge(cu_mm, i)
                dve.wait_ge(z_act, i * 3 + 1)
                link(TS(gm_[:], wk[:, 0, :], 0.0, None, ALU.min))
                dve.wait_ge(z_act, i * 3 + 3)
                TT(out=gm_[:], in0=gm_[:], in1=gl_[:], op=ALU.subtract).then_inc(z_dve, 1)
                for h in range(2):
                    ins = nc.vector.bn_stats(row(bnst, i * 2 + h), av[:, ds(i, 1), h * HALF:(h + 1) * HALF].rearrange("p a f -> p (a f)"))
                ins.then_inc(bn_done, 1)
        link.leave(KT // 2)
        dve.wait_ge(bn_done, C)
        for c in range(C):
            ins = nc.vector.bn_aggr(bnag[:, c, :], bnst[:, 2 * c:2 * c + 2, :].rearrange("p h s -> p (h s)"))
        link(ins)
        link(TS(sm[:, 8:16], bnag[:, :, 1], EPS2, None, ALU.add))
        rsqrt(sm[:, 0:8], sm[:, 8:16], sm[:, 16:24], rstd_done)
        dve.wait_ge(rstd_done, 4)
        link(STT(out=sm[:, 24:32], in0=bnag[:, :, 0], scalar=-1.0, in1=sm[:, 0:8], op0=ALU.mult, op1=ALU.mult))
        for c in range(C):
            TS(av[:, c, :], av[:, c, :], sm[:, c:c + 1], sm[:, 24 + c:25 + c], ALU.mult, ALU.add).then_inc(av_done, 1)
        with dve.Fori(0, KT // 2) as j:
            for u in range(2):
                i = j * 2 + u
                dve.wait_ge(tr_done, i + (KT + 1))
                dve.wait_ge(v_put[u], j * 16)
                nc.vector.tensor_copy(vb[:, u, :, :], wka.rearrange("p (c f) -> p c f", c=C)).then_inc(tr_used, 1)
        for g in range(KT):
            dve.wait_ge(mix_mm, g + 1)
            src = wka if g % 2 == 0 else wkb
            STT(out=mix[:, g, :].rearrange("p (c t) -> p c t", c=C), in0=src.rearrange("p (c t) -> p c t", c=C),
                scalar=V("sg_g", g), in1=rg[:, g, :].unsqueeze(1).to_broadcast([P, C, P]), op0=ALU.mult,
                op1=ALU.add).then_inc(mix_done, 1)

        link(nc.vector.memset(gst[:], 0.0))
        link(nc.vector.memset(sc[:], 0.0))
        link(nc.vector.memset(kp[:], 0.0))
        nc.vector.memset(qc[:], 0.0).then_inc(gst_done, 1)

        def second(ap, m):
            return ap.rearrange("p h (b two r) -> p (h b) two r", two=2, r=m)[:, :, 1, :]

        def first(ap, m):
            return ap.rearrange("p h (b two r) -> p (h b) two r", two=2, r=m)[:, :, 0, :]

        with dve.Fori(0, C // 2) as j:
            link.enter(j, 2 * GLA_LINKS)
            for u in range(2):
                i = j * 2 + u
                N = N_G + j * 6 + 3 * u
                q_, k_, c_ = qkc[:, 0, :, :], qkc[:, 1, :, :], qkc[:, 2, :, :]
                slots = [(u + n) % 2 for n in range(3)]

                def args(n):
                    m = LEVELS[n]
                    ref = c_.rearrange("p h (b two r) -> p (h b) two r", two=2, r=m)[:, :, 0, m - 1:m]
                    ref = ref.to_broadcast([P, 256 // m, m])
                    if n >= 2:
                        dve.wait_ge(lev_ready, i * 7 + n - 1)
                    d = darg[:, n % 2, :, :].rearrange("p a (b r) -> p a b r", r=m)
                    TT(out=d[:, 0], in0=second(c_, m), in1=ref, op=ALU.subtract)
                    TT(out=d[:, 1], in0=ref, in1=first(c_, m), op=ALU.subtract).then_inc(arg_done, 1)

                def scale(n, picked):
                    m = LEVELS[n]
                    dve.wait_ge(lev_exp, i * 7 + n + 1)
                    if n >= 2:
                        dve.wait_ge(lev_mm, i * 7 + n - 1)
                    if picked:
                        dve.wait_ge(lev_used, i * 7 + picked)
                    d = darg[:, n % 2, :, :].rearrange("p a (b r) -> p a b r", r=m)
                    TT(out=qc[:, n % 2, :, :].rearrange("p h (b r) -> p (h b) r", r=m), in0=second(q_, m), in1=d[:, 0], op=ALU.mult)
                    TT(out=first(kp[:, n % 2, :, :], m), in0=first(k_, m), in1=d[:, 1], op=ALU.mult).then_inc(lev_ready, 1)

                def pick(n):
                    m = LEVELS[n]
                    nb = 64 // m
                    dve.wait_ge(cst, 1 + len(LEVELS))
                    dve.wait_ge(lev_mm, i * 7 + n + 1)
                    out = sc[:].rearrange("p h (b two r) -> p h b two r", two=2, r=m)[:, :, :, 1, :]
                    mask = lmask[:, n, :].rearrange("p (b r) -> p b r", r=m).unsqueeze(1).to_broadcast([P, GH, nb, m])
                    src = wk[:, n % 2, 0:256].rearrange("p (h b r) -> p h b r", h=GH, r=m)
                    nc.vector.copy_predicated(out, mask, src).then_inc(lev_used, 1)

                dve.wait_ge(ch_in, i * 48 + 48)
                dve.wait_ge(lev_ready, i * 7)
                args(0)
                args(1)
                scale(0, 0)
                TT(out=kd[:], in0=c_[:, :, P - 1:P].to_broadcast([P, GH, P]), in1=c_, op=ALU.subtract).then_inc(end_arg, 1)
                dve.wait_ge(dg_mm, i + 1)
                args(2)
                dmask = ident[:].bitcast(u32).unsqueeze(1).to_broadcast([P, GH, P])
                nc.vector.copy_predicated(sc[:], dmask, wk[:, 2, :].rearrange("p (h t) -> p h t", h=GH)).then_inc(sc_done, 1)
                dve.wait_ge(sc_done, i + 1)
                scale(1, 0)
                pick(0)
                for n in range(2, 7):
                    if n + 1 < 7:
                        args(n + 1)
                    scale(n, n - 1)
                    pick(n - 1)
                    if n == 3:
                        dve.wait_ge(end_exp, i * 3 + 3)
                        TT(out=qe[:], in0=qe[:], in1=q_, op=ALU.mult)
                        TT(out=kd[:], in0=kd[:], in1=k_, op=ALU.mult).then_inc(kd_done, 1)
                dve.wait_ge(evac_done, N + 1)
                dve.wait_ge(lev_used, i * 7 + 6)
                STT(out=row(mix, i), in0=ea[:], scalar=1.0, in1=row(mix, i), op0=ALU.add, op1=ALU.mult).then_inc(ga_done, 1)
                pick(6)
                dve.wait_ge(evac_done, N + 2)
                STT(out=row(gbuf, i), in0=ec[:], scalar=1.0, in1=eb[:], op0=ALU.add, op1=ALU.mult).then_inc(r_done, 1)
                dve.wait_ge(su_mm, i + 1)
                for h in range(GH):
                    ins = STT(out=gst[:, h, :], in0=gst[:, h, :], scalar=etot[:, h:h + 1],
                              in1=wk[:, 2 + h // 2, (h % 2) * GV:(h % 2 + 1) * GV], op0=ALU.mult, op1=ALU.add)
                ins.then_inc(gst_done, 1)
                dve.wait_ge(o_stat, i + 1)
                link(TS(sm[:, 4:8], wk[:, 0, 0:GH], 1.0 / GV, EPS2, ALU.mult, ALU.add))
                rsqrt(sm[:, 0:4], sm[:, 4:8], sm[:, 8:12], o_rstd)
                dve.wait_ge(evac_done, N + 3)
                dve.wait_ge(r_done, i + 1)
                STT(out=row(gbuf, i), in0=ea[:], scalar=1.0, in1=row(gbuf, i), op0=ALU.add, op1=ALU.mult).then_inc(gb_done, 1)
                dve.wait_ge(o_spread, i + 1)
                TT(out=oc[:].rearrange("p (h w) t -> p h w t", w=2), in0=oc[:].rearrange("p (h w) t -> p h w t", w=2),
                   in1=wk[:, 1, :].rearrange("p (h t) -> p h t", h=GH).unsqueeze(2).to_broadcast([P, GH, 2, P]),
                   op=ALU.mult).then_inc(on_done, 1)
        link.leave(C // 2)

        with dve.Fori(0, KT // 2) as j:
            link.enter(j, 4)
            for u in range(2):
                i = j * 2 + u
                dve.wait_ge(o_in, i * 16 + 16)
                link(TT(out=eb[:], in0=eb[:], in1=row(gbuf, i), op=ALU.mult))
                dve.wait_ge(evac_done, N_U + i + 1)
                link(TT(out=ea[:], in0=ea[:], in1=row(mix, i), op=ALU.mult))
                TT(out=ea[:], in0=ea[:], in1=eb[:], op=ALU.add).then_inc(m_done, 1)
                dve.wait_ge(m_done, i + 1)
                dve.wait_ge(hi_done, 5 * KT + i + 1)
                STT(out=row(ml, i), in0=ea[:], scalar=0.5, in1=row(mh, i).bitcast(f32), op0=ALU.mult,
                    op1=ALU.subtract).then_inc(lo_done, 1)
        link.leave(KT // 2)

        link(nc.vector.memset(acc_a[:], 0.0))
        link(nc.vector.memset(acc_b[:], 0.0))
        with dve.Fori(0, KT // 2) as j:
            link.enter(j, 2)
            for u in range(2):
                n = j * 2 + u
                dve.wait_ge(evac_done, N_OUT2 + n + 1)
                link(STT(out=ea[:], in0=row(h2, n).bitcast(f32), scalar=ALPHA, in1=ea[:], op0=ALU.mult, op1=ALU.add))
                STT(out=row(yr, n), in0=row(l2, n).bitcast(f32), scalar=ALPHA, in1=ea[:], op0=ALU.mult,
                    op1=ALU.add).then_inc(y_done, 1)
                dve.wait_ge(y_done, n + 1)
                dve.wait_ge(a_used, n)
                TT(out=acc_a[:], in0=acc_a[:], in1=row(yr, n), op=ALU.add)
                dve.wait_ge(sq_done, 2 * KT + n + 1)
                TT(out=acc_b[:], in0=acc_b[:], in1=eb[:], op=ALU.add).then_inc(a_used, 1)
        link.leave(KT // 2)

        def layer_norm(count, stats):
            dve.wait_ge(stat_done, stats)
            link(TS(sm[:, 24:32], wk[:, 3, 0:8], 1.0 / D, None, ALU.mult))
            link(TT(out=sm[:, 16:24], in0=sm[:, 24:32], in1=sm[:, 24:32], op=ALU.mult))
            link(STT(out=sm[:, 16:24], in0=wk[:, 3, 8:16], scalar=1.0 / D, in1=sm[:, 16:24], op0=ALU.mult, op1=ALU.subtract))
            link(TS(sm[:, 16:24], sm[:, 16:24], 0.0, EPS2, ALU.max, ALU.add))
            rsqrt(sm[:, 0:8], sm[:, 16:24], sm[:, 32:40])
            STT(out=sm[:, 8:16], in0=sm[:, 24:32], scalar=-1.0, in1=sm[:, 0:8], op0=ALU.mult, op1=ALU.mult).then_inc(rstd_done, 1)
            dve.wait_ge(spread_done, stats)
            for k in range(KT):
                if k >= 2:
                    dve.wait_ge(h_done, count + k - 1)
                link(TT(out=ebuf[:, k % 2, :], in0=yr[:, k, :], in1=wka, op=ALU.mult))
                TT(out=ebuf[:, k % 2, :], in0=ebuf[:, k % 2, :], in1=wkb, op=ALU.add).then_inc(ln_done, 1)
                if count == 0 and k >= 1:
                    low(k - 1)
            if count == 0:
                low(KT - 1)

        def low(k):
            dve.wait_ge(hi_done, 6 * KT + k + 1)
            TT(out=l2[:, k, :], in0=yr[:, k, :], in1=h2[:, k, :].bitcast(f32), op=ALU.subtract).then_inc(lo_done, 1)

        layer_norm(0, 4)
        for k in range(KT):
            TS(yr[:, k, :], yr[:, k, :], ALPHA, None, ALU.mult).then_inc(f_acc, 1)
        with dve.Fori(0, FF_BLOCKS) as b:
            with dve.Fori(0, KT // 2) as j:
                for u in range(2):
                    i = b * KT + j * 2 + u
                    dve.wait_ge(evac_done, N_FF + b * 16 + j * 2 + u + 1)
                    TT(out=ebuf[:, u, :], in0=ebuf[:, u, :], in1=ebuf[:, u, :], op=ALU.mult).then_inc(f_sq, 1)
                    dve.wait_ge(f_sq, i + 1)
                    dve.wait_ge(f_hi, i + 1)
                    TT(out=row(fl, j * 2 + u), in0=ebuf[:, u, :], in1=row(fh, j * 2 + u).bitcast(f32),
                       op=ALU.subtract).then_inc(f_lo, 1)
            nc.vector.memset(acc_a[:], 0.0).then_inc(f_zero, 1)
            nc.vector.memset(acc_b[:], 0.0).then_inc(f_zero, 1)
            with dve.Fori(0, KT // 2) as j:
                for u in range(2):
                    i = b * KT + j * 2 + u
                    yn = row(yr, j * 2 + u)
                    dve.wait_ge(evac_done, N_FF + b * 16 + 8 + j * 2 + u + 1)
                    dve.wait_ge(f_acc, i + KT)
                    TT(out=yn, in0=yn, in1=ebuf[:, u, :], op=ALU.add).then_inc(f_acc, 1)
                    dve.wait_ge(f_acc, i + KT + 1)
                    dve.wait_ge(a_used, i + KT)
                    dve.wait_ge(f_zero, b * 2 + 2)
                    TT(out=acc_a[:], in0=acc_a[:], in1=yn, op=ALU.add)
                    dve.wait_ge(sq_done, i + 3 * KT + 1)
                    TT(out=acc_b[:], in0=acc_b[:], in1=ec[:], op=ALU.add).then_inc(a_used, 1)
        layer_norm(KT, 5)

    @block.tensor
    def _(pe):
        MM = nc.tensor.matmul

        def project(S, N, w, slot, xs, k_ready=None, first=True, last=True, between=None):
            xhi, xlo = xs
            pe.wait_ge(w_split, S + 1)
            if first and N is not None:
                pe.wait_ge(evac_done, N)
            for k in range(KT):
                if k_ready is not None:
                    pe.wait_ge(k_ready[0], k_ready[1] + k + 1)
                for n, (wt, x) in enumerate(((w_hi, xhi), (w_hi, xlo), (w_lo, xhi))):
                    for h in range(2):
                        ins = MM(pt[:, slot, h * HALF:(h + 1) * HALF], wt[:, w, k * P:(k + 1) * P],
                                 x[:, k, h * HALF:(h + 1) * HALF], start=first and k == 0 and n == 0,
                                 stop=last and k == KT - 1 and n == 2)
                if k == KT - 1:
                    ins.then_inc(mm_done, 1)
                if between is not None:
                    between(k)

        def pair(j, S, N, xs, k_ready=None):
            for u in range(2):
                project(j * 2 + (S + u), j * 2 + (N + u - 1), u, u, xs, k_ready)

        def pair_by_k(S, N, xs, k_ready):
            pe.wait_ge(w_split, S + 2)
            pe.wait_ge(evac_done, N)
            for k in range(KT):
                pe.wait_ge(k_ready[0], k_ready[1] + k + 1)
                for u in range(2):
                    for n, (wt, x) in enumerate(((w_hi, xs[0]), (w_hi, xs[1]), (w_lo, xs[0]))):
                        for h in range(2):
                            ins = MM(pt[:, u, h * HALF:(h + 1) * HALF], wt[:, u, k * P:(k + 1) * P],
                                     x[:, k, h * HALF:(h + 1) * HALF], start=k == 0 and n == 0, stop=k == KT - 1 and n == 2)
                    if k == KT - 1:
                        ins.then_inc(mm_done, 1)

        def sums(acc, col):
            for c in range(C):
                ins = MM(wk[:, 3, col + c:col + c + 1], acc[:, c * P:(c + 1) * P], ones[:, 0:1], start=True, stop=True)
            return ins

        def spread(dst, col):
            for c in range(C):
                ins = MM(dst[:, c * P:(c + 1) * P], sm[:, col + c:col + c + 1].to_broadcast([P, P]), ident[:], start=True, stop=True)
            return ins

        pe.wait_ge(cst, 1)
        pe.wait_ge(p_lo_done, 2)
        for n in range(KT):
            w, nt = n // 4, n % 4
            pe.wait_ge(w_split, S_PLE + w + 1)
            if n >= 2:
                pe.wait_ge(evac_done, n - 1)
            for k in range(2):
                for m, (wt, x) in enumerate(((w_hi, p_hi), (w_hi, p_lo), (w_lo, p_hi))):
                    for h in range(2):
                        lhs = wt[:, w, (nt * 2 + k) * P:(nt * 2 + k + 1) * P]
                        ins = MM(pt[:, n % 2, h * HALF:(h + 1) * HALF], lhs, x[:, k, h * HALF:(h + 1) * HALF],
                                 start=k == 0 and m == 0, stop=k == 1 and m == 2)
            ins.then_inc(ple_done, 1)
            if nt == 3:
                pe.wait_ge(ple_done, n + 1)
                pe.sem_inc(mm_done, 1)
        pe.wait_ge(sq_used, KT)
        sums(acc_a, 0).then_inc(stat_done, 1)
        pe.wait_ge(rstd_done, 1)
        spread(wka, 0).then_inc(spread_done, 1)
        pair_by_k(S_XBC, N_XBC, (xh, xl), (lo_done, 0))
        pe.wait_ge(wdt_done, 2)
        for h in range(2):
            for k in range(KT):
                for n, (wt, x) in enumerate(((wdt_hi, xh), (wdt_hi, xl), (wdt_lo, xh))):
                    ins = MM(wk[0:HEADS, h, :], wt[:, k, :], x[:, k, h * HALF:(h + 1) * HALF],
                             start=k == 0 and n == 0, stop=k == KT - 1 and n == 2)
        ins.then_inc(dt_mm, 1)
        pair(1, S_XBC, N_XBC, (xh, xl))
        pe.wait_ge(dt_sb, 1)
        for c in range(C):
            ins = nc.tensor.transpose(wk[:, 3, c * HEADS:(c + 1) * HEADS], dtf[0:HEADS, c * P:(c + 1) * P], ident[0:HEADS, 0:HEADS])
        ins.then_inc(dt_mm, 1)
        with pe.Fori(2, XBC_T // 2 - 1) as j:
            pair(j, S_XBC, N_XBC, (xh, xl))
        pe.wait_ge(adt_done, 1)
        flat = adt[:].rearrange("p c h -> p (c h)")
        MM(wk[:, 3, 0:P], tri[:], flat, start=True, stop=True)
        MM(wk[:, 3, P:2 * P], ones[:, 0:1].to_broadcast([P, P]), flat, start=True, stop=True)
        MM(wk[:, 3, 2 * P:3 * P], flat, tri[:], start=True, stop=True).then_inc(acs_mm, 1)
        pair(XBC_T // 2 - 1, S_XBC, N_XBC, (xh, xl))
        pe.wait_ge(dec_done, 3)
        pe.wait_ge(dec_arg, 1)
        with pe.Fori(0, C) as j:
            S, N = j * 4 + S_SC, j * 4 + N_SC
            project(S, N - 1, 0, 0, (xh, xl))
            pe.wait_ge(stage_done, j + 1)
            pe.wait_ge(s_ready, j)
            pe.wait_ge(y_evac, j)
            for i in range(KT):
                nc.tensor.transpose(wka[:, i * P:(i + 1) * P], st[:, i, :], ident[:])
            nc.tensor.transpose(wk[:, 2, 0:P], st[:, KT, :], ident[:])
            for g in range(GROUPS):
                r = slice(g * 64, g * 64 + 64)
                ins = MM(wk[:, 2, P:2 * P] if g == 0 else wk[:, 3, 0:P], st[r, KT, :], st[r, KT + 1, :], start=True, stop=True)
            ins.then_inc(ssd_a, 1)
            project(S + 1, N, 1, 1, (xh, xl))
            pe.wait_ge(m_ready, j + 1)
            pe.wait_ge(xdd_done, j + 1)
            pe.wait_ge(ce_done, j + 1)
            pe.wait_ge(s_ready, j)
            pe.wait_ge(bt_done, j + 1)
            for h in range(HEADS):
                o = wka[(h % 2) * 64:(h % 2) * 64 + 64, (h // 2) * P:(h // 2 + 1) * P]
                MM(o, xd[:, h, :], rowb[:, h, :], start=True, stop=False)
                MM(o, state[:, h, :], ce[:, h % HG, :], start=False, stop=True)
            for g in range(GROUPS):
                ins = MM(wk[g * 64:g * 64 + 64, 3, :], bt[:, g * 64:g * 64 + 64],
                         xdd[:, g * HG:(g + 1) * HG, :].rearrange("p h q -> p (h q)"), start=True, stop=True)
            ins.then_inc(ssd_b, 1)
            project(S + 2, N + 1, 0, 0, (xh, xl))
            project(S + 3, N + 2, 1, 1, (xh, xl))

        pair(0, S_SB, N_SB, (xh, xl))
        pair(1, S_SB, N_SB, (xh, xl))
        pe.wait_ge(sq_used, 2 * KT)
        pe.wait_ge(s_ready, C)
        pe.wait_ge(y_evac, C)
        sums(acc_g[:, 0, :], 0)
        sums(acc_g[:, 1, :], 8).then_inc(stat_done, 1)
        pair(2, S_SB, N_SB, (xh, xl))
        pe.wait_ge(rstd_done, 2)
        spread(wka, 0)
        spread(wkb, 8).then_inc(spread_done, 1)
        pair(3, S_SB, N_SB, (xh, xl))
        with pe.Fori(0, KT // 2) as j:
            for u in range(2):
                project(j * 4 + (S_OUT + 2 * u), j * 2 + (N_OUT + u - 1), 0, u, (sh, sl), (lo_done, KT), last=False)
                project(j * 4 + (S_OUT + 2 * u + 1), None, 1, u, (yh, yl), (lo_done, 2 * KT), first=False)
        pe.wait_ge(sq_used, 3 * KT)
        sums(acc_a, 0).then_inc(stat_done, 1)
        pe.wait_ge(rstd_done, 3)
        spread(wka, 0).then_inc(spread_done, 1)
        pair_by_k(S_GATE, N_GATE, (xh, xl), (lo_done, 3 * KT))
        with pe.Fori(1, KT // 2) as j:
            pair(j, S_GATE, N_GATE, (xh, xl))
        x2 = (h2, l2)
        def turn(i, u, used=None):
            pe.wait_ge(tr_used, used)
            for c in range(C):
                ins = nc.tensor.transpose(wka[:, c * P:(c + 1) * P], ebuf[:, u, c * P:(c + 1) * P], ident[:])
            ins.then_inc(tr_done, 1)

        def turned(S, N, base):
            project(S, N - 1, 0, 0, x2, (lo_done, 4 * KT))
            with pe.Fori(0, KT // 2 - 1) as j:
                project(j * 2 + (S + 1), j * 2 + N, 1, 1, x2)
                pe.wait_ge(evac_done, j * 2 + (N + 1))
                turn(0, 0, j * 2 + base)
                project(j * 2 + (S + 2), j * 2 + (N + 1), 0, 0, x2)
                pe.wait_ge(evac_done, j * 2 + (N + 2))
                turn(0, 1, j * 2 + (base + 1))
            project(S + 7, N + 6, 1, 1, x2)
            pe.wait_ge(evac_done, N + 7)
            turn(0, 0, base + 6)

        def turned_last(N, base):
            pe.wait_ge(evac_done, N + 8)
            turn(0, 1, base + 7)

        turned(S_AV, N_AV, 0)
        turned_last(N_AV, 0)
        pe.wait_ge(ws_done, 1)
        pe.wait_ge(tr_used, KT)
        for h in range(2):
            ins = MM(wk[:, h, :], ones[:, 0:1].to_broadcast([P, P]),
                     wst[:, 4 * h:4 * h + 4, :].rearrange("p g t -> p (g t)"), start=True, stop=True)
        ins.then_inc(row_mm, 1)
        pe.wait_ge(wl_done, 3)
        for h in range(2):
            for k in range(KT):
                for n, (wt, x) in enumerate(((wl_hi, h2), (wl_hi, l2), (wl_lo, h2))):
                    ins = MM(wk[0:RANK, 2 + h, :], wt[:, k, :], x[:, k, h * HALF:(h + 1) * HALF],
                             start=k == 0 and n == 0, stop=k == KT - 1 and n == 2)
        ins.then_inc(low_mm, 1)
        pe.wait_ge(rg_done, 1)
        with pe.Fori(0, KT // 2) as j:
            for u in range(2):
                i = j * 2 + u
                pe.wait_ge(alc_done, i + 1)
                pe.wait_ge(z_dve, i)
                MM(wk[:, 0, :], alc[0:RANK + 1, u, :], wg2[0:RANK + 1, :], start=True, stop=True).then_inc(z_mm, 1)
                project(j * 2 + (S_QK + u), j * 2 + (N_QK + u - 1), u, u, x2)
                pe.wait_ge(z_dve, i + 1)
                pe.wait_ge(cu_done, i)
                for h in range(GH):
                    ins = MM(wk[:, 1, h * P:(h + 1) * P], gm_[:, h * P:(h + 1) * P], tri[:], start=True, stop=True)
                ins.then_inc(cu_mm, 1)
        pe.wait_ge(cu_done, C)
        turned(S_VAL, N_VAL, KT)
        turned_last(N_VAL, KT)
        pe.wait_ge(av_done, C)
        pe.wait_ge(tr_used, 2 * KT)
        for g in range(KT):
            if g >= 2:
                pe.wait_ge(mix_done, g - 1)
            dst = wka if g % 2 == 0 else wkb
            for c in range(C):
                ins = MM(dst[:, c * P:(c + 1) * P], av[:, c, g * P:(g + 1) * P], wst[:, g, :], start=True, stop=True)
            ins.then_inc(mix_mm, 1)
        pe.wait_ge(mix_done, KT)
        pe.wait_ge(gst_done, 1)
        with pe.Fori(0, C // 2) as j:
            for u in range(2):
                i = j * 2 + u
                S, N = j * 6 + (S_G + 3 * u), j * 6 + (N_G + 3 * u)
                slots = [(u + n) % 2 for n in range(3)]

                def level(n):
                    pe.wait_ge(lev_ready, i * 7 + n + 1)
                    if n >= 2:
                        pe.wait_ge(lev_used, i * 7 + n - 1)
                    for h in range(GH):
                        ins = MM(wk[:, n % 2, h * 64:(h + 1) * 64], kp[:, n % 2, h, :], qc[:, n % 2, h, :], start=True, stop=True)
                    ins.then_inc(lev_mm, 1)

                def in_ga(k):
                    if k == 0:
                        pe.wait_ge(ch_in, i * 48 + 48)
                        pe.wait_ge(gst_done, i + 1)
                        for h in range(GH):
                            ins = MM(wk[:, 2, h * P:(h + 1) * P], qkc[:, 1, h, :], qkc[:, 0, h, :], start=True, stop=True)
                        ins.then_inc(dg_mm, 1)
                    if k == 1:
                        pe.wait_ge(on_done, i)
                    if k in (1, 3, 5, 7):
                        level((k - 1) // 2)

                def in_r(k):
                    if k in (1, 3, 5):
                        level(4 + (k - 1) // 2)
                    if k == 6:
                        pe.wait_ge(kd_done, i + 1)
                        for h in range(GH):
                            ins = nc.tensor.transpose(wk[:, 3, h * P:(h + 1) * P], kd[:, h, :], ident[:])
                        ins.then_inc(kdt_mm, 1)

                def in_gb(k):
                    if k == 1:
                        pe.wait_ge(lev_used, i * 7 + 7)
                        pe.wait_ge(sc_done, i + 1)
                        for v in range(8):
                            h = v // 2
                            o = wka[:, v * P:(v + 1) * P]
                            MM(o, vc[:, v * P:(v + 1) * P], sc[:, h, :], start=True, stop=False)
                            ins = MM(o, gst[:, h, (v % 2) * P:(v % 2 + 1) * P], qe[:, h, :], start=False, stop=True)
                        ins.then_inc(o_mm, 1)
                        pe.wait_ge(kdt_done, i + 1)
                        for h in range(GH):
                            ins = MM(wk[:, 2 + h // 2, (h % 2) * GV:(h % 2 + 1) * GV], kdt[:, h, :], vc[:, h * GV:(h + 1) * GV],
                                     start=True, stop=True)
                        ins.then_inc(su_mm, 1)
                    if k == 4:
                        pe.wait_ge(o_act, i + 1)
                        for h in range(GH):
                            for w in range(2):
                                ins = MM(wk[:, 0, h:h + 1], osq[:, 2 * h + w, :], ones[:, 0:1], start=w == 0, stop=w == 1)
                        ins.then_inc(o_stat, 1)
                    if k == 7:
                        pe.wait_ge(o_rstd, i + 1)
                        for h in range(GH):
                            ins = MM(wk[:, 1, h * P:(h + 1) * P], sm[:, h:h + 1].to_broadcast([P, P]), ident[:], start=True, stop=True)
                        ins.then_inc(o_spread, 1)

                project(S, N - 1, u, slots[0], x2, between=in_ga)
                project(S + 1, N, 1 - u, slots[1], x2, between=in_r)
                project(S + 2, N + 1, u, slots[2], x2, between=in_gb)
        with pe.Fori(0, KT // 2) as j:
            pair(j, S_U, N_U, x2)
        with pe.Fori(0, KT // 2) as j:
            pair(j, S_OUT2, N_OUT2, (mh, ml), (lo_done, 5 * KT))

        def token_stats(used, n):
            pe.wait_ge(a_used, used)
            sums(acc_a, 0)
            sums(acc_b, 8).then_inc(stat_done, 1)
            pe.wait_ge(rstd_done, n)
            spread(wka, 0)
            spread(wkb, 8).then_inc(spread_done, 1)

        pe.wait_ge(gst_done, C + 1)
        pe.wait_ge(on_done, C)
        token_stats(KT, 5)

        def ff2(b):
            with pe.Fori(0, KT // 2) as j:
                for u in range(2):
                    project(b * 16 + j * 2 + (S_FF + 8 + u), b * 16 + j * 2 + (N_FF + 8 + u - 1), u, u, (fh, fl),
                            (f_lo, b * KT))

        pair_by_k(S_FF, N_FF, x2, (lo_done, 6 * KT))
        with pe.Fori(1, KT // 2) as j:
            pair(j, S_FF, N_FF, x2)
        ff2(0)
        with pe.Fori(1, FF_BLOCKS) as b:
            with pe.Fori(0, KT // 2) as j:
                for u in range(2):
                    project(b * 16 + j * 2 + (S_FF + u), b * 16 + j * 2 + (N_FF + u - 1), u, u, x2)
            ff2(b)
        token_stats(KT + FF_BLOCKS * KT, 6)
    ctx.close()


def kernel(**inputs):
    import numpy as _np
    import concourse.bacc as _bacc
    from concourse import mybir as _mybir
    from concourse.bass_utils import run_bass_kernel_spmd as _run

    a = {k: _np.asarray(v) for k, v in inputs.items()}
    w_in, w_in2 = a["w_in"][0], a["w_in_2"][0]

    def tiles(w):
        k, n = w.shape
        return w.reshape(k // 1024, 8, P, n // P, P).transpose(3, 0, 2, 1, 4).reshape(-1, P, 1024)

    def mixed(*ws):
        t = [tiles(w) for w in ws]
        return _np.stack(t, 1).reshape(-1, P, 1024)

    o = XBC_T * P + HEADS
    z, sc_h, sc_b, sc_c, z_sc = (w_in[:, o + i * D:o + (i + 1) * D] for i in range(5))
    u_, v_, qk_, val_, r_ = (w_in2[:, i * D:(i + 1) * D] for i in range(5))
    o2 = 5 * D + RANK
    g_a, g_b = w_in2[:, o2:o2 + D], w_in2[:, o2 + D:o2 + 2 * D]
    w_out = a["w_out"][0]
    w_ple = a["w_ple_proj"][0].reshape(2, P, 2, 4, P).transpose(2, 1, 3, 0, 4).reshape(2, P, 1024)
    ff1 = tiles(a["w_ff1_2"][0]).reshape(FF_BLOCKS, 8, P, 1024)
    ff2 = tiles(a["w_ff2_2"][0]).reshape(8, FF_BLOCKS, P, 1024).transpose(1, 0, 2, 3)
    stream = _np.concatenate([
        w_ple, tiles(w_in[:, 0:XBC_T * P]), mixed(z, sc_c, sc_h, z_sc), tiles(sc_b),
        mixed(w_out[D:], w_out[:D]), tiles(a["w_ple_gate"][0]), tiles(v_), tiles(qk_), tiles(val_),
        mixed(g_a, r_, g_b), tiles(u_), tiles(a["w_out_2"][0]),
        _np.concatenate([ff1, ff2], 1).reshape(-1, P, 1024)])
    b_in = a["b_in_2"][0]
    cols = {"norm_pre": a["norm_pre"], "norm_post": a["norm_post"], "conv_w": a["ssd_conv_w"][0], "conv_b": a["ssd_conv_b"],
            "d_skip": _np.repeat(a["d_skip"][0], HP), "ssd_norm": a["ssd_norm"], "sc_w": a["sc_conv_w"][0],
            "b_u": b_in[0:D], "b_v": b_in[D:2 * D], "b_qk": b_in[2 * D:3 * D], "b_val": b_in[3 * D:4 * D],
            "b_r": b_in[4 * D:5 * D], "b_ga": b_in[o2:o2 + D], "b_gb": b_in[o2 + D:o2 + 2 * D],
            "sg_g": a["sg_ln_g_2"], "sg_b": a["sg_ln_b_2"], "gn": a["gla_norm_g_2"], "ln1_g": a["ln1_g_2"],
            "ln1_b": a["ln1_b_2"], "ln2_g": a["ln2_g_2"], "ln2_b": a["ln2_b_2"]}
    vecs = _np.concatenate([cols[n].reshape(-1, P).T for n, _ in VCOLS], 1)
    arrays = {
        "xT": a["x"][0].T, "pT": a["p"][0, 0].T, "ws": stream, "w_dt": w_in[:, XBC_T * P:o],
        "w_low": w_in2[:, 5 * D:o2], "vecs": vecs, "dt_bias": a["dt_bias"], "a_log": a["a_log"],
        "b_low": b_in[5 * D:o2].reshape(RANK, 1), "w_gate2": a["gla_w_gate2_2"][0], "b_gate": a["gla_b_gate_2"],
        "sg_w": a["sg_w_s_2"][0].transpose(2, 0, 1), "sg_bs": a["sg_b_s_2"].reshape(1, D)}
    nc = _bacc.Bacc("TRN2", target_bir_lowering=False, num_devices=1)
    ins, args = {}, []
    for name, x in arrays.items():
        ins[name + "_d"] = _np.ascontiguousarray(x)
        args.append(nc.dram_tensor(name + "_d", x.shape, _mybir.dt.float32, kind="ExternalInput").ap())
    args.append(nc.dram_tensor("outT_d", (D, T), _mybir.dt.float32, kind="ExternalOutput").ap())
    two_blocks_kernel(nc, *args)
    r = _run(nc, [ins], core_ids=[0])
    return _np.ascontiguousarray(r.results[0]["outT_d"].T).reshape(1, T, D)
```

```python
import math
from contextlib import ExitStack

import numpy as np

import concourse.bass as bass
from concourse import mybir

P = 128
T = 1024
D = 1024
KT = D // P
C = T // P
HALF = 512
HEADS, HP, GROUPS, NS = 16, 64, 2, 64
HG = HEADS // GROUPS
XBC_T = (D + 2 * GROUPS * NS) // P
CW, SW = 4, 3
GH, GK, GV = 4, 128, 256
RANK = 16
FF_BLOCKS = 4
EPS1, EPS2 = 1e-6, 1e-5
ALPHA = 2.0 ** 0.25
Q_SCALE = GK ** -0.5
TEMP = 16.0
LEVELS = [64, 32, 16, 8, 4, 2, 1]

VCOLS = [("norm_pre", 8), ("norm_post", 8), ("conv_w", CW * XBC_T), ("conv_b", XBC_T), ("d_skip", 8),
         ("ssd_norm", 8), ("sc_w", SW * 8), ("b_u", 8), ("b_v", 8), ("b_qk", 8), ("b_val", 8), ("b_r", 8),
         ("b_ga", 8), ("b_gb", 8), ("sg_g", 8), ("sg_b", 8), ("gn", 8), ("ln1_g", 8), ("ln1_b", 8),
         ("ln2_g", 8), ("ln2_b", 8)]
VOFF, _n = {}, 0
for _name, _w in VCOLS:
    VOFF[_name] = _n
    _n += _w
NV = _n
HOFF = {}
for _name in ("half_ga", "half_r", "half_gb", "half_gn", "half_rgn", "qk_s", "qk_b"):
    HOFF[_name] = _n
    _n += 8
NVH = _n

S_PLE, N_PLE = 0, 0
S_XBC, N_XBC = 2, 8
S_SC, N_SC = 12, 18
S_SB, N_SB = 44, 50
S_OUT, N_OUT = 52, 58
S_GATE, N_GATE = 68, 66
S_AV, N_AV = 76, 74
S_QK, N_QK = 84, 82
S_VAL, N_VAL = 92, 90
S_G, N_G = 100, 98
S_U, N_U = 124, 122
S_OUT2, N_OUT2 = 132, 130
S_FF, N_FF = 140, 138
S_ALL = S_FF + FF_BLOCKS * 16


class Chain:

    def __init__(self, eng, sem):
        self.eng, self.sem, self.base, self.n = eng, sem, 0, 0

    def __call__(self, ins):
        self.n += 1
        ins.then_inc(self.sem, 1)
        self.eng.wait_ge(self.sem, self.base + self.n)

    def enter(self, i, per):
        self.start, self.per = self.base + self.n, per
        self.base, self.n = self.start + i * per, 0

    def leave(self, times):
        assert self.n == self.per, (self.n, self.per)
        self.base, self.n = self.start + times * self.per, 0


def two_blocks_kernel(nc, xT, pT, ws, w_dt, w_low, vecs, dt_bias, a_log, b_low, w_gate2, b_gate,
                      sg_w, sg_bs, outT):
    f32, f32r = mybir.dt.float32, mybir.dt.float32r
    u32, i32 = mybir.dt.uint32, mybir.dt.int32
    ALU, ACT = mybir.AluOpType, mybir.ActivationFunctionType
    ds = bass.ds
    ctx = ExitStack()

    BASE = 16512
    W0 = BASE
    A0, A1 = W0 + 24576, W0 + 24576 + 32768
    R2 = A1 + 32768
    R3 = R2 + 32768
    R1 = R3 + 32768
    BC = R1 + 32768
    EAo, EBo, ECo = BC + 8192, BC + 12288, BC + 16384
    K0 = ECo + 4128
    assert K0 + 3904 <= 229344

    def at(name, shape, off, dt=f32):
        return nc.alloc_sbuf_tensor_at(name, [P] + shape, dt, offset=off)

    w_raw = at("w_raw", [2, 1024], W0)
    w_hi = at("w_hi", [2, 1024], W0 + 8192, f32r)
    w_lo = at("w_lo", [2, 1024], W0 + 16384, f32r)
    ea, eb, ec = at("ea", [1024], EAo), at("eb", [1024], EBo), at("ec", [1024], ECo)
    ebuf = at("ebuf", [2, 1024], EAo)
    tri = at("tri", [P], K0)
    ident = at("ident", [P], K0 + 512)
    vec = at("vec", [NVH], K0 + 1024)
    sm = at("sm", [64], K0 + 2240)
    ones = at("ones", [2], K0 + 2496)
    dec = at("dec", [P], K0 + 2560)
    assert 1024 + NVH * 4 <= 2240
    xh, xl = at("xh", [KT, T], A0, f32r), at("xl", [KT, T], A1, f32r)
    x_raw = at("x_raw", [KT, T], R1)
    p_raw, p_hi, p_lo = at("p_raw", [2, T], R2), at("p_hi", [2, T], R3, f32r), at("p_lo", [2, T], R3 + 8192, f32r)
    acc_a, acc_b = at("acc_a", [1024], BC), at("acc_b", [1024], BC + 4096)
    acc_g = at("acc_g", [2, 1024], R3 + 24576)
    raw_p = at("raw_p", [2, T + CW], R2 + 8192)
    conv_o = at("conv_o", [2, T], R2 + 16448)
    wdt_raw, wdt_hi, wdt_lo = (at("wdt_raw", [KT, HEADS], R2 + 24640),
                               at("wdt_hi", [KT, HEADS], R2 + 25152, f32r), at("wdt_lo", [KT, HEADS], R2 + 25664, f32r))
    dtb, alr = at("dtb", [HEADS], R2 + 26176), at("alr", [HEADS], R2 + 26240)
    tmps = [at(f"tmp{i}", [P], R2 + 26304 + 512 * i) for i in range(8)]
    adt = at("adt", [C, HEADS], R2 + 30400)
    dtf = at("dtf", [T], R2)
    acs_row = at("acs_row", [P], R2 + 30912)
    xbc = at("xbc", [XBC_T, T], R1)
    rowb = at("rowb", [HEADS, P], R3)
    st = at("st", [XBC_T, P], R3 + 8192)
    xd = at("xd", [HEADS, HP], R3 + 13312)
    xdd = at("xdd", [HEADS, HP], R3 + 17408)
    ce = at("ce", [HG, P], R3 + 21504)
    bt = at("bt", [P], R3 + 25600)
    cbm = at("cbm", [GROUPS, P], R3 + 26112)
    state = at("state", [HEADS, HP], R3 + 27136)
    dtt = at("dtt", [C, HEADS], R3 + 31232)
    acs = at("acs", [C, HEADS], R3 + 31744)
    et2 = at("et2", [C, HG], K0 + 3072)
    vbuf = at("vbuf", [KT, T], R2)
    ecp = at("ecp", [T + SW - 1], ECo)
    sh, sl = at("sh", [KT, T], R3, f32r), at("sl", [KT, T], R2, f32r)
    yh, yl = xh, at("yl", [KT, T], R1, f32r)
    mm = at("mm", [KT, T], A1)
    xres = x_raw
    h2, l2 = at("h2", [KT, T], R2, f32r), at("l2", [KT, T], R3, f32r)
    av = at("av", [C, D], A0)
    mix = at("mix", [KT, T], A1)
    wl_raw, wl_hi, wl_lo = (at("wl_raw", [KT, RANK], R1), at("wl_hi", [KT, RANK], R1 + 512, f32r),
                            at("wl_lo", [KT, RANK], R1 + 1024, f32r))
    blow = at("blow", [1], R1 + 1536)
    wg2 = at("wg2", [GH * GK], R1 + 2048)
    alow = at("alow", [T], R1 + 4096)
    alc = at("alc", [2, P], R1 + 8192)
    wst = at("wst", [KT, P], R1 + 9216)
    rg = at("rg", [KT, P], R1 + 13312)
    ga_, ge_, gl_, gm_ = (at(f"gz{i}", [512], R1 + 17408 + 2048 * i) for i in range(4))
    cu_o = at("cu_o", [512], R1 + 25600)
    bnst, bnag = at("bnst", [2 * C, 6], R1 + 27648), at("bnag", [C, 2], R1 + 28160)
    vb = at("vb", [2, C, P], BC)
    G = A0
    qkc = at("qkc", [3, GH, P], G)
    vc = at("vc", [D], G + 6144)
    darg = at("darg", [2, 2, 256], G + 10240)
    kp = at("kp", [2, GH, P], G + 14336)
    qc = at("qc", [2, GH, 64], G + 18432)
    sc = at("sc", [GH, P], G + 20480)
    kd = at("kd", [GH, P], G + 22528)
    qe = at("qe", [GH, P], G + 24576)
    kdt = at("kdt", [GH, P], G + 26624)
    gst = at("gst", [GH, GV], G + 28672)
    oc = at("oc", [8, P], BC)
    osq = at("osq", [8, P], BC + 4096)
    lmask_f = at("lmask_f", [7, 64], R3 + 16384)
    lmask = at("lmask", [7, 64], K0 + 3328, mybir.dt.uint8)
    etot = at("etot", [GH], K0 + 2528)
    gbuf = at("gbuf", [KT, T], R1)
    mh, ml = at("mh", [KT, T], A0, f32r), at("ml", [KT, T], A1, f32r)
    yr = at("yr", [KT, T], R1)
    fh, fl = at("fh", [KT, T], A0, f32r), at("fl", [KT, T], A1, f32r)

    pt = ctx.enter_context(nc.psum_tensor("pt", [P, 2, 1024], f32))
    wk = ctx.enter_context(nc.psum_tensor("wk", [P, 4, HALF], f32))
    wka = wk[:, 0:2, :].rearrange("p b n -> p (b n)")
    wkb = wk[:, 2:4, :].rearrange("p b n -> p (b n)")

    nrm, nrm2 = at("nrm", [2, HALF], ECo), at("nrm2", [2, HALF], R2)

    pp_d = nc.dram_tensor("pp_d", [KT, P, T], f32, kind="Internal").ap()
    sz_d = nc.dram_tensor("sz_d", [KT, P, T], f32, kind="Internal").ap()
    acs_d = nc.dram_tensor("acs_d", [C, HEADS * P], f32, kind="Internal").ap()
    qk_d = nc.dram_tensor("qk_d", [KT, P, T], f32, kind="Internal").ap()
    cu_d = nc.dram_tensor("cu_d", [C, P, GH * P], f32, kind="Internal").ap()
    v_d = nc.dram_tensor("v_d", [C, P, D], f32, kind="Internal").ap()
    o_d = nc.dram_tensor("o_d", [KT, P, T], f32, kind="Internal").ap()

    def tile_of(dram, i):
        return dram[ds(i, 1), :, :].rearrange("a p n -> (a p) n")

    def row(t, i):
        return t[:, ds(i, 1), :].rearrange("p a t -> p (a t)")

    def cols(h):
        return slice(h * HALF, (h + 1) * HALF)

    def sem(name):
        return ctx.enter_context(nc.semaphore(name))

    def V(name, i=0, n=1):
        off = VOFF[name] if name in VOFF else HOFF[name]
        return vec[:, ds(off + i, n)]

    w_loaded = [sem("w_loaded0"), sem("w_loaded1")]
    w_hi_done, w_split = sem("w_hi_done"), sem("w_split")
    mm_done = sem("mm_done")
    ple_done = sem("ple_done")
    evac_done = sem("evac_done")
    cst = sem("cst")
    x_in = [sem(f"x_in{k}") for k in range(KT)]
    p_in, vec_in, sml_in = sem("p_in"), sem("vec_in"), sem("sml_in")
    p_hi_done, p_lo_done = sem("p_hi_done"), sem("p_lo_done")
    pp_put = [sem("pp_put0"), sem("pp_put1")]
    sq_done, sq_used = sem("sq_done"), sem("sq_used")
    stat_done = sem("stat_done")
    rstd_done = sem("rstd_done")
    spread_done = sem("spread_done")
    val_done = sem("val_done")
    hi_done = sem("hi_done")
    lo_done = sem("lo_done")
    wdt_done = sem("wdt_done")
    dt_mm, dt_sb, dt_a, dt_b = sem("dt_mm"), sem("dt_sb"), sem("dt_a"), sem("dt_b")
    adt_done, acs_mm, acs_put = sem("adt_done"), sem("acs_mm"), sem("acs_put")
    acs_sb, dec_arg, dec_done = sem("acs_sb"), sem("dec_arg"), sem("dec_done")
    conv_done, silu_done = sem("conv_done"), sem("silu_done")
    stage_done, ssd_a, ssd_b = sem("stage_done"), sem("ssd_a"), sem("ssd_b")
    bt_done, row_in, ce_exp, e_arg, e_exp = sem("bt_done"), sem("row_in"), sem("ce_exp"), sem("e_arg"), sem("e_exp")
    ce_done, xdd_done, m_ready, y_evac, s_ready = sem("ce_done"), sem("xdd_done"), sem("m_ready"), sem("y_evac"), sem("s_ready")
    sz_done, sz_put, u_done, v_done = sem("sz_done"), sem("sz_put"), sem("u_done"), sem("v_done")
    sz_in, yz_done = [sem("sz_in0"), sem("sz_in1")], sem("yz_done")
    ys_done = sem("ys_done")
    pp_in = [sem("pp_in0"), sem("pp_in1")]
    b2_in = sem("b2_in")
    tr_done, tr_used = sem("tr_done"), sem("tr_used")
    wl_done = sem("wl_done")
    low_mm, low_done = sem("low_mm"), sem("low_done")
    alc_done, z_mm, z_act, z_dve, z_min = sem("alc_done"), sem("z_mm"), sem("z_act"), sem("z_dve"), sem("z_min")
    cu_mm, cu_done, cu_put = sem("cu_mm"), sem("cu_done"), sem("cu_put")
    qk_put = [sem("qk_put0"), sem("qk_put1")]
    v_put = [sem("v_put0"), sem("v_put1")]
    bn_done, av_done = sem("bn_done"), sem("av_done")
    ws_done, row_mm, rg_done, mix_mm, mix_done = sem("ws_done"), sem("row_mm"), sem("rg_done"), sem("mix_mm"), sem("mix_done")
    ch_in, vc_in = sem("ch_in"), sem("vc_in")
    arg_done, lev_exp, lev_ready, lev_mm, lev_used = sem("arg_done"), sem("lev_exp"), sem("lev_ready"), sem("lev_mm"), sem("lev_used")
    dg_mm, sc_done, end_exp, end_arg, kd_done = (sem("dg_mm"), sem("sc_done"), sem("end_exp"), sem("end_arg"),
                                                 sem("kd_done"))
    kdt_mm, kdt_done, o_mm, su_mm, gst_done = sem("kdt_mm"), sem("kdt_done"), sem("o_mm"), sem("su_mm"), sem("gst_done")
    o_act, o_stat, o_rstd, o_spread, on_done, o_put = (sem("o_act"), sem("o_stat"), sem("o_rstd"), sem("o_spread"),
                                                      sem("on_done"), sem("o_put"))
    ga_done, r_done, gb_done = sem("ga_done"), sem("r_done"), sem("gb_done")
    o_in, m_done = sem("o_in"), sem("m_done")
    y_done, a_used = sem("y_done"), sem("a_used")
    ln_done, h_done = sem("ln_done"), sem("h_done")
    f_sq, f_hi, f_lo, f_acc, f_zero = sem("f_sq"), sem("f_hi"), sem("f_lo"), sem("f_acc"), sem("f_zero")
    out_ready, out_put = sem("out_ready"), sem("out_put")
    half_mm, half_ev, half_y, half_sq, half_acc, half_val, half_hi, half_lo = (
        sem("half_mm"), sem("half_ev"), sem("half_y"), sem("half_sq"), sem("half_acc"), sem("half_val"), sem("half_hi"),
        sem("half_lo"))
    d_chain, a_chain, p_chain = sem("d_chain"), sem("a_chain"), sem("p_chain")

    block = ctx.enter_context(nc.Block())

    @block.sync
    def _(sp):
        for u in range(2):
            sp.dma_start(w_raw[:, u, :], ws[u, :, :]).then_inc(w_loaded[u], 16)
        with sp.Fori(1, S_ALL // 2) as j:
            for u in range(2):
                tile = sp.snap(j * 2 + u)
                sp.wait_ge(w_split, j * 2 + u - 1)
                sp.dma_start(w_raw[:, u, :], tile_of(ws, tile)).then_inc(w_loaded[u], 16)

    @block.gpsimd
    def _(pool):
        link = Chain(pool, p_chain)
        link(nc.gpsimd.memset(ones[:, 0:1], 1.0))
        link(nc.gpsimd.memset(ones[:, 1:2], 0.0))
        link(nc.gpsimd.memset(ident[:], 0.0))
        link(nc.gpsimd.memset(tri[:], 1.0))
        link(nc.gpsimd.affine_select(out=ident[:], in_=ident[:], compare_op=ALU.not_equal, fill=1.0, base=0,
                                     pattern=[[-1, P]], channel_multiplier=1))
        nc.gpsimd.affine_select(out=tri[:], in_=tri[:], compare_op=ALU.is_ge, fill=0.0, base=0,
                                pattern=[[1, P]], channel_multiplier=-1).then_inc(cst, 1)

        def split(u, loaded):
            pool.wait_ge(w_loaded[u], loaded)
            zeros = ones[:, 1:2].to_broadcast([P, 1024])
            nc.gpsimd.tensor_tensor(out=w_hi[:, u, :], in0=w_raw[:, u, :], in1=zeros, op=ALU.add).then_inc(w_hi_done, 1)

        def rest(u, n):
            pool.wait_ge(w_hi_done, n)
            nc.gpsimd.tensor_tensor(out=w_lo[:, u, :], in0=w_raw[:, u, :], in1=w_hi[:, u, :].bitcast(f32),
                                    op=ALU.subtract).then_inc(w_split, 1)

        for u in range(2):
            split(u, 16)
            rest(u, u + 1)
        for n, m in enumerate(LEVELS):
            v = lmask_f[:, n, :].rearrange("p (b r) -> p b r", r=m)
            link(nc.gpsimd.memset(lmask_f[:, n, :], 1.0))
            link(nc.gpsimd.affine_select(out=v, in_=v, compare_op=ALU.is_ge, fill=0.0, base=0,
                                         pattern=[[-2 * m, 64 // m], [0, m]], channel_multiplier=1))
            nc.gpsimd.affine_select(out=v, in_=v, compare_op=ALU.is_ge, fill=0.0, base=m - 1,
                                    pattern=[[2 * m, 64 // m], [0, m]], channel_multiplier=-1).then_inc(cst, 1)
        def split_pairs(first, end):
            with pool.Fori(first, end) as j:
                for u in range(2):
                    pool.wait_ge(mm_done, j * 2 + u - 1)
                    split(u, j * 16 + 16)
                    rest(u, j * 2 + u + 1)

        def before_norm(S):
            pool.wait_ge(mm_done, S - 1)
            split(0, 16 * (S // 2 + 1))
            rest(0, S + 1)

        def lows(dst, src, high, half_base, base):
            for h in range(2):
                for k in range(KT):
                    pool.wait_ge((half_hi, hi_done)[h], (half_base, base)[h] + k + 1)
                    nc.gpsimd.tensor_tensor(out=dst[:, k, cols(h)], in0=src[:, k, cols(h)],
                                            in1=high[:, k, cols(h)].bitcast(f32),
                                            op=ALU.subtract).then_inc((half_lo, lo_done)[h], 1)

        split_pairs(1, S_GATE // 2)
        before_norm(S_GATE)
        lows(xl, xres, xh, 0, 3 * KT)
        split_pairs(S_GATE // 2 + 1, S_FF // 2)
        before_norm(S_FF)
        lows(l2, yr, h2, KT, 6 * KT)
        split_pairs(S_FF // 2 + 1, S_ALL // 2)

    @block.scalar
    def _(act):
        A = nc.scalar.activation
        link = Chain(act, a_chain)
        act.dma_start(p_raw[:], pT.rearrange("(k p) t -> p k t", p=P)).then_inc(p_in, 16)
        act.dma_start(vec[:, 0:NV], vecs).then_inc(vec_in, 16)
        for k in range(KT):
            act.dma_start(x_raw[:, k, :], xT[k * P:(k + 1) * P, :]).then_inc(x_in[k], 16)
        act.dma_start(wdt_raw[:], w_dt.rearrange("(k p) h -> p k h", p=P)).then_inc(sml_in, 16)
        act.dma_start(dtb[:], dt_bias.to_broadcast([P, HEADS])).then_inc(sml_in, 16)
        act.dma_start(alr[:], a_log.to_broadcast([P, HEADS])).then_inc(sml_in, 16)

        act.wait_ge(p_in, 16)
        for k in range(2):
            A(p_hi[:, k, :], p_raw[:, k, :], ACT.Copy).then_inc(p_hi_done, 1)

        for k in range(KT):
            act.wait_ge(x_in[k], 16)
            if k:
                act.wait_ge(sq_used, k)
            A(ec[:], x_raw[:, k, :], ACT.Square).then_inc(sq_done, 1)
            act.wait_ge(ple_done, k + 1)
            if k >= 2:
                act.wait_ge(pp_put[k % 2], 16 * (k // 2))
            A(ebuf[:, k % 2, :], pt[:, k % 2, :], ACT.Copy, scale=0.5).then_inc(evac_done, 1)
            act.wait_ge(evac_done, k + 1)
            act.dma_start(pp_d[k, :, :], ebuf[:, k % 2, :]).then_inc(pp_put[k % 2], 16)
        act.wait_ge(sml_in, 48)
        A(wdt_hi[:], wdt_raw[:], ACT.Copy).then_inc(wdt_done, 1)
        for k in range(KT):
            act.wait_ge(val_done, k + 1)
            A(xh[:, k, :], x_raw[:, k, :], ACT.Copy).then_inc(hi_done, 1)

        def xbc_pair(j):
            for u in range(2):
                act.wait_ge(mm_done, j * 2 + (S_XBC + u + 1))
                act.wait_ge(conv_done, j * 2)
                A(raw_p[:, u, CW - 1:CW - 1 + T], pt[:, u, :], ACT.Copy).then_inc(evac_done, 1)
            for u in range(2):
                act.wait_ge(conv_done, j * 2 + (u + 1))
                A(row(xbc, j * 2 + u), conv_o[:, u, :], ACT.Silu).then_inc(silu_done, 1)

        act.wait_ge(lo_done, KT)
        xbc_pair(0)
        act.wait_ge(dt_mm, 1)
        A(dtf[0:HEADS, :], wka[0:HEADS, :], ACT.Copy).then_inc(dt_sb, 1)
        xbc_pair(1)
        v, r_, e_, u_, l_ = tmps[0], tmps[1], tmps[2], tmps[3], tmps[4]
        act.wait_ge(dt_a, 1)
        link(A(l_[:], v[:], ACT.Abs))
        A(e_[:], l_[:], ACT.Exp, scale=-1.0).then_inc(dt_b, 1)
        A(alr[:], alr[:], ACT.Exp).then_inc(dt_b, 1)
        act.wait_ge(dt_a, 2)
        A(l_[:], u_[:], ACT.Ln).then_inc(dt_b, 1)

        with act.Fori(2, XBC_T // 2 - 1) as j:
            xbc_pair(j)

        act.wait_ge(acs_mm, 1)
        A(acs[:], wk[:, 3, 0:P].rearrange("p (c h) -> p c h", c=C), ACT.Copy).then_inc(acs_sb, 1)
        A(acs_row[:], wk[:, 3, 2 * P:3 * P], ACT.Copy).then_inc(acs_sb, 1)
        act.wait_ge(acs_sb, 2)
        act.dma_start(acs_d.rearrange("c (h l) -> (c h) l", h=HEADS), acs_row[:]).then_inc(acs_put, 16)
        tot = wk[:, 3, P:2 * P].rearrange("p (c h) -> p c h", c=C)
        A(et2[0:64], tot[0:64, :, 0:HG], ACT.Exp).then_inc(dec_done, 1)
        A(et2[64:128], tot[64:128, :, HG:HEADS], ACT.Exp).then_inc(dec_done, 1)
        act.wait_ge(dec_arg, 1)
        A(dec[:], dec[:], ACT.Exp).then_inc(dec_done, 1)
        act.wait_ge(acs_put, 16)
        xbc_pair(XBC_T // 2 - 1)
        act.wait_ge(silu_done, XBC_T)

        act.wait_ge(pp_put[0], 64)
        act.wait_ge(pp_put[1], 64)
        with act.Fori(0, C) as j:
            S, N = S_SC + j * 4, N_SC + j * 4
            row_src = acs_d[ds(j, 1), :].to_broadcast([P, HEADS * P])
            act.wait_ge(ssd_b, j)
            act.dma_start(rowb[:].rearrange("p h l -> p (h l)"), row_src).then_inc(row_in, 16)
            act.wait_ge(y_evac, j)
            A(st[:], xbc[:, :, ds(j * P, P)], ACT.Copy).then_inc(stage_done, 1)
            act.wait_ge(row_in, j * 16 + 16)
            A(ce[0:64], rowb[0:64, 0:HG, :], ACT.Exp).then_inc(ce_exp, 1)
            A(ce[64:128], rowb[64:128, HG:HEADS, :], ACT.Exp).then_inc(ce_exp, 1)
            act.wait_ge(e_arg, j + 1)
            A(rowb[:], rowb[:], ACT.Exp).then_inc(e_exp, 1)
            act.wait_ge(mm_done, S + 1)
            act.wait_ge(v_done, j)
            A(ea[:], pt[:, 0, :], ACT.Copy, scale=0.5)
            A(eb[:], pt[:, 0, :], ACT.Tanh, scale=0.5).then_inc(evac_done, 1)
            act.wait_ge(ssd_a, j + 1)
            A(bt[:], wk[:, 2, 0:P], ACT.Copy).then_inc(bt_done, 1)
            act.wait_ge(mm_done, S + 2)
            act.wait_ge(sz_done, j + 1)
            act.dma_start(tile_of(sz_d, j), eb[:]).then_inc(sz_put, 16)
            A(ea[:], pt[:, 1, :], ACT.Copy).then_inc(evac_done, 1)
            act.wait_ge(mm_done, S + 3)
            act.wait_ge(sz_put, j * 16 + 16)
            A(eb[:], pt[:, 0, :], ACT.Copy).then_inc(evac_done, 1)
            act.wait_ge(mm_done, S + 4)
            act.wait_ge(u_done, j + 1)
            A(ea[:], pt[:, 1, :], ACT.Copy, scale=0.5)
            A(eb[:], pt[:, 1, :], ACT.Tanh, scale=0.5).then_inc(evac_done, 1)

        act.wait_ge(v_done, C)
        act.dma_start(eb[:], sz_d[0, :, :]).then_inc(sz_in[0], 16)

        def gated(i):
            if i + 1 < KT:
                if i:
                    act.wait_ge(yz_done, i)
                act.dma_start((ec if i % 2 == 0 else eb)[:], sz_d[i + 1, :, :]).then_inc(sz_in[(i + 1) % 2], 16)
            act.wait_ge(yz_done, i + 1)
            act.wait_ge(sq_used, KT + i)
            A(acc_b[:], xbc[:, i, :], ACT.Square).then_inc(sq_done, 1)

        def branch_high(i):
            act.wait_ge(mm_done, S_SB + i + 1)
            act.wait_ge(ys_done, i)
            A(ea[:], pt[:, i % 2, :], ACT.Copy).then_inc(evac_done, 1)
            act.wait_ge(ys_done, i + 1)
            A(sh[:, i, :], vbuf[:, i, :], ACT.Copy).then_inc(hi_done, 1)

        for i in range(KT):
            gated(i)
            if i in (3, 5):
                branch_high((i - 3) // 2)
        for i in range(2, KT):
            branch_high(i)

        act.wait_ge(mm_done, S_OUT)
        for i in range(KT):
            act.wait_ge(val_done, KT + i + 1)
            A(yh[:, i, :], xbc[:, i, :], ACT.Copy).then_inc(hi_done, 1)
        def mixer_out(n, u, c, waits):
            for w in waits:
                act.wait_ge(*w)
            A(mm[:, ds(n, 1), c].rearrange("p a t -> p (a t)"), pt[:, u, c], ACT.Copy)
            act.wait_ge(sq_used, 2 * KT + n)
            return A(eb[:, c], pt[:, u, c], ACT.Square)

        with act.Fori(0, KT // 2 - 1) as j:
            for u in range(2):
                n = j * 2 + u
                mixer_out(n, u, slice(0, T), [(mm_done, S_OUT + 2 * n + 2)]).then_inc(evac_done, 1)
        mixer_out(KT - 2, 0, slice(0, T), [(mm_done, S_OUT + 2 * KT - 2)]).then_inc(evac_done, 1)
        mixer_out(KT - 1, 1, cols(0), [(half_mm, 1)]).then_inc(half_ev, 1)
        for k in range(KT):
            act.dma_start(x_raw[:, k, cols(0)], xT[k * P:(k + 1) * P, cols(0)]).then_inc(x_in[k], 16)
        mixer_out(KT - 1, 1, cols(1), [(mm_done, S_OUT + 2 * KT)]).then_inc(evac_done, 1)

        def weight_high(S):
            act.wait_ge(w_loaded[1], 16 * (S // 2 + 1))
            act.wait_ge(mm_done, S)
            act.wait_ge(w_hi_done, S + 1)
            A(w_hi[:, 1, :], w_raw[:, 1, :], ACT.Copy).then_inc(w_hi_done, 1)

        weight_high(S_GATE)
        for k in range(KT):
            act.wait_ge(x_in[k], 32)
            act.dma_start(x_raw[:, k, cols(1)], xT[k * P:(k + 1) * P, cols(1)]).then_inc(x_in[k], 16)
        for h in range(2):
            for k in range(KT):
                act.wait_ge((half_val, val_done)[h], (0, 2 * KT)[h] + k + 1)
                A(xh[:, k, cols(h)], xres[:, k, cols(h)], ACT.Copy).then_inc((half_hi, hi_done)[h], 1)

        with act.Fori(0, KT // 2) as j:
            for u in range(2):
                i = j * 2 + u
                act.wait_ge(val_done, 3 * KT + i)
                act.dma_start(eb[:], tile_of(pp_d, i)).then_inc(pp_in[u], 16)
                act.wait_ge(mm_done, S_GATE + i + 1)
                A(ea[:], pt[:, u, :], ACT.Tanh, scale=0.5).then_inc(evac_done, 1)
                act.wait_ge(val_done, 3 * KT + i + 1)
                A(h2[:, ds(i, 1), :], xres[:, ds(i, 1), :], ACT.Copy).then_inc(hi_done, 1)

        act.wait_ge(lo_done, 5 * KT)
        act.dma_start(wl_raw[:], w_low.rearrange("(k p) h -> p k h", p=P)).then_inc(b2_in, 16)
        act.dma_start(blow[0:RANK, :], b_low).then_inc(b2_in, 16)
        act.dma_start(wg2[0:RANK, :], w_gate2).then_inc(b2_in, 16)
        act.dma_start(wg2[RANK:RANK + 1, :], b_gate).then_inc(b2_in, 16)
        act.dma_start(wst[:], sg_w).then_inc(b2_in, 16)
        act.dma_start(rg[:].rearrange("p g t -> p (g t)"), sg_bs.to_broadcast([P, D])).then_inc(b2_in, 16)
        act.wait_ge(b2_in, 96)
        A(wl_hi[:], wl_raw[:], ACT.Copy).then_inc(wl_done, 1)
        with act.Fori(0, KT // 2) as j:
            for u in range(2):
                i = j * 2 + u
                act.wait_ge(mm_done, S_AV + i + 1)
                act.wait_ge(tr_done, j * 2)
                A(ebuf[:, u, :], pt[:, u, :], ACT.Gelu_apprx_tanh, bias=V("b_v", i)).then_inc(evac_done, 1)
        act.wait_ge(low_mm, 1)
        act.wait_ge(wl_done, 3)
        A(alow[0:RANK, :], wkb[0:RANK, :], ACT.Identity, bias=blow[0:RANK, :]).then_inc(low_done, 1)
        act.wait_ge(low_done, 1)
        act.wait_ge(tr_done, KT)
        A(alc[0:RANK + 1, 0, :], alow[0:RANK + 1, 0:P], ACT.Copy).then_inc(alc_done, 1)
        with act.Fori(0, KT // 2) as j:
            for u in range(2):
                i = j * 2 + u
                act.wait_ge(z_mm, i + 1)
                act.wait_ge(z_dve, i)
                A(ga_[:], wk[:, 0, :], ACT.Abs).then_inc(z_act, 1)
                act.wait_ge(z_act, i * 3 + 1)
                A(ge_[:], ga_[:], ACT.Exp, scale=-1.0).then_inc(z_act, 1)
                act.wait_ge(z_act, i * 3 + 2)
                A(gl_[:], ge_[:], ACT.Ln, bias=ones[:, 0:1]).then_inc(z_act, 1)
                A(alc[0:RANK + 1, 1 - u, :], alow[0:RANK + 1, ds((i + 1) % C * P, P)], ACT.Copy).then_inc(alc_done, 1)
                act.wait_ge(mm_done, S_QK + i + 1)
                act.wait_ge(qk_put[u], j * 16)
                A(ebuf[:, u, :], pt[:, u, :], ACT.Identity, scale=V("qk_s", i), bias=V("qk_b", i)).then_inc(evac_done, 1)
                act.wait_ge(evac_done, N_QK + i + 1)
                act.dma_start(tile_of(qk_d, i), ebuf[:, u, :]).then_inc(qk_put[u], 16)
                act.wait_ge(cu_mm, i + 1)
                act.wait_ge(cu_put, i * 16)
                A(cu_o[:], wk[:, 1, :], ACT.Copy, scale=1.0 / TEMP).then_inc(cu_done, 1)
                act.wait_ge(cu_done, i + 1)
                act.dma_start(tile_of(cu_d, i), cu_o[:]).then_inc(cu_put, 16)
        act.wait_ge(qk_put[0], 64)
        act.wait_ge(qk_put[1], 64)
        act.wait_ge(cu_put, 128)
        with act.Fori(0, KT // 2) as j:
            for u in range(2):
                i = j * 2 + u
                act.wait_ge(mm_done, S_VAL + i + 1)
                act.wait_ge(tr_done, j * 2 + KT)
                A(ebuf[:, u, :], pt[:, u, :], ACT.Identity, bias=V("b_val", i)).then_inc(evac_done, 1)
            for u in range(2):
                i = j * 2 + u
                act.wait_ge(tr_used, KT + i + 1)
                act.dma_start(v_d.rearrange("c p f -> p c f")[:, :, ds(i * P, P)], vb[:, u, :, :]).then_inc(v_put[u], 16)
        act.wait_ge(mix_mm, KT)

        def load_chunk(i):
            act.dma_start(qkc[:, 0:2, :, :].rearrange("p a h t -> p (a h) t"),
                          qk_d.rearrange("i p t -> p i t")[:, :, ds(i * P, P)]).then_inc(ch_in, 16)
            act.dma_start(qkc[:, 2, :, :].rearrange("p h t -> p (h t)"), tile_of(cu_d, i)).then_inc(ch_in, 16)

        load_chunk(0)
        act.wait_ge(gst_done, 1)
        with act.Fori(0, C // 2) as j:
            for u in range(2):
                i = j * 2 + u
                S = S_G + j * 6 + 3 * u
                if_slot = [(u + n) % 2 for n in range(3)]
                act.wait_ge(ch_in, i * 32 + 32)
                act.wait_ge(gst_done, i + 1)
                A(qe[:], qkc[:, 2, :, :], ACT.Exp).then_inc(end_exp, 1)
                A(etot[:], qkc[:, 2, :, P - 1], ACT.Exp).then_inc(end_exp, 1)
                for n in range(7):
                    act.wait_ge(arg_done, i * 7 + n + 1)
                    A(darg[:, n % 2, :, :], darg[:, n % 2, :, :], ACT.Exp).then_inc(lev_exp, 1)
                    if n == 1:
                        act.wait_ge(v_put[0], 64)
                        act.wait_ge(v_put[1], 64)
                        act.dma_start(vc[:], tile_of(v_d, i)).then_inc(vc_in, 16)
                    if n == 2:
                        act.wait_ge(end_arg, i + 1)
                        A(kd[:], kd[:], ACT.Exp).then_inc(end_exp, 1)
                    if n == 5:
                        act.wait_ge(mm_done, S + 1)
                        act.wait_ge(gb_done, i)
                        A(ea[:], pt[:, if_slot[0], :], ACT.Tanh, scale=0.5, bias=V("half_ga", i)).then_inc(evac_done, 1)
                act.wait_ge(mm_done, S + 2)
                A(eb[:], pt[:, if_slot[1], :], ACT.Identity, scale=V("half_gn", i), bias=V("half_rgn", i))
                A(ec[:], pt[:, if_slot[1], :], ACT.Tanh, scale=0.5, bias=V("half_r", i)).then_inc(evac_done, 1)
                act.wait_ge(kdt_mm, i + 1)
                A(kdt[:], wk[:, 3, :].rearrange("p (h t) -> p h t", h=GH), ACT.Copy).then_inc(kdt_done, 1)
                act.wait_ge(o_mm, i + 1)
                act.wait_ge(o_put, i * 16)
                A(oc[:], wka.rearrange("p (i t) -> p i t", i=8), ACT.Copy)
                A(osq[:], wka.rearrange("p (i t) -> p i t", i=8), ACT.Square).then_inc(o_act, 1)
                act.wait_ge(su_mm, i + 1)
                load_chunk((i + 1) % C)
                act.wait_ge(mm_done, S + 3)
                act.wait_ge(ga_done, i + 1)
                A(ea[:], pt[:, if_slot[2], :], ACT.Tanh, scale=0.5, bias=V("half_gb", i)).then_inc(evac_done, 1)
                act.wait_ge(on_done, i + 1)
                act.dma_start(o_d.rearrange("i p t -> p i t")[:, :, ds(i * P, P)], oc[:]).then_inc(o_put, 16)
        act.wait_ge(o_put, 128)
        act.wait_ge(gb_done, C)
        act.wait_ge(ch_in, (C + 1) * 32)

        with act.Fori(0, KT // 2) as j:
            for u in range(2):
                i = j * 2 + u
                act.wait_ge(lo_done, 5 * KT + i)
                act.dma_start(eb[:], tile_of(o_d, i)).then_inc(o_in, 16)
                act.wait_ge(mm_done, S_U + i + 1)
                A(ea[:], pt[:, u, :], ACT.Gelu_apprx_tanh, bias=V("b_u", i)).then_inc(evac_done, 1)
                act.wait_ge(m_done, i + 1)
                A(mh[:, ds(i, 1), :].rearrange("p a t -> p (a t)"), ea[:], ACT.Copy, scale=0.5).then_inc(hi_done, 1)
        act.wait_ge(lo_done, 6 * KT)
        with act.Fori(0, KT // 2 - 1) as j:
            for u in range(2):
                n = j * 2 + u
                act.wait_ge(mm_done, S_OUT2 + n + 1)
                act.wait_ge(y_done, n)
                A(ea[:], pt[:, u, :], ACT.Copy).then_inc(evac_done, 1)
                act.wait_ge(y_done, n + 1)
                act.wait_ge(a_used, n)
                A(eb[:], yr[:, ds(n, 1), :].rearrange("p a t -> p (a t)"), ACT.Square).then_inc(sq_done, 1)
        for h in range(2):
            for u in range(2):
                n = KT - 2 + u
                act.wait_ge((half_mm, mm_done)[h], (2 + u, S_OUT2 + n + 1)[h])
                act.wait_ge((y_done, half_y)[h], (KT - 2, 1 + u)[h])
                A(ea[:, cols(u)], pt[:, u, cols(h)], ACT.Copy).then_inc((half_ev, evac_done)[h], 1)
                act.wait_ge((half_y, y_done)[h], (1 + u, n + 1)[h])
                act.wait_ge((a_used, half_acc)[h], (KT - 2, 2 + u)[h])
                A(eb[:, cols(u)], yr[:, n, cols(h)], ACT.Square).then_inc((half_sq, sq_done)[h], 1)
        weight_high(S_FF)
        for h in range(2):
            for k in range(KT):
                q = h * KT + k
                act.wait_ge(ln_done, q + 1)
                A(yr[:, k, cols(h)], nrm[:, q % 2, :], ACT.Identity, scale=V("ln1_g", k), bias=V("ln1_b", k)).then_inc(h_done, 1)
                act.wait_ge(h_done, q + 1)
                A(h2[:, k, cols(h)], yr[:, k, cols(h)], ACT.Copy).then_inc((half_hi, hi_done)[h], 1)
        def ff1(b):
            with act.Fori(0, KT // 2) as j:
                for u in range(2):
                    i = b * KT + j * 2 + u
                    act.wait_ge(mm_done, S_FF + b * 16 + j * 2 + u + 1)
                    act.wait_ge(f_lo, b * KT + j * 2)
                    A(ebuf[:, u, :], pt[:, u, :], ACT.Relu).then_inc(evac_done, 1)
                    act.wait_ge(f_sq, i + 1)
                    A(fh[:, ds(j * 2 + u, 1), :].rearrange("p a t -> p (a t)"), ebuf[:, u, :], ACT.Copy).then_inc(f_hi, 1)

        def ff2(b, pairs):
            with act.Fori(0, pairs) as j:
                for u in range(2):
                    i = b * KT + j * 2 + u
                    act.wait_ge(mm_done, S_FF + b * 16 + 8 + j * 2 + u + 1)
                    act.wait_ge(f_lo, b * KT + KT)
                    act.wait_ge(f_acc, b * KT + j * 2 + KT)
                    A(ebuf[:, u, :], pt[:, u, :], ACT.Copy).then_inc(evac_done, 1)
                    act.wait_ge(f_acc, i + (KT + 1))
                    act.wait_ge(a_used, KT + i)
                    A(ec[:], yr[:, ds(j * 2 + u, 1), :].rearrange("p a t -> p (a t)"), ACT.Square).then_inc(sq_done, 1)

        with act.Fori(0, FF_BLOCKS - 1) as b:
            ff1(b)
            ff2(b, KT // 2)
        ff1(FF_BLOCKS - 1)
        ff2(FF_BLOCKS - 1, KT // 2 - 1)
        for h in range(2):
            for u in range(2):
                n = KT - 2 + u
                act.wait_ge((half_mm, mm_done)[h], (4 + u, S_ALL - 1 + u)[h])
                act.wait_ge(f_acc, KT * FF_BLOCKS + KT - 2)
                A(ebuf[:, u, cols(h)], pt[:, u, cols(h)], ACT.Copy).then_inc((half_ev, evac_done)[h], 1)
                act.wait_ge((half_y, f_acc)[h], (3 + u, KT * FF_BLOCKS + n + 1)[h])
                act.wait_ge((a_used, half_acc)[h], (KT * FF_BLOCKS + KT - 2, 4 + u)[h])
                A(ec[:, cols(u)], yr[:, n, cols(h)], ACT.Square).then_inc((half_sq, sq_done)[h], 1)
        for h in range(2):
            for k in range(KT):
                q = h * KT + k
                act.wait_ge(ln_done, 2 * KT + q + 1)
                A(yr[:, k, cols(h)], nrm2[:, q % 2, :], ACT.Identity, scale=V("ln2_g", k), bias=V("ln2_b", k)).then_inc(h_done, 1)
                act.wait_ge(h_done, 2 * KT + q + 1)
                act.dma_start(outT[k * P:(k + 1) * P, cols(h)], yr[:, k, cols(h)]).then_inc(out_put, 16)
        act.wait_ge(out_put, 2 * KT * 16)

    @block.vector
    def _(dve):
        link = Chain(dve, d_chain)
        TT, TS, STT = nc.vector.tensor_tensor, nc.vector.tensor_scalar, nc.vector.scalar_tensor_tensor

        def rsqrt(y, v, t, done=None):
            link(TS(t.bitcast(i32), v.bitcast(i32), 1, None, ALU.arith_shift_right))
            link(TS(y.bitcast(i32), t.bitcast(i32), -1, 0x5f3759df, ALU.mult, ALU.add))
            for n in range(3):
                link(STT(out=t, in0=y, scalar=-0.5, in1=y, op0=ALU.mult, op1=ALU.mult))
                link(TT(out=t, in0=t, in1=v, op=ALU.mult))
                ins = STT(out=y, in0=t, scalar=1.5, in1=y, op0=ALU.add, op1=ALU.mult)
                if n < 2 or done is None:
                    link(ins)
                else:
                    ins.then_inc(done, 1)

        GLA_LINKS = 11

        link(nc.vector.memset(raw_p[:, :, 0:CW - 1], 0.0))
        dve.wait_ge(vec_in, 16)
        for k in range(2):
            dve.wait_ge(p_hi_done, k + 1)
            TT(out=p_lo[:, k, :], in0=p_raw[:, k, :], in1=p_hi[:, k, :].bitcast(f32), op=ALU.subtract).then_inc(p_lo_done, 1)
        dve.wait_ge(cst, 1 + len(LEVELS))
        link(nc.vector.tensor_copy(lmask[:], lmask_f[:]))
        for new, old in (("half_ga", "b_ga"), ("half_r", "b_r"), ("half_gb", "b_gb"), ("half_gn", "gn")):
            link(TS(V(new, 0, 8), V(old, 0, 8), 0.5, None, ALU.mult))
        link(TT(out=V("half_rgn", 0, 8), in0=V("half_gn", 0, 8), in1=V("b_r", 0, 8), op=ALU.mult))
        link(nc.vector.memset(V("qk_s", 0, 4), Q_SCALE))
        link(nc.vector.memset(V("qk_s", 4, 4), 1.0))
        link(TT(out=V("qk_b", 0, 8), in0=V("qk_s", 0, 8), in1=V("b_qk", 0, 8), op=ALU.mult))

        for k in range(KT):
            dve.wait_ge(sq_done, k + 1)
            if k == 0:
                nc.vector.tensor_copy(acc_a[:], ec[:]).then_inc(sq_used, 1)
            else:
                dve.wait_ge(sq_used, k)
                TT(out=acc_a[:], in0=acc_a[:], in1=ec[:], op=ALU.add).then_inc(sq_used, 1)

        def scale_of(eps, width):
            link(TS(sm[:, 8:16], wk[:, 3, 0:8], 1.0 / width, eps, ALU.mult, ALU.add))
            rsqrt(sm[:, 0:8], sm[:, 8:16], sm[:, 16:24], rstd_done)

        dve.wait_ge(stat_done, 1)
        scale_of(EPS1, D)
        dve.wait_ge(wdt_done, 1)
        TT(out=wdt_lo[:], in0=wdt_raw[:], in1=wdt_hi[:].bitcast(f32), op=ALU.subtract).then_inc(wdt_done, 1)
        dve.wait_ge(spread_done, 1)
        for k in range(KT):
            STT(out=x_raw[:, k, :], in0=x_raw[:, k, :], scalar=V("norm_pre", k), in1=wka, op0=ALU.mult,
                op1=ALU.mult).then_inc(val_done, 1)
            dve.wait_ge(hi_done, k + 1)
            TT(out=xl[:, k, :], in0=x_raw[:, k, :], in1=xh[:, k, :].bitcast(f32), op=ALU.subtract).then_inc(lo_done, 1)

        def conv_pair(j):
            for u in range(2):
                dve.wait_ge(evac_done, j * 2 + (N_XBC + u + 1))
                dve.wait_ge(silu_done, j * 2)
                link(TS(conv_o[:, u, :], raw_p[:, u, 0:T], V("conv_w", j * 2 + u), V("conv_b", j * 2 + u), ALU.mult, ALU.add))
                for k in range(1, CW):
                    ins = STT(out=conv_o[:, u, :], in0=raw_p[:, u, k:k + T], scalar=V("conv_w", j * 2 + (u + k * XBC_T)),
                              in1=conv_o[:, u, :], op0=ALU.mult, op1=ALU.add)
                    if k < CW - 1:
                        link(ins)
                    else:
                        ins.then_inc(conv_done, 1)

        conv_pair(0)
        conv_pair(1)
        v, r_, e_, u_, l_, z_, q_, g_ = tmps
        ch = lambda t: t[:].rearrange("p (c h) -> p c h", c=C)
        dve.wait_ge(dt_mm, 2)
        TT(out=ch(v), in0=wk[:, 3, 0:P].rearrange("p (c h) -> p c h", c=C),
           in1=dtb[:].unsqueeze(1).to_broadcast([P, C, HEADS]), op=ALU.add).then_inc(dt_a, 1)
        dve.wait_ge(dt_a, 1)
        link(TS(r_[:], v[:], 0.0, None, ALU.max))
        dve.wait_ge(dt_b, 1)
        TS(u_[:], e_[:], 1.0, None, ALU.add).then_inc(dt_a, 1)
        dve.wait_ge(dt_a, 2)
        link(TS(q_[:], u_[:], -1.0, None, ALU.add))
        link(TS(z_[:], q_[:], 0.0, None, ALU.is_equal))
        link(TT(out=q_[:], in0=q_[:], in1=z_[:], op=ALU.add))
        link(nc.vector.reciprocal(g_[:], q_[:]))
        link(TT(out=q_[:], in0=g_[:], in1=e_[:], op=ALU.mult))
        dve.wait_ge(dt_b, 3)
        link(TT(out=q_[:], in0=q_[:], in1=l_[:], op=ALU.mult))
        link(TT(out=z_[:], in0=z_[:], in1=e_[:], op=ALU.mult))
        link(TT(out=q_[:], in0=q_[:], in1=z_[:], op=ALU.add))
        link(TT(out=dtt[:], in0=ch(q_), in1=ch(r_), op=ALU.add))
        link(TS(alr[:], alr[:], -1.0, None, ALU.mult))
        TT(out=adt[:], in0=dtt[:], in1=alr[:].unsqueeze(1).to_broadcast([P, C, HEADS]), op=ALU.mult).then_inc(adt_done, 1)

        with dve.Fori(2, XBC_T // 2 - 1) as j:
            link.enter(j - 2, 2 * (CW - 1))
            conv_pair(j)
        link.leave(XBC_T // 2 - 3)

        dve.wait_ge(dec_done, 2)
        TT(out=dec[:], in0=wk[:, 3, P:2 * P], in1=acs[:].rearrange("p c h -> p (c h)"), op=ALU.subtract).then_inc(dec_arg, 1)
        conv_pair(XBC_T // 2 - 1)
        nc.vector.memset(state[:], 0.0)
        link(nc.vector.memset(ecp[:, 0:SW - 1], 0.0))
        dve.wait_ge(dec_done, 3)

        SC_LINKS = 7
        with dve.Fori(0, C) as j:
            link.enter(j, SC_LINKS)
            N = N_SC + j * 4
            dve.wait_ge(row_in, j * 16 + 16)
            dve.wait_ge(ce_exp, j * 2 + 2)
            for h in range(HEADS):
                ins = TS(rowb[:, h, :], rowb[:, h, :], acs[:].rearrange("p c h -> p (c h)")[:, ds(j * HEADS + h, 1)],
                         0.0, ALU.subtract, ALU.min)
            ins.then_inc(e_arg, 1)
            dve.wait_ge(ssd_a, j + 1)
            dts = dtt[:, ds(j, 1), :].rearrange("p a h -> p (a h)").unsqueeze(2).to_broadcast([P, HEADS, HP])
            link(TT(out=xd[:], in0=wka.rearrange("p (h q) -> p h q", h=HEADS), in1=dts, op=ALU.mult))
            decs = dec[:, ds(j * HEADS, HEADS)].unsqueeze(2).to_broadcast([P, HEADS, HP])
            TT(out=xdd[:], in0=xd[:], in1=decs, op=ALU.mult).then_inc(xdd_done, 1)
            dve.wait_ge(bt_done, j + 1)
            for g in range(GROUPS):
                cb_src = wk[:, 2, P:2 * P] if g == 0 else wk[:, 3, 0:P]
                ins = TT(out=cbm[:, g, :], in0=cb_src, in1=tri[:], op=ALU.mult)
            link(ins)
            TT(out=ce[:], in0=ce[:], in1=st[:, XBC_T - 1, :].unsqueeze(1).to_broadcast([P, HG, P]),
               op=ALU.mult).then_inc(ce_done, 1)
            dve.wait_ge(e_exp, j + 1)
            for g in range(GROUPS):
                ins = TT(out=rowb[:, g * HG:(g + 1) * HG, :], in0=rowb[:, g * HG:(g + 1) * HG, :],
                         in1=cbm[:, g, :].unsqueeze(1).to_broadcast([P, HG, P]), op=ALU.mult)
            ins.then_inc(m_ready, 1)
            dve.wait_ge(evac_done, N + 1)
            STT(out=eb[:], in0=eb[:], scalar=1.0, in1=ea[:], op0=ALU.add, op1=ALU.mult).then_inc(sz_done, 1)
            dve.wait_ge(ssd_b, j + 1)
            for i in range(KT):
                ins = STT(out=xbc[:, i, ds(j * P, P)], in0=st[:, i, :], scalar=V("d_skip", i),
                          in1=wka[:, i * P:(i + 1) * P], op0=ALU.mult, op1=ALU.add)
            ins.then_inc(y_evac, 1)
            for g in range(GROUPS):
                rows, hs = slice(g * 64, g * 64 + 64), slice(g * HG, (g + 1) * HG)
                ins = TT(out=state[rows, hs, :], in0=state[rows, hs, :],
                         in1=et2[rows, ds(j, 1), :].rearrange("p a h -> p (a h)").unsqueeze(2).to_broadcast([64, HG, HP]),
                         op=ALU.mult)
            link(ins)
            for g in range(GROUPS):
                rows, hs = slice(g * 64, g * 64 + 64), slice(g * HG, (g + 1) * HG)
                ins = TT(out=state[rows, hs, :], in0=state[rows, hs, :],
                         in1=wk[rows, 3, :].rearrange("p (h q) -> p h q", h=HG), op=ALU.add)
            ins.then_inc(s_ready, 1)
            dve.wait_ge(evac_done, N + 3)
            TT(out=ecp[:, SW - 1:SW - 1 + T], in0=ea[:], in1=eb[:], op=ALU.mult).then_inc(u_done, 1)
            dve.wait_ge(u_done, j + 1)
            vj = row(vbuf, j)
            link(TS(vj, ecp[:, 0:T], V("sc_w", j), None, ALU.mult))
            for k in range(1, SW):
                link(STT(out=vj, in0=ecp[:, k:k + T], scalar=V("sc_w", j + 8 * k), in1=vj, op0=ALU.mult, op1=ALU.add))
            dve.wait_ge(evac_done, N + 4)
            link(STT(out=ea[:], in0=eb[:], scalar=1.0, in1=ea[:], op0=ALU.add, op1=ALU.mult))
            TT(out=vj, in0=vj, in1=ea[:], op=ALU.mult).then_inc(v_done, 1)
        link.leave(C)

        dve.wait_ge(y_evac, C)
        def gated(i):
            acc = acc_g[:, i // 4, :]
            buf = eb if i % 2 == 0 else ec
            dve.wait_ge(sz_in[i % 2], 16 * (i // 2 + 1))
            TT(out=xbc[:, i, :], in0=xbc[:, i, :], in1=buf[:], op=ALU.mult).then_inc(yz_done, 1)
            if i:
                dve.wait_ge(sq_used, KT + i)
            dve.wait_ge(sq_done, KT + i + 1)
            if i % 4 == 0:
                nc.vector.tensor_copy(acc, acc_b[:]).then_inc(sq_used, 1)
            else:
                TT(out=acc, in0=acc, in1=acc_b[:], op=ALU.add).then_inc(sq_used, 1)

        def branch(i):
            dve.wait_ge(evac_done, N_SB + i + 1)
            TT(out=vbuf[:, i, :], in0=vbuf[:, i, :], in1=ea[:], op=ALU.mult).then_inc(ys_done, 1)
            dve.wait_ge(hi_done, KT + i + 1)
            TT(out=sl[:, i, :], in0=vbuf[:, i, :], in1=sh[:, i, :].bitcast(f32), op=ALU.subtract).then_inc(lo_done, 1)

        for i in range(KT):
            gated(i)
            if i in (3, 5):
                branch((i - 3) // 2)
        for i in range(2, 4):
            branch(i)
        dve.wait_ge(stat_done, 2)
        link(TS(sm[:, 16:32], wk[:, 3, 0:16], 2.0 / D, EPS1, ALU.mult, ALU.add))
        rsqrt(sm[:, 0:16], sm[:, 16:32], sm[:, 32:48], rstd_done)
        for i in range(4, 6):
            branch(i)
        dve.wait_ge(spread_done, 2)
        for i in range(KT):
            STT(out=xbc[:, i, :], in0=xbc[:, i, :], scalar=V("ssd_norm", i), in1=wka if i < 4 else wkb, op0=ALU.mult,
                op1=ALU.mult).then_inc(val_done, 1)
        for i in range(6, KT):
            branch(i)
        for i in range(KT):
            dve.wait_ge(hi_done, 2 * KT + i + 1)
            TT(out=yl[:, i, :], in0=xbc[:, i, :], in1=yh[:, i, :].bitcast(f32), op=ALU.subtract).then_inc(lo_done, 1)

        link(nc.vector.memset(acc_a[:], 0.0))
        with dve.Fori(0, KT // 2 - 1) as j:
            for u in range(2):
                n = j * 2 + u
                dve.wait_ge(evac_done, N_OUT + n + 1)
                dve.wait_ge(sq_used, 2 * KT + n)
                TT(out=acc_a[:], in0=acc_a[:], in1=eb[:], op=ALU.add).then_inc(sq_used, 1)
        dve.wait_ge(evac_done, N_OUT + KT - 1)
        dve.wait_ge(sq_used, 3 * KT - 2)
        TT(out=acc_a[:], in0=acc_a[:], in1=eb[:], op=ALU.add).then_inc(sq_used, 1)

        def last_squares(h):
            dve.wait_ge((half_ev, evac_done)[h], (1, N_OUT + KT)[h])
            dve.wait_ge(sq_used, 3 * KT - 1)
            TT(out=acc_a[:, cols(h)], in0=acc_a[:, cols(h)], in1=eb[:, cols(h)], op=ALU.add).then_inc((half_acc, sq_used)[h], 1)

        def half_scale(h):
            dve.wait_ge(stat_done, 3 + h)
            a, b = 4 * h, 4 * h + 4
            link(TS(sm[:, 8 + a:8 + b], wk[:, 3, a:b], 1.0 / D, EPS1, ALU.mult, ALU.add))
            rsqrt(sm[:, a:b], sm[:, 8 + a:8 + b], sm[:, 16 + a:16 + b], rstd_done)

        def weight_low(S):
            dve.wait_ge(w_hi_done, S + 2)
            dve.wait_ge(w_split, S + 1)
            TT(out=w_lo[:, 1, :], in0=w_raw[:, 1, :], in1=w_hi[:, 1, :].bitcast(f32), op=ALU.subtract).then_inc(w_split, 1)

        def residual(q):
            h, k = divmod(q, KT)
            c = cols(h)
            dve.wait_ge(spread_done, 3 + h)
            link(STT(out=nrm[:, q % 2, :], in0=mm[:, k, c], scalar=V("norm_post", k), in1=wka[:, c], op0=ALU.mult, op1=ALU.mult))
            dve.wait_ge(x_in[k], 32 + 16 * h)
            TT(out=xres[:, k, c], in0=xres[:, k, c], in1=nrm[:, q % 2, :], op=ALU.add).then_inc((half_val, val_done)[h], 1)

        last_squares(0)
        half_scale(0)
        residual(0)
        last_squares(1)
        residual(1)
        weight_low(S_GATE)
        for q in range(2, 5):
            residual(q)
        half_scale(1)
        for q in range(5, 2 * KT):
            residual(q)
        with dve.Fori(0, KT // 2) as j:
            link.enter(j, 2)
            for u in range(2):
                i = j * 2 + u
                dve.wait_ge(evac_done, N_GATE + i + 1)
                dve.wait_ge(pp_in[u], j * 16 + 16)
                link(STT(out=ea[:], in0=ea[:], scalar=1.0, in1=eb[:], op0=ALU.add, op1=ALU.mult))
                TT(out=row(xres, i), in0=row(xres, i), in1=ea[:], op=ALU.add).then_inc(val_done, 1)
                dve.wait_ge(val_done, 3 * KT + i + 1)
                dve.wait_ge(hi_done, 4 * KT + i + 1)
                TT(out=row(l2, i), in0=row(xres, i), in1=row(h2, i).bitcast(f32), op=ALU.subtract).then_inc(lo_done, 1)
        link.leave(KT // 2)

        dve.wait_ge(b2_in, 96)
        dve.wait_ge(wl_done, 1)
        TT(out=wl_lo[:], in0=wl_raw[:], in1=wl_hi[:].bitcast(f32), op=ALU.subtract).then_inc(wl_done, 1)
        nc.vector.memset(alow[0:RANK + 1, :], 1.0).then_inc(wl_done, 1)
        TT(out=wst[:], in0=wst[:], in1=tri[:].unsqueeze(1).to_broadcast([P, KT, P]), op=ALU.mult).then_inc(ws_done, 1)
        with dve.Fori(0, KT // 2) as j:
            for u in range(2):
                i = j * 2 + u
                dve.wait_ge(tr_done, i + 1)
                nc.vector.tensor_copy(av[:, :, ds(i * P, P)], wka.rearrange("p (c f) -> p c f", c=C)).then_inc(tr_used, 1)
        dve.wait_ge(tr_used, KT)
        dve.wait_ge(row_mm, 1)
        for g in range(KT):
            ins = STT(out=rg[:, g, :], in0=wka[:, g * P:(g + 1) * P], scalar=V("sg_b", g), in1=rg[:, g, :],
                      op0=ALU.mult, op1=ALU.add)
        ins.then_inc(rg_done, 1)
        with dve.Fori(0, KT // 2) as j:
            link.enter(j, 2)
            for u in range(2):
                i = j * 2 + u
                dve.wait_ge(z_mm, i + 1)
                dve.wait_ge(z_dve, i)
                dve.wait_ge(cu_mm, i)
                dve.wait_ge(z_act, i * 3 + 1)
                link(TS(gm_[:], wk[:, 0, :], 0.0, None, ALU.min))
                dve.wait_ge(z_act, i * 3 + 3)
                TT(out=gm_[:], in0=gm_[:], in1=gl_[:], op=ALU.subtract).then_inc(z_dve, 1)
                for h in range(2):
                    ins = nc.vector.bn_stats(row(bnst, i * 2 + h), av[:, ds(i, 1), h * HALF:(h + 1) * HALF].rearrange("p a f -> p (a f)"))
                ins.then_inc(bn_done, 1)
        link.leave(KT // 2)
        dve.wait_ge(bn_done, C)
        for c in range(C):
            ins = nc.vector.bn_aggr(bnag[:, c, :], bnst[:, 2 * c:2 * c + 2, :].rearrange("p h s -> p (h s)"))
        link(ins)
        link(TS(sm[:, 8:16], bnag[:, :, 1], EPS2, None, ALU.add))
        rsqrt(sm[:, 0:8], sm[:, 8:16], sm[:, 16:24], rstd_done)
        dve.wait_ge(rstd_done, 5)
        link(STT(out=sm[:, 24:32], in0=bnag[:, :, 0], scalar=-1.0, in1=sm[:, 0:8], op0=ALU.mult, op1=ALU.mult))
        for c in range(C):
            TS(av[:, c, :], av[:, c, :], sm[:, c:c + 1], sm[:, 24 + c:25 + c], ALU.mult, ALU.add).then_inc(av_done, 1)
        def value(i):
            dve.wait_ge(tr_done, i + (KT + 1))
            if i >= 2:
                dve.wait_ge(v_put[i % 2], 16 * (i // 2))
            nc.vector.tensor_copy(vb[:, i % 2, :, :], wka.rearrange("p (c f) -> p c f", c=C)).then_inc(tr_used, 1)

        def mixed(g):
            dve.wait_ge(mix_mm, g + 1)
            STT(out=mix[:, g, :].rearrange("p (c t) -> p c t", c=C), in0=wkb.rearrange("p (c t) -> p c t", c=C),
                scalar=V("sg_g", g), in1=rg[:, g, :].unsqueeze(1).to_broadcast([P, C, P]), op0=ALU.mult,
                op1=ALU.add).then_inc(mix_done, 1)

        for i in range(KT - 1):
            value(i)
            mixed(i)
        mixed(KT - 1)
        value(KT - 1)

        link(nc.vector.memset(gst[:], 0.0))
        link(nc.vector.memset(sc[:], 0.0))
        link(nc.vector.memset(kp[:], 0.0))
        nc.vector.memset(qc[:], 0.0).then_inc(gst_done, 1)

        def second(ap, m):
            return ap.rearrange("p h (b two r) -> p (h b) two r", two=2, r=m)[:, :, 1, :]

        def first(ap, m):
            return ap.rearrange("p h (b two r) -> p (h b) two r", two=2, r=m)[:, :, 0, :]

        with dve.Fori(0, C // 2) as j:
            link.enter(j, 2 * GLA_LINKS)
            for u in range(2):
                i = j * 2 + u
                N = N_G + j * 6 + 3 * u
                q_, k_, c_ = qkc[:, 0, :, :], qkc[:, 1, :, :], qkc[:, 2, :, :]
                slots = [(u + n) % 2 for n in range(3)]

                def args(n):
                    m = LEVELS[n]
                    ref = c_.rearrange("p h (b two r) -> p (h b) two r", two=2, r=m)[:, :, 0, m - 1:m]
                    ref = ref.to_broadcast([P, 256 // m, m])
                    if n >= 2:
                        dve.wait_ge(lev_ready, i * 7 + n - 1)
                    d = darg[:, n % 2, :, :].rearrange("p a (b r) -> p a b r", r=m)
                    TT(out=d[:, 0], in0=second(c_, m), in1=ref, op=ALU.subtract)
                    TT(out=d[:, 1], in0=ref, in1=first(c_, m), op=ALU.subtract).then_inc(arg_done, 1)

                def scale(n, picked):
                    m = LEVELS[n]
                    dve.wait_ge(lev_exp, i * 7 + n + 1)
                    if n >= 2:
                        dve.wait_ge(lev_mm, i * 7 + n - 1)
                    if picked:
                        dve.wait_ge(lev_used, i * 7 + picked)
                    d = darg[:, n % 2, :, :].rearrange("p a (b r) -> p a b r", r=m)
                    TT(out=qc[:, n % 2, :, :].rearrange("p h (b r) -> p (h b) r", r=m), in0=second(q_, m), in1=d[:, 0], op=ALU.mult)
                    TT(out=first(kp[:, n % 2, :, :], m), in0=first(k_, m), in1=d[:, 1], op=ALU.mult).then_inc(lev_ready, 1)

                def pick(n):
                    m = LEVELS[n]
                    nb = 64 // m
                    dve.wait_ge(cst, 1 + len(LEVELS))
                    dve.wait_ge(lev_mm, i * 7 + n + 1)
                    out = sc[:].rearrange("p h (b two r) -> p h b two r", two=2, r=m)[:, :, :, 1, :]
                    mask = lmask[:, n, :].rearrange("p (b r) -> p b r", r=m).unsqueeze(1).to_broadcast([P, GH, nb, m])
                    src = wk[:, n % 2, 0:256].rearrange("p (h b r) -> p h b r", h=GH, r=m)
                    nc.vector.copy_predicated(out, mask, src).then_inc(lev_used, 1)

                dve.wait_ge(ch_in, i * 32 + 32)
                dve.wait_ge(lev_ready, i * 7)
                args(0)
                args(1)
                scale(0, 0)
                TT(out=kd[:], in0=c_[:, :, P - 1:P].to_broadcast([P, GH, P]), in1=c_, op=ALU.subtract).then_inc(end_arg, 1)
                dve.wait_ge(dg_mm, i + 1)
                args(2)
                dmask = ident[:].bitcast(u32).unsqueeze(1).to_broadcast([P, GH, P])
                nc.vector.copy_predicated(sc[:], dmask, wk[:, 2, :].rearrange("p (h t) -> p h t", h=GH)).then_inc(sc_done, 1)
                dve.wait_ge(sc_done, i + 1)
                scale(1, 0)
                pick(0)
                for n in range(2, 7):
                    if n + 1 < 7:
                        args(n + 1)
                    scale(n, n - 1)
                    pick(n - 1)
                    if n == 3:
                        dve.wait_ge(end_exp, i * 3 + 3)
                        TT(out=qe[:], in0=qe[:], in1=q_, op=ALU.mult)
                        TT(out=kd[:], in0=kd[:], in1=k_, op=ALU.mult).then_inc(kd_done, 1)
                dve.wait_ge(evac_done, N + 1)
                dve.wait_ge(lev_used, i * 7 + 6)
                STT(out=row(mix, i), in0=ea[:], scalar=1.0, in1=row(mix, i), op0=ALU.add, op1=ALU.mult).then_inc(ga_done, 1)
                pick(6)
                dve.wait_ge(evac_done, N + 2)
                STT(out=row(gbuf, i), in0=ec[:], scalar=1.0, in1=eb[:], op0=ALU.add, op1=ALU.mult).then_inc(r_done, 1)
                dve.wait_ge(su_mm, i + 1)
                for h in range(GH):
                    ins = STT(out=gst[:, h, :], in0=gst[:, h, :], scalar=etot[:, h:h + 1],
                              in1=wk[:, 2 + h // 2, (h % 2) * GV:(h % 2 + 1) * GV], op0=ALU.mult, op1=ALU.add)
                ins.then_inc(gst_done, 1)
                dve.wait_ge(o_stat, i + 1)
                link(TS(sm[:, 4:8], wk[:, 0, 0:GH], 1.0 / GV, EPS2, ALU.mult, ALU.add))
                rsqrt(sm[:, 0:4], sm[:, 4:8], sm[:, 8:12], o_rstd)
                dve.wait_ge(evac_done, N + 3)
                dve.wait_ge(r_done, i + 1)
                STT(out=row(gbuf, i), in0=ea[:], scalar=1.0, in1=row(gbuf, i), op0=ALU.add, op1=ALU.mult).then_inc(gb_done, 1)
                dve.wait_ge(o_spread, i + 1)
                TT(out=oc[:].rearrange("p (h w) t -> p h w t", w=2), in0=oc[:].rearrange("p (h w) t -> p h w t", w=2),
                   in1=wk[:, 1, :].rearrange("p (h t) -> p h t", h=GH).unsqueeze(2).to_broadcast([P, GH, 2, P]),
                   op=ALU.mult).then_inc(on_done, 1)
        link.leave(C // 2)

        with dve.Fori(0, KT // 2) as j:
            link.enter(j, 4)
            for u in range(2):
                i = j * 2 + u
                dve.wait_ge(o_in, i * 16 + 16)
                link(TT(out=eb[:], in0=eb[:], in1=row(gbuf, i), op=ALU.mult))
                dve.wait_ge(evac_done, N_U + i + 1)
                link(TT(out=ea[:], in0=ea[:], in1=row(mix, i), op=ALU.mult))
                TT(out=ea[:], in0=ea[:], in1=eb[:], op=ALU.add).then_inc(m_done, 1)
                dve.wait_ge(m_done, i + 1)
                dve.wait_ge(hi_done, 5 * KT + i + 1)
                STT(out=row(ml, i), in0=ea[:], scalar=0.5, in1=row(mh, i).bitcast(f32), op0=ALU.mult,
                    op1=ALU.subtract).then_inc(lo_done, 1)
        link.leave(KT // 2)

        link(nc.vector.memset(acc_a[:], 0.0))
        link(nc.vector.memset(acc_b[:], 0.0))
        with dve.Fori(0, KT // 2 - 1) as j:
            link.enter(j, 2)
            for u in range(2):
                n = j * 2 + u
                dve.wait_ge(evac_done, N_OUT2 + n + 1)
                link(STT(out=ea[:], in0=row(h2, n).bitcast(f32), scalar=ALPHA, in1=ea[:], op0=ALU.mult, op1=ALU.add))
                STT(out=row(yr, n), in0=row(l2, n).bitcast(f32), scalar=ALPHA, in1=ea[:], op0=ALU.mult,
                    op1=ALU.add).then_inc(y_done, 1)
                dve.wait_ge(y_done, n + 1)
                dve.wait_ge(a_used, n)
                TT(out=acc_a[:], in0=acc_a[:], in1=row(yr, n), op=ALU.add)
                dve.wait_ge(sq_done, 2 * KT + n + 1)
                TT(out=acc_b[:], in0=acc_b[:], in1=eb[:], op=ALU.add).then_inc(a_used, 1)
        link.leave(KT // 2 - 1)

        def add_up(h, u, ready, before, squares, sq):
            n, c = KT - 2 + u, cols(h)
            dve.wait_ge(*ready)
            dve.wait_ge(*before)
            TT(out=acc_a[:, c], in0=acc_a[:, c], in1=yr[:, n, c], op=ALU.add)
            dve.wait_ge(*squares)
            TT(out=acc_b[:, c], in0=acc_b[:, c], in1=sq[:, cols(u)], op=ALU.add).then_inc((half_acc, a_used)[h], 1)

        def sums_before(h, u, used, halves):
            if h == 0:
                return (a_used, used) if u == 0 else (half_acc, halves)
            return (a_used, used + u)

        def last_y(h, u):
            n, c, b = KT - 2 + u, cols(h), cols(u)
            dve.wait_ge((half_ev, evac_done)[h], (2 + u, N_OUT2 + n + 1)[h])
            link(STT(out=ea[:, b], in0=h2[:, n, c].bitcast(f32), scalar=ALPHA, in1=ea[:, b], op0=ALU.mult, op1=ALU.add))
            STT(out=yr[:, n, c], in0=l2[:, n, c].bitcast(f32), scalar=ALPHA, in1=ea[:, b], op0=ALU.mult,
                op1=ALU.add).then_inc((half_y, y_done)[h], 1)
            add_up(h, u, ((half_y, 1 + u), (y_done, n + 1))[h], sums_before(h, u, KT - 2, 2),
                   ((half_sq, 1 + u), (sq_done, 2 * KT + n + 1))[h], eb)

        def ln_scale(h, stats):
            dve.wait_ge(stat_done, stats + h)
            a = 4 * h
            mean, var, r = sm[:, 24 + a:28 + a], sm[:, 16 + a:20 + a], sm[:, a:4 + a]
            link(TS(mean, wk[:, 3, a:4 + a], 1.0 / D, None, ALU.mult))
            link(TT(out=var, in0=mean, in1=mean, op=ALU.mult))
            link(STT(out=var, in0=wk[:, 3, 8 + a:12 + a], scalar=1.0 / D, in1=var, op0=ALU.mult, op1=ALU.subtract))
            link(TS(var, var, 0.0, EPS2, ALU.max, ALU.add))
            rsqrt(r, var, sm[:, 32 + a:36 + a])
            STT(out=sm[:, 8 + a:12 + a], in0=mean, scalar=-1.0, in1=r, op0=ALU.mult, op1=ALU.mult).then_inc(rstd_done, 1)

        def normalise(q, buf, count, stats):
            h, k = divmod(q, KT)
            dve.wait_ge(spread_done, stats + h)
            if q >= 2:
                dve.wait_ge(h_done, count + q - 1)
            link(TT(out=buf[:, q % 2, :], in0=yr[:, k, cols(h)], in1=wka[:, cols(h)], op=ALU.mult))
            TT(out=buf[:, q % 2, :], in0=buf[:, q % 2, :], in1=wkb[:, cols(h)], op=ALU.add).then_inc(ln_done, 1)

        last_y(0, 0)
        last_y(0, 1)
        ln_scale(0, 5)
        last_y(1, 0)
        last_y(1, 1)
        normalise(0, nrm, 0, 5)
        weight_low(S_FF)
        normalise(1, nrm, 0, 5)
        normalise(2, nrm, 0, 5)
        ln_scale(1, 5)
        for q in range(3, 2 * KT):
            normalise(q, nrm, 0, 5)
        for k in range(KT):
            dve.wait_ge(lo_done, 6 * KT + k + 1)
            TS(yr[:, k, :], yr[:, k, :], ALPHA, None, ALU.mult).then_inc(f_acc, 1)

        def ff1(b):
            with dve.Fori(0, KT // 2) as j:
                for u in range(2):
                    i = b * KT + j * 2 + u
                    dve.wait_ge(evac_done, N_FF + b * 16 + j * 2 + u + 1)
                    TT(out=ebuf[:, u, :], in0=ebuf[:, u, :], in1=ebuf[:, u, :], op=ALU.mult).then_inc(f_sq, 1)
                    dve.wait_ge(f_sq, i + 1)
                    dve.wait_ge(f_hi, i + 1)
                    TT(out=row(fl, j * 2 + u), in0=ebuf[:, u, :], in1=row(fh, j * 2 + u).bitcast(f32),
                       op=ALU.subtract).then_inc(f_lo, 1)
            nc.vector.memset(acc_a[:], 0.0).then_inc(f_zero, 1)
            nc.vector.memset(acc_b[:], 0.0).then_inc(f_zero, 1)

        def ff2(b, pairs):
            with dve.Fori(0, pairs) as j:
                for u in range(2):
                    i = b * KT + j * 2 + u
                    yn = row(yr, j * 2 + u)
                    dve.wait_ge(evac_done, N_FF + b * 16 + 8 + j * 2 + u + 1)
                    dve.wait_ge(f_acc, i + KT)
                    TT(out=yn, in0=yn, in1=ebuf[:, u, :], op=ALU.add).then_inc(f_acc, 1)
                    dve.wait_ge(f_acc, i + KT + 1)
                    dve.wait_ge(a_used, i + KT)
                    dve.wait_ge(f_zero, b * 2 + 2)
                    TT(out=acc_a[:], in0=acc_a[:], in1=yn, op=ALU.add)
                    dve.wait_ge(sq_done, i + 3 * KT + 1)
                    TT(out=acc_b[:], in0=acc_b[:], in1=ec[:], op=ALU.add).then_inc(a_used, 1)

        with dve.Fori(0, FF_BLOCKS - 1) as b:
            ff1(b)
            ff2(b, KT // 2)
        ff1(FF_BLOCKS - 1)
        ff2(FF_BLOCKS - 1, KT // 2 - 1)

        def last_f(h, u):
            n, c, done = KT - 2 + u, cols(h), KT * FF_BLOCKS
            dve.wait_ge((half_ev, evac_done)[h], (4 + u, N_FF + 16 * FF_BLOCKS - 1 + u)[h])
            dve.wait_ge(f_acc, done + KT - 2)
            TT(out=yr[:, n, c], in0=yr[:, n, c], in1=ebuf[:, u, c], op=ALU.add).then_inc((half_y, f_acc)[h], 1)
            add_up(h, u, ((half_y, 3 + u), (f_acc, done + n + 1))[h], sums_before(h, u, done + KT - 2, 4),
                   ((half_sq, 3 + u), (sq_done, done + 2 * KT + n + 1))[h], ec)

        last_f(0, 0)
        last_f(0, 1)
        ln_scale(0, 7)
        last_f(1, 0)
        last_f(1, 1)
        normalise(0, nrm2, 2 * KT, 7)
        normalise(1, nrm2, 2 * KT, 7)
        ln_scale(1, 7)
        for q in range(2, 2 * KT):
            normalise(q, nrm2, 2 * KT, 7)

    @block.tensor
    def _(pe):
        MM = nc.tensor.matmul

        def project(S, N, w, slot, xs, k_ready=None, first=True, last=True, between=None):
            xhi, xlo = xs
            pe.wait_ge(w_split, S + 1)
            if first and N is not None:
                pe.wait_ge(evac_done, N)
            for k in range(KT):
                if k_ready is not None:
                    pe.wait_ge(k_ready[0], k_ready[1] + k + 1)
                for n, (wt, x) in enumerate(((w_hi, xhi), (w_hi, xlo), (w_lo, xhi))):
                    for h in range(2):
                        ins = MM(pt[:, slot, h * HALF:(h + 1) * HALF], wt[:, w, k * P:(k + 1) * P],
                                 x[:, k, h * HALF:(h + 1) * HALF], start=first and k == 0 and n == 0,
                                 stop=last and k == KT - 1 and n == 2)
                if k == KT - 1:
                    ins.then_inc(mm_done, 1)
                if between is not None:
                    between(k)

        def pair(j, S, N, xs, k_ready=None):
            for u in range(2):
                project(j * 2 + (S + u), j * 2 + (N + u - 1), u, u, xs, k_ready)

        def project_half(w, slot, xs, h, first=True, last=True, between=None):
            for k in range(KT):
                for n, (wt, x) in enumerate(((w_hi, xs[0]), (w_hi, xs[1]), (w_lo, xs[0]))):
                    ins = MM(pt[:, slot, cols(h)], wt[:, w, k * P:(k + 1) * P], x[:, k, cols(h)],
                             start=first and k == 0 and n == 0, stop=last and k == KT - 1 and n == 2)
                if between is not None and k < KT - 1:
                    between(k)
            return ins

        def pair_by_half(S, N, xs, half_base, base, between):
            pe.wait_ge(evac_done, N)
            for h in range(2):
                for k in range(KT):
                    pe.wait_ge((half_lo, lo_done)[h], (half_base, base)[h] + k + 1)
                    for u in range(2):
                        pe.wait_ge(w_split, S + 1 + u)
                        for n, (wt, x) in enumerate(((w_hi, xs[0]), (w_hi, xs[1]), (w_lo, xs[0]))):
                            ins = MM(pt[:, u, cols(h)], wt[:, u, k * P:(k + 1) * P], x[:, k, cols(h)],
                                     start=k == 0 and n == 0, stop=k == KT - 1 and n == 2)
                        if h == 1 and k == KT - 1:
                            ins.then_inc(mm_done, 1)
                    if h == 0:
                        between(k)

        def pair_by_k(S, N, xs, k_ready):
            pe.wait_ge(w_split, S + 2)
            pe.wait_ge(evac_done, N)
            for k in range(KT):
                pe.wait_ge(k_ready[0], k_ready[1] + k + 1)
                for u in range(2):
                    for n, (wt, x) in enumerate(((w_hi, xs[0]), (w_hi, xs[1]), (w_lo, xs[0]))):
                        for h in range(2):
                            ins = MM(pt[:, u, h * HALF:(h + 1) * HALF], wt[:, u, k * P:(k + 1) * P],
                                     x[:, k, h * HALF:(h + 1) * HALF], start=k == 0 and n == 0, stop=k == KT - 1 and n == 2)
                    if k == KT - 1:
                        ins.then_inc(mm_done, 1)

        def sums(acc, col):
            for c in range(C):
                ins = MM(wk[:, 3, col + c:col + c + 1], acc[:, c * P:(c + 1) * P], ones[:, 0:1], start=True, stop=True)
            return ins

        def half_sums(acc, col, h):
            for c in range(4 * h, 4 * h + 4):
                ins = MM(wk[:, 3, col + c:col + c + 1], acc[:, c * P:(c + 1) * P], ones[:, 0:1], start=True, stop=True)
            return ins

        def half_spread(dst, col, h):
            for c in range(4 * h, 4 * h + 4):
                ins = MM(dst[:, c * P:(c + 1) * P], sm[:, col + c:col + c + 1].to_broadcast([P, P]), ident[:], start=True, stop=True)
            return ins

        def spread(dst, col):
            for c in range(C):
                ins = MM(dst[:, c * P:(c + 1) * P], sm[:, col + c:col + c + 1].to_broadcast([P, P]), ident[:], start=True, stop=True)
            return ins

        pe.wait_ge(cst, 1)
        pe.wait_ge(p_lo_done, 2)
        for n in range(KT):
            w, nt = n // 4, n % 4
            pe.wait_ge(w_split, S_PLE + w + 1)
            if n >= 2:
                pe.wait_ge(evac_done, n - 1)
            for k in range(2):
                for m, (wt, x) in enumerate(((w_hi, p_hi), (w_hi, p_lo), (w_lo, p_hi))):
                    for h in range(2):
                        lhs = wt[:, w, (nt * 2 + k) * P:(nt * 2 + k + 1) * P]
                        ins = MM(pt[:, n % 2, h * HALF:(h + 1) * HALF], lhs, x[:, k, h * HALF:(h + 1) * HALF],
                                 start=k == 0 and m == 0, stop=k == 1 and m == 2)
            ins.then_inc(ple_done, 1)
            if nt == 3:
                pe.wait_ge(ple_done, n + 1)
                pe.sem_inc(mm_done, 1)
        pe.wait_ge(sq_used, KT)
        sums(acc_a, 0).then_inc(stat_done, 1)
        pe.wait_ge(rstd_done, 1)
        spread(wka, 0).then_inc(spread_done, 1)
        pair_by_k(S_XBC, N_XBC, (xh, xl), (lo_done, 0))
        pe.wait_ge(wdt_done, 2)
        for h in range(2):
            for k in range(KT):
                for n, (wt, x) in enumerate(((wdt_hi, xh), (wdt_hi, xl), (wdt_lo, xh))):
                    ins = MM(wk[0:HEADS, h, :], wt[:, k, :], x[:, k, h * HALF:(h + 1) * HALF],
                             start=k == 0 and n == 0, stop=k == KT - 1 and n == 2)
        ins.then_inc(dt_mm, 1)
        pair(1, S_XBC, N_XBC, (xh, xl))
        pe.wait_ge(dt_sb, 1)
        for c in range(C):
            ins = nc.tensor.transpose(wk[:, 3, c * HEADS:(c + 1) * HEADS], dtf[0:HEADS, c * P:(c + 1) * P], ident[0:HEADS, 0:HEADS])
        ins.then_inc(dt_mm, 1)
        with pe.Fori(2, XBC_T // 2 - 1) as j:
            pair(j, S_XBC, N_XBC, (xh, xl))
        pe.wait_ge(adt_done, 1)
        flat = adt[:].rearrange("p c h -> p (c h)")
        MM(wk[:, 3, 0:P], tri[:], flat, start=True, stop=True)
        MM(wk[:, 3, P:2 * P], ones[:, 0:1].to_broadcast([P, P]), flat, start=True, stop=True)
        MM(wk[:, 3, 2 * P:3 * P], flat, tri[:], start=True, stop=True).then_inc(acs_mm, 1)
        pair(XBC_T // 2 - 1, S_XBC, N_XBC, (xh, xl))
        pe.wait_ge(dec_done, 3)
        pe.wait_ge(dec_arg, 1)
        with pe.Fori(0, C) as j:
            S, N = j * 4 + S_SC, j * 4 + N_SC
            project(S, N - 1, 0, 0, (xh, xl))
            pe.wait_ge(stage_done, j + 1)
            pe.wait_ge(s_ready, j)
            pe.wait_ge(y_evac, j)
            for i in range(KT):
                nc.tensor.transpose(wka[:, i * P:(i + 1) * P], st[:, i, :], ident[:])
            nc.tensor.transpose(wk[:, 2, 0:P], st[:, KT, :], ident[:])
            for g in range(GROUPS):
                r = slice(g * 64, g * 64 + 64)
                ins = MM(wk[:, 2, P:2 * P] if g == 0 else wk[:, 3, 0:P], st[r, KT, :], st[r, KT + 1, :], start=True, stop=True)
            ins.then_inc(ssd_a, 1)
            project(S + 1, N, 1, 1, (xh, xl))
            pe.wait_ge(m_ready, j + 1)
            pe.wait_ge(xdd_done, j + 1)
            pe.wait_ge(ce_done, j + 1)
            pe.wait_ge(s_ready, j)
            pe.wait_ge(bt_done, j + 1)
            for h in range(HEADS):
                o = wka[(h % 2) * 64:(h % 2) * 64 + 64, (h // 2) * P:(h // 2 + 1) * P]
                MM(o, xd[:, h, :], rowb[:, h, :], start=True, stop=False)
                MM(o, state[:, h, :], ce[:, h % HG, :], start=False, stop=True)
            for g in range(GROUPS):
                ins = MM(wk[g * 64:g * 64 + 64, 3, :], bt[:, g * 64:g * 64 + 64],
                         xdd[:, g * HG:(g + 1) * HG, :].rearrange("p h q -> p (h q)"), start=True, stop=True)
            ins.then_inc(ssd_b, 1)
            project(S + 2, N + 1, 0, 0, (xh, xl))
            project(S + 3, N + 2, 1, 1, (xh, xl))

        pair(0, S_SB, N_SB, (xh, xl))
        pair(1, S_SB, N_SB, (xh, xl))
        pe.wait_ge(sq_used, 2 * KT)
        pe.wait_ge(s_ready, C)
        pe.wait_ge(y_evac, C)
        sums(acc_g[:, 0, :], 0)
        sums(acc_g[:, 1, :], 8).then_inc(stat_done, 1)
        pair(2, S_SB, N_SB, (xh, xl))
        pe.wait_ge(rstd_done, 2)
        spread(wka, 0)
        spread(wkb, 8).then_inc(spread_done, 1)
        pair(3, S_SB, N_SB, (xh, xl))
        def mixer(j, u):
            project(j * 4 + (S_OUT + 2 * u), j * 2 + (N_OUT + u - 1), 0, u, (sh, sl), (lo_done, KT), last=False)
            project(j * 4 + (S_OUT + 2 * u + 1), None, 1, u, (yh, yl), (lo_done, 2 * KT), first=False)

        with pe.Fori(0, KT // 2 - 1) as j:
            for u in range(2):
                mixer(j, u)
        mixer(KT // 2 - 1, 0)

        def mixer_sums(h, ready):
            pe.wait_ge(*ready)
            half_sums(acc_a, 0, h).then_inc(stat_done, 1)

        def mixer_spread(h):
            pe.wait_ge(rstd_done, 3 + h)
            half_spread(wka, 0, h).then_inc(spread_done, 1)

        pe.wait_ge(w_split, S_OUT + 2 * KT - 1)
        pe.wait_ge(evac_done, N_OUT + KT - 2)
        project_half(0, 1, (sh, sl), 0, last=False)
        pe.wait_ge(w_split, S_OUT + 2 * KT)
        project_half(1, 1, (yh, yl), 0, first=False).then_inc(half_mm, 1)
        project_half(0, 1, (sh, sl), 1, last=False,
                     between=lambda k: mixer_sums(0, (half_acc, 1)) if k == 6 else None).then_inc(mm_done, 1)
        project_half(1, 1, (yh, yl), 1, first=False, between=lambda k: mixer_spread(0) if k == 6 else None).then_inc(mm_done, 1)

        def in_gate(k):
            if k == 1:
                mixer_sums(1, (sq_used, 3 * KT))
            if k == 4:
                mixer_spread(1)

        pair_by_half(S_GATE, N_GATE, (xh, xl), 0, 3 * KT, in_gate)
        with pe.Fori(1, KT // 2) as j:
            pair(j, S_GATE, N_GATE, (xh, xl))
        x2 = (h2, l2)
        def turn(u, used):
            pe.wait_ge(tr_used, used)
            for c in range(C):
                ins = nc.tensor.transpose(wka[:, c * P:(c + 1) * P], ebuf[:, u, c * P:(c + 1) * P], ident[:])
            ins.then_inc(tr_done, 1)

        def turned(S, N, base):
            project(S, N - 1, 0, 0, x2, (lo_done, 4 * KT))
            with pe.Fori(0, KT // 2 - 1) as j:
                project(j * 2 + (S + 1), j * 2 + N, 1, 1, x2)
                pe.wait_ge(evac_done, j * 2 + (N + 1))
                turn(0, j * 2 + base)
                project(j * 2 + (S + 2), j * 2 + (N + 1), 0, 0, x2)
                pe.wait_ge(evac_done, j * 2 + (N + 2))
                turn(1, j * 2 + (base + 1))
            project(S + 7, N + 6, 1, 1, x2)
            pe.wait_ge(evac_done, N + 7)
            turn(0, base + 6)
            pe.wait_ge(evac_done, N + 8)
            turn(1, base + 7)

        turned(S_AV, N_AV, 0)
        pe.wait_ge(ws_done, 1)
        pe.wait_ge(tr_used, KT)
        for h in range(2):
            ins = MM(wk[:, h, :], ones[:, 0:1].to_broadcast([P, P]),
                     wst[:, 4 * h:4 * h + 4, :].rearrange("p g t -> p (g t)"), start=True, stop=True)
        ins.then_inc(row_mm, 1)
        pe.wait_ge(wl_done, 3)
        for h in range(2):
            for k in range(KT):
                for n, (wt, x) in enumerate(((wl_hi, h2), (wl_hi, l2), (wl_lo, h2))):
                    ins = MM(wk[0:RANK, 2 + h, :], wt[:, k, :], x[:, k, h * HALF:(h + 1) * HALF],
                             start=k == 0 and n == 0, stop=k == KT - 1 and n == 2)
        ins.then_inc(low_mm, 1)
        pe.wait_ge(rg_done, 1)
        with pe.Fori(0, KT // 2) as j:
            for u in range(2):
                i = j * 2 + u
                pe.wait_ge(alc_done, i + 1)
                pe.wait_ge(z_dve, i)
                MM(wk[:, 0, :], alc[0:RANK + 1, u, :], wg2[0:RANK + 1, :], start=True, stop=True).then_inc(z_mm, 1)
                project(j * 2 + (S_QK + u), j * 2 + (N_QK + u - 1), u, u, x2)
                pe.wait_ge(z_dve, i + 1)
                pe.wait_ge(cu_done, i)
                for h in range(GH):
                    ins = MM(wk[:, 1, h * P:(h + 1) * P], gm_[:, h * P:(h + 1) * P], tri[:], start=True, stop=True)
                ins.then_inc(cu_mm, 1)
        pe.wait_ge(cu_done, C)

        def mix_tokens(g):
            pe.wait_ge(av_done, C)
            if g:
                pe.wait_ge(mix_done, g)
            for c in range(C):
                ins = MM(wkb[:, c * P:(c + 1) * P], av[:, c, g * P:(g + 1) * P], wst[:, g, :], start=True, stop=True)
            ins.then_inc(mix_mm, 1)

        for i in range(KT):
            project(S_VAL + i, N_VAL + i - 1, i % 2, i % 2, x2)
            if i:
                pe.wait_ge(evac_done, N_VAL + i)
                turn((i - 1) % 2, KT + i - 1)
                mix_tokens(i - 1)
        mix_tokens(KT - 1)
        pe.wait_ge(evac_done, N_VAL + KT)
        turn(1, 2 * KT - 1)
        pe.wait_ge(tr_used, 2 * KT)
        pe.wait_ge(mix_done, KT)
        pe.wait_ge(gst_done, 1)
        with pe.Fori(0, C // 2) as j:
            for u in range(2):
                i = j * 2 + u
                S, N = j * 6 + (S_G + 3 * u), j * 6 + (N_G + 3 * u)
                slots = [(u + n) % 2 for n in range(3)]

                def level(n):
                    pe.wait_ge(lev_ready, i * 7 + n + 1)
                    if n >= 2:
                        pe.wait_ge(lev_used, i * 7 + n - 1)
                    for h in range(GH):
                        ins = MM(wk[:, n % 2, h * 64:(h + 1) * 64], kp[:, n % 2, h, :], qc[:, n % 2, h, :], start=True, stop=True)
                    ins.then_inc(lev_mm, 1)

                def in_ga(k):
                    if k == 0:
                        pe.wait_ge(ch_in, i * 32 + 32)
                        pe.wait_ge(gst_done, i + 1)
                        for h in range(GH):
                            ins = MM(wk[:, 2, h * P:(h + 1) * P], qkc[:, 1, h, :], qkc[:, 0, h, :], start=True, stop=True)
                        ins.then_inc(dg_mm, 1)
                    if k == 1:
                        pe.wait_ge(on_done, i)
                    if k in (3, 5, 7):
                        level((k - 3) // 2)

                def in_r(k):
                    if k in (1, 3, 5, 7):
                        level(3 + (k - 1) // 2)
                    if k == 6:
                        pe.wait_ge(kd_done, i + 1)
                        for h in range(GH):
                            ins = nc.tensor.transpose(wk[:, 3, h * P:(h + 1) * P], kd[:, h, :], ident[:])
                        ins.then_inc(kdt_mm, 1)

                def in_gb(k):
                    if k == 1:
                        pe.wait_ge(lev_used, i * 7 + 7)
                        pe.wait_ge(sc_done, i + 1)
                        pe.wait_ge(vc_in, i * 16 + 16)
                        for v in range(8):
                            h = v // 2
                            o = wka[:, v * P:(v + 1) * P]
                            MM(o, vc[:, v * P:(v + 1) * P], sc[:, h, :], start=True, stop=False)
                            ins = MM(o, gst[:, h, (v % 2) * P:(v % 2 + 1) * P], qe[:, h, :], start=False, stop=True)
                        ins.then_inc(o_mm, 1)
                        pe.wait_ge(kdt_done, i + 1)
                        for h in range(GH):
                            ins = MM(wk[:, 2 + h // 2, (h % 2) * GV:(h % 2 + 1) * GV], kdt[:, h, :], vc[:, h * GV:(h + 1) * GV],
                                     start=True, stop=True)
                        ins.then_inc(su_mm, 1)
                    if k == 4:
                        pe.wait_ge(o_act, i + 1)
                        for h in range(GH):
                            for w in range(2):
                                ins = MM(wk[:, 0, h:h + 1], osq[:, 2 * h + w, :], ones[:, 0:1], start=w == 0, stop=w == 1)
                        ins.then_inc(o_stat, 1)
                    if k == 7:
                        pe.wait_ge(o_rstd, i + 1)
                        for h in range(GH):
                            ins = MM(wk[:, 1, h * P:(h + 1) * P], sm[:, h:h + 1].to_broadcast([P, P]), ident[:], start=True, stop=True)
                        ins.then_inc(o_spread, 1)

                project(S, N - 1, u, slots[0], x2, between=in_ga)
                project(S + 1, N, 1 - u, slots[1], x2, between=in_r)
                project(S + 2, N + 1, u, slots[2], x2, between=in_gb)
        with pe.Fori(0, KT // 2) as j:
            pair(j, S_U, N_U, x2)
        def ln_sums(h, ready):
            pe.wait_ge(*ready)
            half_sums(acc_a, 0, h)
            half_sums(acc_b, 8, h).then_inc(stat_done, 1)

        def ln_spread(h, n):
            pe.wait_ge(rstd_done, n)
            half_spread(wka, 0, h)
            half_spread(wkb, 8, h).then_inc(spread_done, 1)

        def last_pair(S, N, xs, halves, n, k_ready=None):
            pe.wait_ge(w_split, S + 1)
            pe.wait_ge(evac_done, N - 1)
            if k_ready is not None:
                pe.wait_ge(*k_ready)
            project_half(0, 0, xs, 0).then_inc(half_mm, 1)
            pe.wait_ge(w_split, S + 2)
            pe.wait_ge(evac_done, N)
            project_half(1, 1, xs, 0).then_inc(half_mm, 1)
            project_half(0, 0, xs, 1, between=lambda k: ln_sums(0, (half_acc, halves)) if k == 6 else None).then_inc(mm_done, 1)
            project_half(1, 1, xs, 1, between=lambda k: ln_spread(0, n) if k == 6 else None).then_inc(mm_done, 1)

        with pe.Fori(0, KT // 2 - 1) as j:
            pair(j, S_OUT2, N_OUT2, (mh, ml), (lo_done, 5 * KT))
        last_pair(S_OUT2 + KT - 2, N_OUT2 + KT - 2, (mh, ml), 3, 6)

        def in_ff(k):
            if k == 0:
                ln_sums(1, (a_used, KT))
            if k == 3:
                ln_spread(1, 7)

        def ff2(b, pairs):
            with pe.Fori(0, pairs) as j:
                for u in range(2):
                    project(b * 16 + j * 2 + (S_FF + 8 + u), b * 16 + j * 2 + (N_FF + 8 + u - 1), u, u, (fh, fl),
                            (f_lo, b * KT))

        def ff1(b, first=0):
            with pe.Fori(first, KT // 2) as j:
                for u in range(2):
                    project(b * 16 + j * 2 + (S_FF + u), b * 16 + j * 2 + (N_FF + u - 1), u, u, x2)

        pair_by_half(S_FF, N_FF, x2, KT, 6 * KT, in_ff)
        ff1(0, 1)
        ff2(0, KT // 2)
        with pe.Fori(1, FF_BLOCKS - 1) as b:
            ff1(b)
            ff2(b, KT // 2)
        ff1(FF_BLOCKS - 1)
        ff2(FF_BLOCKS - 1, KT // 2 - 1)
        last_pair(S_ALL - 2, N_FF + 16 * FF_BLOCKS - 2, (fh, fl), 5, 8)
        ln_sums(1, (a_used, KT + FF_BLOCKS * KT))
        ln_spread(1, 9)
    ctx.close()


def kernel(**inputs):
    import numpy as _np
    import concourse.bacc as _bacc
    from concourse import mybir as _mybir
    from concourse.bass_utils import run_bass_kernel_spmd as _run

    a = {k: _np.asarray(v) for k, v in inputs.items()}
    w_in, w_in2 = a["w_in"][0], a["w_in_2"][0]

    def tiles(w):
        k, n = w.shape
        return w.reshape(k // 1024, 8, P, n // P, P).transpose(3, 0, 2, 1, 4).reshape(-1, P, 1024)

    def mixed(*ws):
        t = [tiles(w) for w in ws]
        return _np.stack(t, 1).reshape(-1, P, 1024)

    o = XBC_T * P + HEADS
    z, sc_h, sc_b, sc_c, z_sc = (w_in[:, o + i * D:o + (i + 1) * D] for i in range(5))
    u_, v_, qk_, val_, r_ = (w_in2[:, i * D:(i + 1) * D] for i in range(5))
    o2 = 5 * D + RANK
    g_a, g_b = w_in2[:, o2:o2 + D], w_in2[:, o2 + D:o2 + 2 * D]
    w_out = a["w_out"][0]
    w_ple = a["w_ple_proj"][0].reshape(2, P, 2, 4, P).transpose(2, 1, 3, 0, 4).reshape(2, P, 1024)
    ff1 = tiles(a["w_ff1_2"][0]).reshape(FF_BLOCKS, 8, P, 1024)
    ff2 = tiles(a["w_ff2_2"][0]).reshape(8, FF_BLOCKS, P, 1024).transpose(1, 0, 2, 3)
    stream = _np.concatenate([
        w_ple, tiles(w_in[:, 0:XBC_T * P]), mixed(z, sc_c, sc_h, z_sc), tiles(sc_b),
        mixed(w_out[D:], w_out[:D]), tiles(a["w_ple_gate"][0]), tiles(v_), tiles(qk_), tiles(val_),
        mixed(g_a, r_, g_b), tiles(u_), tiles(a["w_out_2"][0]),
        _np.concatenate([ff1, ff2], 1).reshape(-1, P, 1024)])
    b_in = a["b_in_2"][0]
    cols = {"norm_pre": a["norm_pre"], "norm_post": a["norm_post"], "conv_w": a["ssd_conv_w"][0], "conv_b": a["ssd_conv_b"],
            "d_skip": _np.repeat(a["d_skip"][0], HP), "ssd_norm": a["ssd_norm"], "sc_w": a["sc_conv_w"][0],
            "b_u": b_in[0:D], "b_v": b_in[D:2 * D], "b_qk": b_in[2 * D:3 * D], "b_val": b_in[3 * D:4 * D],
            "b_r": b_in[4 * D:5 * D], "b_ga": b_in[o2:o2 + D], "b_gb": b_in[o2 + D:o2 + 2 * D],
            "sg_g": a["sg_ln_g_2"], "sg_b": a["sg_ln_b_2"], "gn": a["gla_norm_g_2"], "ln1_g": a["ln1_g_2"],
            "ln1_b": a["ln1_b_2"], "ln2_g": a["ln2_g_2"], "ln2_b": a["ln2_b_2"]}
    vecs = _np.concatenate([cols[n].reshape(-1, P).T for n, _ in VCOLS], 1)
    arrays = {
        "xT": a["x"][0].T, "pT": a["p"][0, 0].T, "ws": stream, "w_dt": w_in[:, XBC_T * P:o],
        "w_low": w_in2[:, 5 * D:o2], "vecs": vecs, "dt_bias": a["dt_bias"], "a_log": a["a_log"],
        "b_low": b_in[5 * D:o2].reshape(RANK, 1), "w_gate2": a["gla_w_gate2_2"][0], "b_gate": a["gla_b_gate_2"],
        "sg_w": a["sg_w_s_2"][0].transpose(2, 0, 1), "sg_bs": a["sg_b_s_2"].reshape(1, D)}
    nc = _bacc.Bacc("TRN2", target_bir_lowering=False, num_devices=1)
    ins, args = {}, []
    for name, x in arrays.items():
        ins[name + "_d"] = _np.ascontiguousarray(x)
        args.append(nc.dram_tensor(name + "_d", x.shape, _mybir.dt.float32, kind="ExternalInput").ap())
    args.append(nc.dram_tensor("outT_d", (D, T), _mybir.dt.float32, kind="ExternalOutput").ap())
    two_blocks_kernel(nc, *args)
    r = _run(nc, [ins], core_ids=[0])
    return _np.ascontiguousarray(r.results[0]["outT_d"].T).reshape(1, T, D)
```

```python
import math
from contextlib import ExitStack

import numpy as np

import concourse.bass as bass
from concourse import mybir

P = 128
T = 1024
D = 1024
KT = D // P
C = T // P
HALF = 512
QUARTER = T // 4
HEADS, HP, GROUPS, NS = 16, 64, 2, 64
HG = HEADS // GROUPS
XBC_T = (D + 2 * GROUPS * NS) // P
CW, SW = 4, 3
GH, GK, GV = 4, 128, 256
RANK = 16
FF_BLOCKS = 4
EPS1, EPS2 = 1e-6, 1e-5
ALPHA = 2.0 ** 0.25
Q_SCALE = GK ** -0.5
TEMP = 16.0
LEVELS = [64, 32, 16, 8, 4, 2, 1]

VCOLS = [("norm_pre", 8), ("norm_post", 8), ("conv_w", CW * XBC_T), ("conv_b", XBC_T), ("d_skip", 8),
         ("ssd_norm", 8), ("sc_w", SW * 8), ("b_u", 8), ("b_v", 8), ("b_qk", 8), ("b_val", 8), ("b_r", 8),
         ("b_ga", 8), ("b_gb", 8), ("sg_g", 8), ("sg_b", 8), ("gn", 8), ("ln1_g", 8), ("ln1_b", 8),
         ("ln2_g", 8), ("ln2_b", 8)]
VOFF, _n = {}, 0
for _name, _w in VCOLS:
    VOFF[_name] = _n
    _n += _w
NV = _n
HOFF = {}
for _name in ("half_ga", "half_r", "half_gb", "half_gn", "half_rgn", "qk_s", "qk_b"):
    HOFF[_name] = _n
    _n += 8
NVH = _n

S_PLE, N_PLE = 0, 0
S_XBC, N_XBC = 2, 8
S_SC, N_SC = 12, 18
S_SB, N_SB = 44, 50
S_OUT, N_OUT = 52, 58
S_GATE, N_GATE = 68, 66
S_AV, N_AV = 76, 74
S_QK, N_QK = 84, 82
S_VAL, N_VAL = 92, 90
S_G, N_G = 100, 98
S_U, N_U = 124, 122
S_OUT2, N_OUT2 = 132, 130
S_FF, N_FF = 140, 138
S_ALL = S_FF + FF_BLOCKS * 16


class Chain:

    def __init__(self, eng, sem):
        self.eng, self.sem, self.base, self.n = eng, sem, 0, 0

    def __call__(self, ins):
        self.n += 1
        ins.then_inc(self.sem, 1)
        self.eng.wait_ge(self.sem, self.base + self.n)

    def enter(self, i, per):
        self.start, self.per = self.base + self.n, per
        self.base, self.n = self.start + i * per, 0

    def leave(self, times):
        assert self.n == self.per, (self.n, self.per)
        self.base, self.n = self.start + times * self.per, 0


def two_blocks_kernel(nc, xT, pT, ws, w_dt, w_low, vecs, dt_bias, a_log, b_low, w_gate2, b_gate,
                      sg_w, sg_bs, outT):
    f32, f32r = mybir.dt.float32, mybir.dt.float32r
    u32, i32 = mybir.dt.uint32, mybir.dt.int32
    ALU, ACT = mybir.AluOpType, mybir.ActivationFunctionType
    ds = bass.ds
    ctx = ExitStack()

    BASE = 16512
    W0 = BASE
    A0, A1 = W0 + 24576, W0 + 24576 + 32768
    R2 = A1 + 32768
    R3 = R2 + 32768
    R1 = R3 + 32768
    BC = R1 + 32768
    EAo, EBo, ECo = BC + 8192, BC + 12288, BC + 16384
    K0 = ECo + 4128
    assert K0 + 3904 <= 229344

    def at(name, shape, off, dt=f32):
        return nc.alloc_sbuf_tensor_at(name, [P] + shape, dt, offset=off)

    w_raw = at("w_raw", [2, 1024], W0)
    w_hi = at("w_hi", [2, 1024], W0 + 8192, f32r)
    w_lo = at("w_lo", [2, 1024], W0 + 16384, f32r)
    ea, eb, ec = at("ea", [1024], EAo), at("eb", [1024], EBo), at("ec", [1024], ECo)
    ebuf = at("ebuf", [2, 1024], EAo)
    tri = at("tri", [P], K0)
    ident = at("ident", [P], K0 + 512)
    vec = at("vec", [NVH], K0 + 1024)
    sm = at("sm", [64], K0 + 2240)
    ones = at("ones", [2], K0 + 2496)
    dec = at("dec", [P], K0 + 2560)
    assert 1024 + NVH * 4 <= 2240
    xh, xl = at("xh", [KT, T], A0, f32r), at("xl", [KT, T], A1, f32r)
    x_raw = at("x_raw", [KT, T], R1)
    p_raw, p_hi, p_lo = at("p_raw", [2, T], R2), at("p_hi", [2, T], R3, f32r), at("p_lo", [2, T], R3 + 8192, f32r)
    acc_a, acc_b = at("acc_a", [1024], BC), at("acc_b", [1024], BC + 4096)
    acc_g = at("acc_g", [2, 1024], R3 + 24576)
    raw_p = at("raw_p", [2, T + CW], R2 + 8192)
    conv_o = at("conv_o", [2, T], R2 + 16448)
    wdt_raw = at("wdt_raw", [KT, HEADS], R2 + 24640)
    dtb, alr = at("dtb", [HEADS], R2 + 26176), at("alr", [HEADS], R2 + 26240)
    tmps = [at(f"tmp{i}", [P], R2 + 26304 + 512 * i) for i in range(8)]
    adt = at("adt", [C, HEADS], R2 + 30400)
    dtf = at("dtf", [T], R2)
    acs_row = at("acs_row", [P], R2 + 30912)
    xbc = at("xbc", [XBC_T, T], R1)
    rowb = at("rowb", [HEADS, P], R3)
    st = at("st", [XBC_T, P], R3 + 8192)
    xd = at("xd", [HEADS, HP], R3 + 13312)
    xdd = at("xdd", [HEADS, HP], R3 + 17408)
    ce = at("ce", [HG, P], R3 + 21504)
    bt = at("bt", [P], R3 + 25600)
    cbm = at("cbm", [GROUPS, P], R3 + 26112)
    state = at("state", [HEADS, HP], R3 + 27136)
    dtt = at("dtt", [C, HEADS], R3 + 31232)
    acs = at("acs", [C, HEADS], R3 + 31744)
    et2 = at("et2", [C, HG], K0 + 3072)
    vbuf = at("vbuf", [KT, T], R2)
    ecp = at("ecp", [T + SW - 1], ECo)
    sh, sl = at("sh", [KT, T], R3, f32r), at("sl", [KT, T], R2, f32r)
    yh, yl = xh, at("yl", [KT, T], R1, f32r)
    mm = at("mm", [KT, T], A1)
    xres = x_raw
    h2, l2 = at("h2", [KT, T], R2, f32r), at("l2", [KT, T], R3, f32r)
    av = at("av", [C, D], A0)
    mix = at("mix", [KT, T], A1)
    wl_raw = at("wl_raw", [KT, RANK], R1)
    blow = at("blow", [1], R1 + 1536)
    wg2 = at("wg2", [GH * GK], R1 + 2048)
    alow = at("alow", [T], R1 + 4096)
    alc = at("alc", [2, P], R1 + 8192)
    wst = at("wst", [KT, P], R1 + 9216)
    rg = at("rg", [KT, P], R1 + 13312)
    ga_, ge_, gl_, gm_ = (at(f"gz{i}", [512], R1 + 17408 + 2048 * i) for i in range(4))
    cu_o = at("cu_o", [512], R1 + 25600)
    bnst, bnag = at("bnst", [2 * C, 6], R1 + 27648), at("bnag", [C, 2], R1 + 28160)
    vb = at("vb", [2, C, P], BC)
    G = A0
    qkc = at("qkc", [3, GH, P], G)
    vc = at("vc", [D], G + 6144)
    darg = at("darg", [2, 2, 256], G + 10240)
    kp = at("kp", [2, GH, P], G + 14336)
    qc = at("qc", [2, GH, 64], G + 18432)
    sc = at("sc", [GH, P], G + 20480)
    kd = at("kd", [GH, P], G + 22528)
    qe = at("qe", [GH, P], G + 24576)
    kdt = at("kdt", [GH, P], G + 26624)
    gst = at("gst", [GH, GV], G + 28672)
    oc = at("oc", [8, P], BC)
    osq = at("osq", [8, P], BC + 4096)
    lmask_f = at("lmask_f", [7, 64], R3 + 16384)
    lmask = at("lmask", [7, 64], K0 + 3328, mybir.dt.uint8)
    etot = at("etot", [GH], K0 + 2528)
    gbuf = at("gbuf", [KT, T], R1)
    mh, ml = at("mh", [KT, T], A0, f32r), at("ml", [KT, T], A1, f32r)
    yr = at("yr", [KT, T], R1)
    fh, fl = at("fh", [KT, T], A0, f32r), at("fl", [KT, T], A1, f32r)

    pt = ctx.enter_context(nc.psum_tensor("pt", [P, 2, 1024], f32))
    wk = ctx.enter_context(nc.psum_tensor("wk", [P, 4, HALF], f32))
    wka = wk[:, 0:2, :].rearrange("p b n -> p (b n)")
    wkb = wk[:, 2:4, :].rearrange("p b n -> p (b n)")

    nrm, nrm2 = at("nrm", [2, HALF], ECo), at("nrm2", [2, HALF], R2)

    pp_d = nc.dram_tensor("pp_d", [KT, P, T], f32, kind="Internal").ap()
    sz_d = nc.dram_tensor("sz_d", [KT, P, T], f32, kind="Internal").ap()
    acs_d = nc.dram_tensor("acs_d", [C, HEADS * P], f32, kind="Internal").ap()
    qk_d = nc.dram_tensor("qk_d", [KT, P, T], f32, kind="Internal").ap()
    cu_d = nc.dram_tensor("cu_d", [C, P, GH * P], f32, kind="Internal").ap()
    v_d = nc.dram_tensor("v_d", [C, P, D], f32, kind="Internal").ap()
    o_d = nc.dram_tensor("o_d", [KT, P, T], f32, kind="Internal").ap()

    def tile_of(dram, i):
        return dram[ds(i, 1), :, :].rearrange("a p n -> (a p) n")

    def row(t, i):
        return t[:, ds(i, 1), :].rearrange("p a t -> p (a t)")

    def cols(h):
        return slice(h * HALF, (h + 1) * HALF)

    def sem(name):
        return ctx.enter_context(nc.semaphore(name))

    def V(name, i=0, n=1):
        off = VOFF[name] if name in VOFF else HOFF[name]
        return vec[:, ds(off + i, n)]

    w_loaded = [sem("w_loaded0"), sem("w_loaded1")]
    w_hi_done, w_split = sem("w_hi_done"), sem("w_split")
    mm_done = sem("mm_done")
    ple_done = sem("ple_done")
    evac_done = sem("evac_done")
    cst = sem("cst")
    x_in = [[sem(f"x_in{h}_{k}") for k in range(KT)] for h in range(2)]
    first_sq, first_acc = sem("first_sq"), sem("first_acc")
    p_in, vec_in, sml_in = sem("p_in"), sem("vec_in"), sem("sml_in")
    p_hi_done, p_lo_done = sem("p_hi_done"), sem("p_lo_done")
    pp_put = [sem("pp_put0"), sem("pp_put1")]
    sq_done, sq_used = sem("sq_done"), sem("sq_used")
    stat_done = sem("stat_done")
    rstd_done = sem("rstd_done")
    spread_done = sem("spread_done")
    val_done = sem("val_done")
    hi_done = sem("hi_done")
    lo_done = sem("lo_done")
    dt_mm, dt_sb, dt_a, dt_b = sem("dt_mm"), sem("dt_sb"), sem("dt_a"), sem("dt_b")
    adt_done, acs_mm, acs_put = sem("adt_done"), sem("acs_mm"), sem("acs_put")
    acs_sb, dec_arg, dec_done = sem("acs_sb"), sem("dec_arg"), sem("dec_done")
    conv_done, silu_done = sem("conv_done"), sem("silu_done")
    stage_done, ssd_a, ssd_b = sem("stage_done"), sem("ssd_a"), sem("ssd_b")
    bt_done, row_in, ce_exp, e_arg, e_exp = sem("bt_done"), sem("row_in"), sem("ce_exp"), sem("e_arg"), sem("e_exp")
    ce_done, xdd_done, m_ready, y_evac, s_ready = sem("ce_done"), sem("xdd_done"), sem("m_ready"), sem("y_evac"), sem("s_ready")
    sz_done, sz_put, u_done, v_done = sem("sz_done"), sem("sz_put"), sem("u_done"), sem("v_done")
    sz_in, yz_done = [sem("sz_in0"), sem("sz_in1")], sem("yz_done")
    ys_done = sem("ys_done")
    pp_in = [sem("pp_in0"), sem("pp_in1")]
    b2_in = sem("b2_in")
    tr_done, tr_used = sem("tr_done"), sem("tr_used")
    low_ones_done = sem("low_ones_done")
    low_mm, low_done = sem("low_mm"), sem("low_done")
    alc_done, z_mm, z_act, z_dve, z_min = sem("alc_done"), sem("z_mm"), sem("z_act"), sem("z_dve"), sem("z_min")
    cu_mm, cu_done, cu_put = sem("cu_mm"), sem("cu_done"), sem("cu_put")
    qk_put = [sem("qk_put0"), sem("qk_put1")]
    v_put = [sem("v_put0"), sem("v_put1")]
    bn_done, av_done = sem("bn_done"), sem("av_done")
    ws_done, row_mm, rg_done, mix_mm, mix_done = sem("ws_done"), sem("row_mm"), sem("rg_done"), sem("mix_mm"), sem("mix_done")
    ch_in, vc_in = sem("ch_in"), sem("vc_in")
    arg_done, lev_exp, lev_ready, lev_mm, lev_used = sem("arg_done"), sem("lev_exp"), sem("lev_ready"), sem("lev_mm"), sem("lev_used")
    dg_mm, sc_done, end_exp, end_arg, kd_done = (sem("dg_mm"), sem("sc_done"), sem("end_exp"), sem("end_arg"),
                                                 sem("kd_done"))
    kdt_mm, kdt_done, o_mm, su_mm, gst_done = sem("kdt_mm"), sem("kdt_done"), sem("o_mm"), sem("su_mm"), sem("gst_done")
    o_sum = sem("o_sum")
    o_act, o_stat, o_rstd, o_spread, on_done, o_put = (sem("o_act"), sem("o_stat"), sem("o_rstd"), sem("o_spread"),
                                                      sem("on_done"), sem("o_put"))
    ga_done, r_done, gb_done = sem("ga_done"), sem("r_done"), sem("gb_done")
    o_in, m_done = sem("o_in"), sem("m_done")
    y_done, a_used = sem("y_done"), sem("a_used")
    ln_done, h_done = sem("ln_done"), sem("h_done")
    f_sq, f_hi, f_lo, f_acc, f_zero = sem("f_sq"), sem("f_hi"), sem("f_lo"), sem("f_acc"), sem("f_zero")
    out_ready, out_put = sem("out_ready"), sem("out_put")
    half_mm, half_ev, half_y, half_sq, half_acc, half_val, half_hi, half_lo = (
        sem("half_mm"), sem("half_ev"), sem("half_y"), sem("half_sq"), sem("half_acc"), sem("half_val"), sem("half_hi"),
        sem("half_lo"))
    d_chain, a_chain, p_chain = sem("d_chain"), sem("a_chain"), sem("p_chain")

    block = ctx.enter_context(nc.Block())

    @block.sync
    def _(sp):
        for u in range(2):
            sp.dma_start(w_raw[:, u, :], ws[u, :, :]).then_inc(w_loaded[u], 16)
        for h in range(2):
            for k in range(KT):
                sp.dma_start(x_raw[:, k, cols(h)], xT[k * P:(k + 1) * P, cols(h)]).then_inc(x_in[h][k], 16)

        def weights(first, end):
            with sp.Fori(first, end) as j:
                for u in range(2):
                    tile = sp.snap(j * 2 + u)
                    sp.wait_ge(w_split, j * 2 + u - 1)
                    sp.dma_start(w_raw[:, u, :], tile_of(ws, tile)).then_inc(w_loaded[u], 16)

        weights(1, S_GATE // 2 + 1)
        for h in range(2):
            sp.wait_ge((half_mm, mm_done)[h], (1, S_OUT + 2 * KT)[h])
            for k in range(KT):
                sp.dma_start(x_raw[:, k, cols(h)], xT[k * P:(k + 1) * P, cols(h)]).then_inc(x_in[h][k], 16)
        weights(S_GATE // 2 + 1, S_ALL // 2)
        for h in range(2):
            for k in range(KT):
                sp.wait_ge(h_done, 2 * KT + h * KT + k + 1)
                sp.dma_start(outT[k * P:(k + 1) * P, cols(h)], yr[:, k, cols(h)]).then_inc(out_put, 16)
        sp.wait_ge(out_put, 2 * KT * 16)

    @block.gpsimd
    def _(pool):
        link = Chain(pool, p_chain)
        link(nc.gpsimd.memset(ones[:, 0:1], 1.0))
        link(nc.gpsimd.memset(ones[:, 1:2], 0.0))
        link(nc.gpsimd.memset(ident[:], 0.0))
        link(nc.gpsimd.memset(tri[:], 1.0))
        link(nc.gpsimd.affine_select(out=ident[:], in_=ident[:], compare_op=ALU.not_equal, fill=1.0, base=0,
                                     pattern=[[-1, P]], channel_multiplier=1))
        nc.gpsimd.affine_select(out=tri[:], in_=tri[:], compare_op=ALU.is_ge, fill=0.0, base=0,
                                pattern=[[1, P]], channel_multiplier=-1).then_inc(cst, 1)

        def split(u, loaded):
            pool.wait_ge(w_loaded[u], loaded)
            zeros = ones[:, 1:2].to_broadcast([P, 1024])
            nc.gpsimd.tensor_tensor(out=w_hi[:, u, :], in0=w_raw[:, u, :], in1=zeros, op=ALU.add).then_inc(w_hi_done, 1)

        def rest(u, n):
            pool.wait_ge(w_hi_done, n)
            nc.gpsimd.tensor_tensor(out=w_lo[:, u, :], in0=w_raw[:, u, :], in1=w_hi[:, u, :].bitcast(f32),
                                    op=ALU.subtract).then_inc(w_split, 1)

        for u in range(2):
            split(u, 16)
            rest(u, u + 1)
        for n, m in enumerate(LEVELS):
            v = lmask_f[:, n, :].rearrange("p (b r) -> p b r", r=m)
            link(nc.gpsimd.memset(lmask_f[:, n, :], 1.0))
            link(nc.gpsimd.affine_select(out=v, in_=v, compare_op=ALU.is_ge, fill=0.0, base=0,
                                         pattern=[[-2 * m, 64 // m], [0, m]], channel_multiplier=1))
            nc.gpsimd.affine_select(out=v, in_=v, compare_op=ALU.is_ge, fill=0.0, base=m - 1,
                                    pattern=[[2 * m, 64 // m], [0, m]], channel_multiplier=-1).then_inc(cst, 1)
        def split_pairs(first, end):
            with pool.Fori(first, end) as j:
                for u in range(2):
                    pool.wait_ge(mm_done, j * 2 + u - 1)
                    split(u, j * 16 + 16)
                    rest(u, j * 2 + u + 1)

        def before_norm(S):
            pool.wait_ge(mm_done, S - 1)
            split(0, 16 * (S // 2 + 1))
            rest(0, S + 1)

        def lows(dst, src, high, half_base, base):
            for h in range(2):
                for k in range(KT):
                    pool.wait_ge((half_hi, hi_done)[h], (half_base, base)[h] + k + 1)
                    nc.gpsimd.tensor_tensor(out=dst[:, k, cols(h)], in0=src[:, k, cols(h)],
                                            in1=high[:, k, cols(h)].bitcast(f32),
                                            op=ALU.subtract).then_inc((half_lo, lo_done)[h], 1)

        split_pairs(1, S_GATE // 2)
        before_norm(S_GATE)
        lows(xl, xres, xh, KT, 3 * KT)
        split_pairs(S_GATE // 2 + 1, S_FF // 2)
        before_norm(S_FF)
        lows(l2, yr, h2, 2 * KT, 6 * KT)
        split_pairs(S_FF // 2 + 1, S_ALL // 2)

    @block.scalar
    def _(act):
        A = nc.scalar.activation
        link = Chain(act, a_chain)
        act.dma_start(p_raw[:], pT.rearrange("(k p) t -> p k t", p=P)).then_inc(p_in, 16)
        act.dma_start(vec[:, 0:NV], vecs).then_inc(vec_in, 16)
        act.dma_start(wdt_raw[:], w_dt.rearrange("(k p) h -> p k h", p=P)).then_inc(sml_in, 16)
        act.dma_start(dtb[:], dt_bias.to_broadcast([P, HEADS])).then_inc(sml_in, 16)
        act.dma_start(alr[:], a_log.to_broadcast([P, HEADS])).then_inc(sml_in, 16)

        act.wait_ge(p_in, 16)
        for k in range(2):
            A(p_hi[:, k, :], p_raw[:, k, :], ACT.Copy).then_inc(p_hi_done, 1)

        def square(q):
            h, k = divmod(q, KT)
            act.wait_ge(x_in[h][k], 16)
            if q in (KT, KT + 1):
                act.wait_ge(first_acc, q - 1)
            elif q >= 2:
                act.wait_ge((first_acc, sq_used)[h], k - 1)
            A(ec[:, cols(q % 2)], x_raw[:, k, cols(h)], ACT.Square).then_inc((first_sq, sq_done)[h], 1)

        def embedding(k):
            act.wait_ge(ple_done, k + 1)
            if k >= 2:
                act.wait_ge(pp_put[k % 2], 16 * (k // 2))
            A(ebuf[:, k % 2, :], pt[:, k % 2, :], ACT.Copy, scale=0.5).then_inc(evac_done, 1)
            act.wait_ge(evac_done, k + 1)
            act.dma_start(pp_d[k, :, :], ebuf[:, k % 2, :]).then_inc(pp_put[k % 2], 16)

        def high(q):
            h, k = divmod(q, KT)
            act.wait_ge((half_val, val_done)[h], k + 1)
            A(xh[:, k, cols(h)], x_raw[:, k, cols(h)], ACT.Copy).then_inc((half_hi, hi_done)[h], 1)

        for step, first, end in ((square, 0, 4), (embedding, 0, 1), (square, 4, 6), (embedding, 1, 2), (square, 6, 8),
                                 (embedding, 2, 3), (square, 8, 10), (embedding, 3, 4), (square, 10, 12),
                                 (embedding, 4, 5), (high, 0, 3), (square, 12, 14), (embedding, 5, 6), (high, 3, 5),
                                 (square, 14, 16), (embedding, 6, 7), (high, 5, 8), (embedding, 7, 8)):
            for q in range(first, end):
                step(q)
        for q in range(KT, 2 * KT):
            high(q)

        def xbc_pair(j):
            for u in range(2):
                act.wait_ge(mm_done, j * 2 + (S_XBC + u + 1))
                act.wait_ge(conv_done, j * 2)
                A(raw_p[:, u, CW - 1:CW - 1 + T], pt[:, u, :], ACT.Copy).then_inc(evac_done, 1)
            for u in range(2):
                act.wait_ge(conv_done, j * 2 + (u + 1))
                A(row(xbc, j * 2 + u), conv_o[:, u, :], ACT.Silu).then_inc(silu_done, 1)

        act.wait_ge(lo_done, KT)
        xbc_pair(0)
        act.wait_ge(dt_mm, 1)
        for q in range(4):
            ins = A(dtf[0:HEADS, q * QUARTER:(q + 1) * QUARTER], wk[32 * q:32 * q + HEADS, 0, 0:QUARTER], ACT.Copy)
        ins.then_inc(dt_sb, 1)
        xbc_pair(1)
        v, r_, e_, u_, l_ = tmps[0], tmps[1], tmps[2], tmps[3], tmps[4]
        act.wait_ge(dt_a, 1)
        link(A(l_[:], v[:], ACT.Abs))
        A(e_[:], l_[:], ACT.Exp, scale=-1.0).then_inc(dt_b, 1)
        A(alr[:], alr[:], ACT.Exp).then_inc(dt_b, 1)
        act.wait_ge(dt_a, 2)
        A(l_[:], u_[:], ACT.Ln).then_inc(dt_b, 1)

        with act.Fori(2, XBC_T // 2 - 1) as j:
            xbc_pair(j)

        act.wait_ge(acs_mm, 1)
        A(acs[:], wk[:, 3, 0:P].rearrange("p (c h) -> p c h", c=C), ACT.Copy).then_inc(acs_sb, 1)
        A(acs_row[:], wk[:, 3, 2 * P:3 * P], ACT.Copy).then_inc(acs_sb, 1)
        act.wait_ge(acs_sb, 2)
        act.dma_start(acs_d.rearrange("c (h l) -> (c h) l", h=HEADS), acs_row[:]).then_inc(acs_put, 16)
        tot = wk[:, 3, P:2 * P].rearrange("p (c h) -> p c h", c=C)
        A(et2[0:64], tot[0:64, :, 0:HG], ACT.Exp).then_inc(dec_done, 1)
        A(et2[64:128], tot[64:128, :, HG:HEADS], ACT.Exp).then_inc(dec_done, 1)
        act.wait_ge(dec_arg, 1)
        A(dec[:], dec[:], ACT.Exp).then_inc(dec_done, 1)
        act.wait_ge(acs_put, 16)
        xbc_pair(XBC_T // 2 - 1)
        act.wait_ge(silu_done, XBC_T)

        act.wait_ge(pp_put[0], 64)
        act.wait_ge(pp_put[1], 64)
        with act.Fori(0, C) as j:
            S, N = S_SC + j * 4, N_SC + j * 4
            row_src = acs_d[ds(j, 1), :].to_broadcast([P, HEADS * P])
            act.wait_ge(ssd_b, j)
            act.dma_start(rowb[:].rearrange("p h l -> p (h l)"), row_src).then_inc(row_in, 16)
            act.wait_ge(y_evac, j)
            A(st[:], xbc[:, :, ds(j * P, P)], ACT.Copy).then_inc(stage_done, 1)
            act.wait_ge(row_in, j * 16 + 16)
            A(ce[0:64], rowb[0:64, 0:HG, :], ACT.Exp).then_inc(ce_exp, 1)
            A(ce[64:128], rowb[64:128, HG:HEADS, :], ACT.Exp).then_inc(ce_exp, 1)
            act.wait_ge(e_arg, j + 1)
            A(rowb[:], rowb[:], ACT.Exp).then_inc(e_exp, 1)
            act.wait_ge(mm_done, S + 1)
            act.wait_ge(v_done, j)
            A(ea[:], pt[:, 0, :], ACT.Copy, scale=0.5)
            A(eb[:], pt[:, 0, :], ACT.Tanh, scale=0.5).then_inc(evac_done, 1)
            act.wait_ge(ssd_a, j + 1)
            A(bt[:], wk[:, 2, 0:P], ACT.Copy).then_inc(bt_done, 1)
            act.wait_ge(mm_done, S + 2)
            act.wait_ge(sz_done, j + 1)
            act.dma_start(tile_of(sz_d, j), eb[:]).then_inc(sz_put, 16)
            A(ea[:], pt[:, 1, :], ACT.Copy).then_inc(evac_done, 1)
            act.wait_ge(mm_done, S + 3)
            act.wait_ge(sz_put, j * 16 + 16)
            A(eb[:], pt[:, 0, :], ACT.Copy).then_inc(evac_done, 1)
            act.wait_ge(mm_done, S + 4)
            act.wait_ge(u_done, j + 1)
            A(ea[:], pt[:, 1, :], ACT.Copy, scale=0.5)
            A(eb[:], pt[:, 1, :], ACT.Tanh, scale=0.5).then_inc(evac_done, 1)

        act.dma_start(acc_a[:], sz_d[0, :, :]).then_inc(sz_in[0], 16)
        act.wait_ge(v_done, C)

        def gated(i):
            if i + 1 < KT:
                if i:
                    act.wait_ge(yz_done, i)
                act.dma_start((ec if i % 2 == 0 else eb)[:], sz_d[i + 1, :, :]).then_inc(sz_in[(i + 1) % 2], 16)
            act.wait_ge(yz_done, i + 1)
            act.wait_ge(sq_used, KT + i)
            A(acc_b[:], xbc[:, i, :], ACT.Square).then_inc(sq_done, 1)

        def branch_high(i):
            act.wait_ge(mm_done, S_SB + i + 1)
            act.wait_ge(ys_done, i)
            A(ea[:], pt[:, i % 2, :], ACT.Copy).then_inc(evac_done, 1)
            act.wait_ge(ys_done, i + 1)
            A(sh[:, i, :], vbuf[:, i, :], ACT.Copy).then_inc(hi_done, 1)

        for i in range(KT):
            gated(i)
            if i in (3, 5):
                branch_high((i - 3) // 2)
        for i in range(2, KT):
            branch_high(i)

        act.wait_ge(mm_done, S_OUT)
        for i in range(KT):
            act.wait_ge(val_done, KT + i + 1)
            A(yh[:, i, :], xbc[:, i, :], ACT.Copy).then_inc(hi_done, 1)
        def mixer_out(n, u, c, waits):
            for w in waits:
                act.wait_ge(*w)
            A(mm[:, ds(n, 1), c].rearrange("p a t -> p (a t)"), pt[:, u, c], ACT.Copy)
            act.wait_ge(sq_used, 2 * KT + n)
            return A(eb[:, c], pt[:, u, c], ACT.Square)

        with act.Fori(0, KT // 2 - 1) as j:
            for u in range(2):
                n = j * 2 + u
                mixer_out(n, u, slice(0, T), [(mm_done, S_OUT + 2 * n + 2)]).then_inc(evac_done, 1)
        mixer_out(KT - 2, 0, slice(0, T), [(mm_done, S_OUT + 2 * KT - 2)]).then_inc(evac_done, 1)
        mixer_out(KT - 1, 1, cols(0), [(half_mm, 1)]).then_inc(half_ev, 1)

        def residual_high(q):
            h, k = divmod(q, KT)
            act.wait_ge((half_val, val_done)[h], (KT, 2 * KT)[h] + k + 1)
            A(xh[:, k, cols(h)], xres[:, k, cols(h)], ACT.Copy).then_inc((half_hi, hi_done)[h], 1)

        for q in range(2):
            residual_high(q)
        mixer_out(KT - 1, 1, cols(1), [(mm_done, S_OUT + 2 * KT)]).then_inc(evac_done, 1)

        def weight_high(S):
            act.wait_ge(w_loaded[1], 16 * (S // 2 + 1))
            act.wait_ge(mm_done, S)
            act.wait_ge(w_hi_done, S + 1)
            A(w_hi[:, 1, :], w_raw[:, 1, :], ACT.Copy).then_inc(w_hi_done, 1)

        weight_high(S_GATE)
        for q in range(2, 2 * KT):
            residual_high(q)

        with act.Fori(0, KT // 2) as j:
            for u in range(2):
                i = j * 2 + u
                act.wait_ge(val_done, 3 * KT + i)
                act.dma_start(eb[:], tile_of(pp_d, i)).then_inc(pp_in[u], 16)
                act.wait_ge(mm_done, S_GATE + i + 1)
                A(ea[:], pt[:, u, :], ACT.Tanh, scale=0.5).then_inc(evac_done, 1)
                act.wait_ge(val_done, 3 * KT + i + 1)
                A(h2[:, ds(i, 1), :], xres[:, ds(i, 1), :], ACT.Copy).then_inc(hi_done, 1)

        act.wait_ge(lo_done, 5 * KT)
        act.dma_start(wl_raw[:], w_low.rearrange("(k p) h -> p k h", p=P)).then_inc(b2_in, 16)
        act.dma_start(blow[0:RANK, :], b_low).then_inc(b2_in, 16)
        act.dma_start(wg2[0:RANK, :], w_gate2).then_inc(b2_in, 16)
        act.dma_start(wg2[RANK:RANK + 1, :], b_gate).then_inc(b2_in, 16)
        act.dma_start(wst[:], sg_w).then_inc(b2_in, 16)
        act.dma_start(rg[:].rearrange("p g t -> p (g t)"), sg_bs.to_broadcast([P, D])).then_inc(b2_in, 16)
        act.wait_ge(b2_in, 96)
        with act.Fori(0, KT // 2) as j:
            for u in range(2):
                i = j * 2 + u
                act.wait_ge(mm_done, S_AV + i + 1)
                act.wait_ge(tr_done, j * 2)
                A(ebuf[:, u, :], pt[:, u, :], ACT.Gelu_apprx_tanh, bias=V("b_v", i)).then_inc(evac_done, 1)
        act.wait_ge(low_mm, 1)
        act.wait_ge(low_ones_done, 1)
        for q in range(4):
            ins = A(alow[0:RANK, q * QUARTER:(q + 1) * QUARTER], wk[32 * q:32 * q + RANK, 2, 0:QUARTER], ACT.Identity,
                    bias=blow[0:RANK, :])
        ins.then_inc(low_done, 1)
        act.wait_ge(low_done, 1)
        act.wait_ge(tr_done, KT)
        A(alc[0:RANK + 1, 0, :], alow[0:RANK + 1, 0:P], ACT.Copy).then_inc(alc_done, 1)
        with act.Fori(0, KT // 2) as j:
            for u in range(2):
                i = j * 2 + u
                act.wait_ge(z_mm, i + 1)
                act.wait_ge(z_dve, i)
                A(ga_[:], wk[:, 0, :], ACT.Abs).then_inc(z_act, 1)
                act.wait_ge(z_act, i * 3 + 1)
                A(ge_[:], ga_[:], ACT.Exp, scale=-1.0).then_inc(z_act, 1)
                act.wait_ge(z_act, i * 3 + 2)
                A(gl_[:], ge_[:], ACT.Ln, bias=ones[:, 0:1]).then_inc(z_act, 1)
                A(alc[0:RANK + 1, 1 - u, :], alow[0:RANK + 1, ds((i + 1) % C * P, P)], ACT.Copy).then_inc(alc_done, 1)
                act.wait_ge(mm_done, S_QK + i + 1)
                act.wait_ge(qk_put[u], j * 16)
                A(ebuf[:, u, :], pt[:, u, :], ACT.Identity, scale=V("qk_s", i), bias=V("qk_b", i)).then_inc(evac_done, 1)
                act.wait_ge(evac_done, N_QK + i + 1)
                act.dma_start(tile_of(qk_d, i), ebuf[:, u, :]).then_inc(qk_put[u], 16)
                act.wait_ge(cu_mm, i + 1)
                act.wait_ge(cu_put, i * 16)
                A(cu_o[:], wk[:, 1, :], ACT.Copy, scale=1.0 / TEMP).then_inc(cu_done, 1)
                act.wait_ge(cu_done, i + 1)
                act.dma_start(tile_of(cu_d, i), cu_o[:]).then_inc(cu_put, 16)
        act.wait_ge(qk_put[0], 64)
        act.wait_ge(qk_put[1], 64)
        act.wait_ge(cu_put, 128)
        def value(i, u, turned):
            act.wait_ge(mm_done, S_VAL + i + 1)
            act.wait_ge(tr_done, turned)
            A(ebuf[:, u, :], pt[:, u, :], ACT.Identity, bias=V("b_val", i)).then_inc(evac_done, 1)

        def put_value(i, u):
            act.wait_ge(tr_used, KT + i + 1)
            act.dma_start(v_d.rearrange("c p f -> p c f")[:, :, ds(i * P, P)], vb[:, u, :, :]).then_inc(v_put[u], 16)

        with act.Fori(0, KT // 2 - 1) as j:
            for u in range(2):
                value(j * 2 + u, u, j * 2 + KT)
            for u in range(2):
                put_value(j * 2 + u, u)
        for u in range(2):
            value(KT - 2 + u, u, 2 * KT - 2)
        put_value(KT - 2, 0)
        act.wait_ge(mix_mm, KT)

        def load_chunk(i):
            act.dma_start(qkc[:, 0:2, :, :].rearrange("p a h t -> p (a h) t"),
                          qk_d.rearrange("i p t -> p i t")[:, :, ds(i * P, P)]).then_inc(ch_in, 16)
            act.dma_start(qkc[:, 2, :, :].rearrange("p h t -> p (h t)"), tile_of(cu_d, i)).then_inc(ch_in, 16)

        load_chunk(0)
        put_value(KT - 1, 1)
        act.wait_ge(gst_done, 1)
        with act.Fori(0, C // 2) as j:
            for u in range(2):
                i = j * 2 + u
                S = S_G + j * 6 + 3 * u
                if_slot = [(u + n) % 2 for n in range(3)]
                act.wait_ge(ch_in, i * 32 + 32)
                act.wait_ge(gst_done, i + 1)
                A(qe[:], qkc[:, 2, :, :], ACT.Exp).then_inc(end_exp, 1)
                A(etot[:], qkc[:, 2, :, P - 1], ACT.Exp).then_inc(end_exp, 1)
                for n in range(7):
                    act.wait_ge(arg_done, i * 7 + n + 1)
                    A(darg[:, n % 2, :, :], darg[:, n % 2, :, :], ACT.Exp).then_inc(lev_exp, 1)
                    if n == 1:
                        act.wait_ge(v_put[0], 64)
                        act.wait_ge(v_put[1], 64)
                        act.dma_start(vc[:], tile_of(v_d, i)).then_inc(vc_in, 16)
                    if n == 2:
                        act.wait_ge(end_arg, i + 1)
                        A(kd[:], kd[:], ACT.Exp).then_inc(end_exp, 1)
                    if n == 5:
                        act.wait_ge(mm_done, S + 1)
                        act.wait_ge(gb_done, i)
                        A(ea[:], pt[:, if_slot[0], :], ACT.Tanh, scale=0.5, bias=V("half_ga", i)).then_inc(evac_done, 1)
                act.wait_ge(mm_done, S + 2)
                A(eb[:], pt[:, if_slot[1], :], ACT.Identity, scale=V("half_gn", i), bias=V("half_rgn", i))
                A(ec[:], pt[:, if_slot[1], :], ACT.Tanh, scale=0.5, bias=V("half_r", i)).then_inc(evac_done, 1)
                act.wait_ge(kdt_mm, i + 1)
                A(kdt[:], wk[:, 3, :].rearrange("p (h t) -> p h t", h=GH), ACT.Copy).then_inc(kdt_done, 1)
                act.wait_ge(o_mm, i + 1)
                act.wait_ge(o_put, i * 16)
                A(oc[:], wka.rearrange("p (i t) -> p i t", i=8), ACT.Copy)
                A(osq[:], wka.rearrange("p (i t) -> p i t", i=8), ACT.Square).then_inc(o_act, 1)
                act.wait_ge(su_mm, i + 1)
                load_chunk((i + 1) % C)
                act.wait_ge(mm_done, S + 3)
                act.wait_ge(ga_done, i + 1)
                A(ea[:], pt[:, if_slot[2], :], ACT.Tanh, scale=0.5, bias=V("half_gb", i)).then_inc(evac_done, 1)
                act.wait_ge(on_done, i + 1)
                act.dma_start(o_d.rearrange("i p t -> p i t")[:, :, ds(i * P, P)], oc[:]).then_inc(o_put, 16)
        act.wait_ge(o_put, 128)
        act.wait_ge(gb_done, C)
        act.wait_ge(ch_in, (C + 1) * 32)

        with act.Fori(0, KT // 2) as j:
            for u in range(2):
                i = j * 2 + u
                act.wait_ge(lo_done, 5 * KT + i)
                act.dma_start(eb[:], tile_of(o_d, i)).then_inc(o_in, 16)
                act.wait_ge(mm_done, S_U + i + 1)
                A(ea[:], pt[:, u, :], ACT.Gelu_apprx_tanh, bias=V("b_u", i)).then_inc(evac_done, 1)
                act.wait_ge(m_done, i + 1)
                A(mh[:, ds(i, 1), :].rearrange("p a t -> p (a t)"), ea[:], ACT.Copy, scale=0.5).then_inc(hi_done, 1)
        act.wait_ge(lo_done, 6 * KT)
        with act.Fori(0, KT // 2 - 1) as j:
            for u in range(2):
                n = j * 2 + u
                act.wait_ge(mm_done, S_OUT2 + n + 1)
                act.wait_ge(y_done, n)
                A(ea[:], pt[:, u, :], ACT.Copy).then_inc(evac_done, 1)
                act.wait_ge(y_done, n + 1)
                act.wait_ge(a_used, n)
                A(eb[:], yr[:, ds(n, 1), :].rearrange("p a t -> p (a t)"), ACT.Square).then_inc(sq_done, 1)

        def last_copy(h, u):
            act.wait_ge((half_mm, mm_done)[h], (2 + u, S_OUT2 + KT - 1 + u)[h])
            act.wait_ge((y_done, half_y)[h], (KT - 2, 1 + u)[h])
            A(ea[:, cols(u)], pt[:, u, cols(h)], ACT.Copy).then_inc((half_ev, evac_done)[h], 1)

        def last_square(h, u):
            n = KT - 2 + u
            act.wait_ge((half_y, y_done)[h], (1 + u, n + 1)[h])
            act.wait_ge((a_used, half_acc)[h], (KT - 2, 2 + u)[h])
            A(eb[:, cols(u)], yr[:, n, cols(h)], ACT.Square).then_inc((half_sq, sq_done)[h], 1)

        def ln1(q):
            h, k = divmod(q, KT)
            act.wait_ge(ln_done, q + 1)
            A(yr[:, k, cols(h)], nrm[:, q % 2, :], ACT.Identity, scale=V("ln1_g", k), bias=V("ln1_b", k)).then_inc(h_done, 1)
            act.wait_ge(h_done, q + 1)
            A(h2[:, k, cols(h)], yr[:, k, cols(h)], ACT.Copy).then_inc((half_hi, hi_done)[h], 1)

        for h, u in ((0, 0), (0, 1), (1, 0)):
            last_copy(h, u)
            last_square(h, u)
        ln1(0)
        last_copy(1, 1)
        ln1(1)
        last_square(1, 1)
        weight_high(S_FF)
        for q in range(2, 2 * KT):
            ln1(q)
        def ff1(b):
            with act.Fori(0, KT // 2) as j:
                for u in range(2):
                    i = b * KT + j * 2 + u
                    act.wait_ge(mm_done, S_FF + b * 16 + j * 2 + u + 1)
                    act.wait_ge(f_lo, b * KT + j * 2)
                    A(ebuf[:, u, :], pt[:, u, :], ACT.Relu).then_inc(evac_done, 1)
                    act.wait_ge(f_sq, i + 1)
                    A(fh[:, ds(j * 2 + u, 1), :].rearrange("p a t -> p (a t)"), ebuf[:, u, :], ACT.Copy).then_inc(f_hi, 1)

        def ff2(b, pairs):
            with act.Fori(0, pairs) as j:
                for u in range(2):
                    i = b * KT + j * 2 + u
                    act.wait_ge(mm_done, S_FF + b * 16 + 8 + j * 2 + u + 1)
                    act.wait_ge(f_lo, b * KT + KT)
                    act.wait_ge(f_acc, b * KT + j * 2 + KT)
                    A(ebuf[:, u, :], pt[:, u, :], ACT.Copy).then_inc(evac_done, 1)
                    act.wait_ge(f_acc, i + (KT + 1))
                    act.wait_ge(a_used, KT + i)
                    A(ec[:], yr[:, ds(j * 2 + u, 1), :].rearrange("p a t -> p (a t)"), ACT.Square).then_inc(sq_done, 1)

        with act.Fori(0, FF_BLOCKS - 1) as b:
            ff1(b)
            ff2(b, KT // 2)
        ff1(FF_BLOCKS - 1)
        ff2(FF_BLOCKS - 1, KT // 2 - 1)

        def last_copy(h, u):
            act.wait_ge((half_mm, mm_done)[h], (4 + u, S_ALL - 1 + u)[h])
            act.wait_ge(f_acc, KT * FF_BLOCKS + KT - 2)
            A(ebuf[:, u, cols(h)], pt[:, u, cols(h)], ACT.Copy).then_inc((half_ev, evac_done)[h], 1)

        def last_square(h, u):
            n = KT - 2 + u
            act.wait_ge((half_y, f_acc)[h], (3 + u, KT * FF_BLOCKS + n + 1)[h])
            act.wait_ge((a_used, half_acc)[h], (KT * FF_BLOCKS + KT - 2, 4 + u)[h])
            A(ec[:, cols(u)], yr[:, n, cols(h)], ACT.Square).then_inc((half_sq, sq_done)[h], 1)

        def ln2(q):
            h, k = divmod(q, KT)
            act.wait_ge(ln_done, 2 * KT + q + 1)
            A(yr[:, k, cols(h)], nrm2[:, q % 2, :], ACT.Identity, scale=V("ln2_g", k), bias=V("ln2_b", k)).then_inc(h_done, 1)

        for h, u in ((0, 0), (0, 1), (1, 0)):
            last_copy(h, u)
            last_square(h, u)
        ln2(0)
        last_copy(1, 1)
        ln2(1)
        last_square(1, 1)
        for q in range(2, 2 * KT):
            ln2(q)

    @block.vector
    def _(dve):
        link = Chain(dve, d_chain)
        TT, TS, STT = nc.vector.tensor_tensor, nc.vector.tensor_scalar, nc.vector.scalar_tensor_tensor

        def rsqrt(y, v, t, done=None):
            link(TS(t.bitcast(i32), v.bitcast(i32), 1, None, ALU.arith_shift_right))
            link(TS(y.bitcast(i32), t.bitcast(i32), -1, 0x5f3759df, ALU.mult, ALU.add))
            for n in range(3):
                link(STT(out=t, in0=y, scalar=-0.5, in1=y, op0=ALU.mult, op1=ALU.mult))
                link(TT(out=t, in0=t, in1=v, op=ALU.mult))
                ins = STT(out=y, in0=t, scalar=1.5, in1=y, op0=ALU.add, op1=ALU.mult)
                if n < 2 or done is None:
                    link(ins)
                else:
                    ins.then_inc(done, 1)

        GLA_LINKS = 11

        link(nc.vector.memset(raw_p[:, :, 0:CW - 1], 0.0))
        dve.wait_ge(vec_in, 16)
        for k in range(2):
            dve.wait_ge(p_hi_done, k + 1)
            TT(out=p_lo[:, k, :], in0=p_raw[:, k, :], in1=p_hi[:, k, :].bitcast(f32), op=ALU.subtract).then_inc(p_lo_done, 1)
        def half_scale(h, n):
            dve.wait_ge(stat_done, n)
            a, b = 4 * h, 4 * h + 4
            link(TS(sm[:, 8 + a:8 + b], wk[:, 3, a:b], 1.0 / D, EPS1, ALU.mult, ALU.add))
            rsqrt(sm[:, a:b], sm[:, 8 + a:8 + b], sm[:, 16 + a:16 + b], rstd_done)

        def add_square(q):
            h, k = divmod(q, KT)
            dve.wait_ge((first_sq, sq_done)[h], k + 1)
            if k:
                dve.wait_ge((first_acc, sq_used)[h], k)
                ins = TT(out=acc_a[:, cols(h)], in0=acc_a[:, cols(h)], in1=ec[:, cols(q % 2)], op=ALU.add)
            else:
                ins = nc.vector.tensor_copy(acc_a[:, cols(h)], ec[:, cols(q % 2)])
            ins.then_inc((first_acc, sq_used)[h], 1)

        def scaled(q):
            h, k = divmod(q, KT)
            dve.wait_ge(spread_done, 1 + h)
            STT(out=x_raw[:, k, cols(h)], in0=x_raw[:, k, cols(h)], scalar=V("norm_pre", k), in1=wka[:, cols(h)],
                op0=ALU.mult, op1=ALU.mult).then_inc((half_val, val_done)[h], 1)
            if k:
                scaled_low(q - 1)

        def scaled_low(q):
            h, k = divmod(q, KT)
            dve.wait_ge((half_hi, hi_done)[h], k + 1)
            TT(out=xl[:, k, cols(h)], in0=x_raw[:, k, cols(h)], in1=xh[:, k, cols(h)].bitcast(f32),
               op=ALU.subtract).then_inc((half_lo, lo_done)[h], 1)

        for q in range(KT):
            add_square(q)
        half_scale(0, 1)
        for step, first, end in ((add_square, 8, 12), (scaled, 0, 4), (add_square, 12, 14), (scaled, 4, 6),
                                 (add_square, 14, 16), (scaled, 6, 8), (scaled_low, 7, 8)):
            for q in range(first, end):
                step(q)
        half_scale(1, 2)
        for q in range(KT, 2 * KT):
            scaled(q)
        scaled_low(2 * KT - 1)

        dve.wait_ge(cst, 1 + len(LEVELS))
        link(nc.vector.tensor_copy(lmask[:], lmask_f[:]))
        for new, old in (("half_ga", "b_ga"), ("half_r", "b_r"), ("half_gb", "b_gb"), ("half_gn", "gn")):
            link(TS(V(new, 0, 8), V(old, 0, 8), 0.5, None, ALU.mult))
        link(TT(out=V("half_rgn", 0, 8), in0=V("half_gn", 0, 8), in1=V("b_r", 0, 8), op=ALU.mult))
        link(nc.vector.memset(V("qk_s", 0, 4), Q_SCALE))
        link(nc.vector.memset(V("qk_s", 4, 4), 1.0))
        link(TT(out=V("qk_b", 0, 8), in0=V("qk_s", 0, 8), in1=V("b_qk", 0, 8), op=ALU.mult))

        def conv_pair(j):
            for u in range(2):
                dve.wait_ge(evac_done, j * 2 + (N_XBC + u + 1))
                dve.wait_ge(silu_done, j * 2)
                link(TS(conv_o[:, u, :], raw_p[:, u, 0:T], V("conv_w", j * 2 + u), V("conv_b", j * 2 + u), ALU.mult, ALU.add))
                for k in range(1, CW):
                    ins = STT(out=conv_o[:, u, :], in0=raw_p[:, u, k:k + T], scalar=V("conv_w", j * 2 + (u + k * XBC_T)),
                              in1=conv_o[:, u, :], op0=ALU.mult, op1=ALU.add)
                    if k < CW - 1:
                        link(ins)
                    else:
                        ins.then_inc(conv_done, 1)

        conv_pair(0)
        conv_pair(1)
        v, r_, e_, u_, l_, z_, q_, g_ = tmps
        ch = lambda t: t[:].rearrange("p (c h) -> p c h", c=C)
        dve.wait_ge(dt_mm, 2)
        TT(out=ch(v), in0=wk[:, 3, 0:P].rearrange("p (c h) -> p c h", c=C),
           in1=dtb[:].unsqueeze(1).to_broadcast([P, C, HEADS]), op=ALU.add).then_inc(dt_a, 1)
        dve.wait_ge(dt_a, 1)
        link(TS(r_[:], v[:], 0.0, None, ALU.max))
        dve.wait_ge(dt_b, 1)
        TS(u_[:], e_[:], 1.0, None, ALU.add).then_inc(dt_a, 1)
        dve.wait_ge(dt_a, 2)
        link(TS(q_[:], u_[:], -1.0, None, ALU.add))
        link(TS(z_[:], q_[:], 0.0, None, ALU.is_equal))
        link(TT(out=q_[:], in0=q_[:], in1=z_[:], op=ALU.add))
        link(nc.vector.reciprocal(g_[:], q_[:]))
        link(TT(out=q_[:], in0=g_[:], in1=e_[:], op=ALU.mult))
        dve.wait_ge(dt_b, 3)
        link(TT(out=q_[:], in0=q_[:], in1=l_[:], op=ALU.mult))
        link(TT(out=z_[:], in0=z_[:], in1=e_[:], op=ALU.mult))
        link(TT(out=q_[:], in0=q_[:], in1=z_[:], op=ALU.add))
        link(TT(out=dtt[:], in0=ch(q_), in1=ch(r_), op=ALU.add))
        link(TS(alr[:], alr[:], -1.0, None, ALU.mult))
        TT(out=adt[:], in0=dtt[:], in1=alr[:].unsqueeze(1).to_broadcast([P, C, HEADS]), op=ALU.mult).then_inc(adt_done, 1)

        with dve.Fori(2, XBC_T // 2 - 1) as j:
            link.enter(j - 2, 2 * (CW - 1))
            conv_pair(j)
        link.leave(XBC_T // 2 - 3)

        dve.wait_ge(dec_done, 2)
        TT(out=dec[:], in0=wk[:, 3, P:2 * P], in1=acs[:].rearrange("p c h -> p (c h)"), op=ALU.subtract).then_inc(dec_arg, 1)
        conv_pair(XBC_T // 2 - 1)
        nc.vector.memset(state[:], 0.0)
        link(nc.vector.memset(ecp[:, 0:SW - 1], 0.0))
        dve.wait_ge(dec_done, 3)

        SC_LINKS = 7
        with dve.Fori(0, C) as j:
            link.enter(j, SC_LINKS)
            N = N_SC + j * 4
            dve.wait_ge(row_in, j * 16 + 16)
            dve.wait_ge(ce_exp, j * 2 + 2)
            for h in range(HEADS):
                ins = TS(rowb[:, h, :], rowb[:, h, :], acs[:].rearrange("p c h -> p (c h)")[:, ds(j * HEADS + h, 1)],
                         0.0, ALU.subtract, ALU.min)
            ins.then_inc(e_arg, 1)
            dve.wait_ge(ssd_a, j + 1)
            dts = dtt[:, ds(j, 1), :].rearrange("p a h -> p (a h)").unsqueeze(2).to_broadcast([P, HEADS, HP])
            link(TT(out=xd[:], in0=wka.rearrange("p (h q) -> p h q", h=HEADS), in1=dts, op=ALU.mult))
            decs = dec[:, ds(j * HEADS, HEADS)].unsqueeze(2).to_broadcast([P, HEADS, HP])
            TT(out=xdd[:], in0=xd[:], in1=decs, op=ALU.mult).then_inc(xdd_done, 1)
            dve.wait_ge(bt_done, j + 1)
            for g in range(GROUPS):
                cb_src = wk[:, 2, P:2 * P] if g == 0 else wk[:, 3, 0:P]
                ins = TT(out=cbm[:, g, :], in0=cb_src, in1=tri[:], op=ALU.mult)
            link(ins)
            TT(out=ce[:], in0=ce[:], in1=st[:, XBC_T - 1, :].unsqueeze(1).to_broadcast([P, HG, P]),
               op=ALU.mult).then_inc(ce_done, 1)
            dve.wait_ge(e_exp, j + 1)
            for g in range(GROUPS):
                ins = TT(out=rowb[:, g * HG:(g + 1) * HG, :], in0=rowb[:, g * HG:(g + 1) * HG, :],
                         in1=cbm[:, g, :].unsqueeze(1).to_broadcast([P, HG, P]), op=ALU.mult)
            ins.then_inc(m_ready, 1)
            dve.wait_ge(evac_done, N + 1)
            STT(out=eb[:], in0=eb[:], scalar=1.0, in1=ea[:], op0=ALU.add, op1=ALU.mult).then_inc(sz_done, 1)
            dve.wait_ge(ssd_b, j + 1)
            for i in range(KT):
                ins = STT(out=xbc[:, i, ds(j * P, P)], in0=st[:, i, :], scalar=V("d_skip", i),
                          in1=wka[:, i * P:(i + 1) * P], op0=ALU.mult, op1=ALU.add)
            ins.then_inc(y_evac, 1)
            for g in range(GROUPS):
                rows, hs = slice(g * 64, g * 64 + 64), slice(g * HG, (g + 1) * HG)
                ins = TT(out=state[rows, hs, :], in0=state[rows, hs, :],
                         in1=et2[rows, ds(j, 1), :].rearrange("p a h -> p (a h)").unsqueeze(2).to_broadcast([64, HG, HP]),
                         op=ALU.mult)
            link(ins)
            for g in range(GROUPS):
                rows, hs = slice(g * 64, g * 64 + 64), slice(g * HG, (g + 1) * HG)
                ins = TT(out=state[rows, hs, :], in0=state[rows, hs, :],
                         in1=wk[rows, 3, :].rearrange("p (h q) -> p h q", h=HG), op=ALU.add)
            ins.then_inc(s_ready, 1)
            dve.wait_ge(evac_done, N + 3)
            TT(out=ecp[:, SW - 1:SW - 1 + T], in0=ea[:], in1=eb[:], op=ALU.mult).then_inc(u_done, 1)
            dve.wait_ge(u_done, j + 1)
            vj = row(vbuf, j)
            link(TS(vj, ecp[:, 0:T], V("sc_w", j), None, ALU.mult))
            for k in range(1, SW):
                link(STT(out=vj, in0=ecp[:, k:k + T], scalar=V("sc_w", j + 8 * k), in1=vj, op0=ALU.mult, op1=ALU.add))
            dve.wait_ge(evac_done, N + 4)
            link(STT(out=ea[:], in0=eb[:], scalar=1.0, in1=ea[:], op0=ALU.add, op1=ALU.mult))
            TT(out=vj, in0=vj, in1=ea[:], op=ALU.mult).then_inc(v_done, 1)
        link.leave(C)

        dve.wait_ge(y_evac, C)
        def gated(i):
            acc = acc_g[:, i // 4, :]
            buf = (eb if i else acc_a) if i % 2 == 0 else ec
            dve.wait_ge(sz_in[i % 2], 16 * (i // 2 + 1))
            TT(out=xbc[:, i, :], in0=xbc[:, i, :], in1=buf[:], op=ALU.mult).then_inc(yz_done, 1)
            if i:
                dve.wait_ge(sq_used, KT + i)
            dve.wait_ge(sq_done, KT + i + 1)
            if i % 4 == 0:
                nc.vector.tensor_copy(acc, acc_b[:]).then_inc(sq_used, 1)
            else:
                TT(out=acc, in0=acc, in1=acc_b[:], op=ALU.add).then_inc(sq_used, 1)

        def branch(i):
            dve.wait_ge(evac_done, N_SB + i + 1)
            TT(out=vbuf[:, i, :], in0=vbuf[:, i, :], in1=ea[:], op=ALU.mult).then_inc(ys_done, 1)
            dve.wait_ge(hi_done, KT + i + 1)
            TT(out=sl[:, i, :], in0=vbuf[:, i, :], in1=sh[:, i, :].bitcast(f32), op=ALU.subtract).then_inc(lo_done, 1)

        for i in range(KT):
            gated(i)
            if i in (3, 5):
                branch((i - 3) // 2)
        for i in range(2, 4):
            branch(i)
        dve.wait_ge(stat_done, 3)
        link(TS(sm[:, 16:32], wk[:, 3, 0:16], 2.0 / D, EPS1, ALU.mult, ALU.add))
        rsqrt(sm[:, 0:16], sm[:, 16:32], sm[:, 32:48], rstd_done)
        for i in range(4, 6):
            branch(i)
        dve.wait_ge(spread_done, 3)
        for i in range(KT):
            STT(out=xbc[:, i, :], in0=xbc[:, i, :], scalar=V("ssd_norm", i), in1=wka if i < 4 else wkb, op0=ALU.mult,
                op1=ALU.mult).then_inc(val_done, 1)
        for i in range(6, KT):
            branch(i)
        for i in range(KT):
            dve.wait_ge(hi_done, 2 * KT + i + 1)
            TT(out=yl[:, i, :], in0=xbc[:, i, :], in1=yh[:, i, :].bitcast(f32), op=ALU.subtract).then_inc(lo_done, 1)

        link(nc.vector.memset(acc_a[:], 0.0))
        with dve.Fori(0, KT // 2 - 1) as j:
            for u in range(2):
                n = j * 2 + u
                dve.wait_ge(evac_done, N_OUT + n + 1)
                dve.wait_ge(sq_used, 2 * KT + n)
                TT(out=acc_a[:], in0=acc_a[:], in1=eb[:], op=ALU.add).then_inc(sq_used, 1)
        dve.wait_ge(evac_done, N_OUT + KT - 1)
        dve.wait_ge(sq_used, 3 * KT - 2)
        TT(out=acc_a[:], in0=acc_a[:], in1=eb[:], op=ALU.add).then_inc(sq_used, 1)

        def last_squares(h):
            dve.wait_ge((half_ev, evac_done)[h], (1, N_OUT + KT)[h])
            dve.wait_ge(sq_used, 3 * KT - 1)
            TT(out=acc_a[:, cols(h)], in0=acc_a[:, cols(h)], in1=eb[:, cols(h)], op=ALU.add).then_inc((half_acc, sq_used)[h], 1)

        def weight_low(S):
            dve.wait_ge(w_hi_done, S + 2)
            dve.wait_ge(w_split, S + 1)
            TT(out=w_lo[:, 1, :], in0=w_raw[:, 1, :], in1=w_hi[:, 1, :].bitcast(f32), op=ALU.subtract).then_inc(w_split, 1)

        def residual(q):
            h, k = divmod(q, KT)
            c = cols(h)
            dve.wait_ge(spread_done, 4 + h)
            link(STT(out=nrm[:, q % 2, :], in0=mm[:, k, c], scalar=V("norm_post", k), in1=wka[:, c], op0=ALU.mult, op1=ALU.mult))
            dve.wait_ge(x_in[h][k], 32)
            TT(out=xres[:, k, c], in0=xres[:, k, c], in1=nrm[:, q % 2, :], op=ALU.add).then_inc((half_val, val_done)[h], 1)

        last_squares(0)
        half_scale(0, 4)
        residual(0)
        residual(1)
        last_squares(1)
        weight_low(S_GATE)
        residual(2)
        residual(3)
        half_scale(1, 5)
        for q in range(4, 2 * KT):
            residual(q)
        with dve.Fori(0, KT // 2) as j:
            link.enter(j, 2)
            for u in range(2):
                i = j * 2 + u
                dve.wait_ge(evac_done, N_GATE + i + 1)
                dve.wait_ge(pp_in[u], j * 16 + 16)
                link(STT(out=ea[:], in0=ea[:], scalar=1.0, in1=eb[:], op0=ALU.add, op1=ALU.mult))
                TT(out=row(xres, i), in0=row(xres, i), in1=ea[:], op=ALU.add).then_inc(val_done, 1)
                dve.wait_ge(val_done, 3 * KT + i + 1)
                dve.wait_ge(hi_done, 4 * KT + i + 1)
                TT(out=row(l2, i), in0=row(xres, i), in1=row(h2, i).bitcast(f32), op=ALU.subtract).then_inc(lo_done, 1)
        link.leave(KT // 2)

        dve.wait_ge(b2_in, 96)
        nc.vector.memset(alow[0:RANK + 1, :], 1.0).then_inc(low_ones_done, 1)
        TT(out=wst[:], in0=wst[:], in1=tri[:].unsqueeze(1).to_broadcast([P, KT, P]), op=ALU.mult).then_inc(ws_done, 1)
        def gating(i):
            dve.wait_ge(tr_done, i + 1)
            nc.vector.tensor_copy(av[:, :, ds(i * P, P)], wka.rearrange("p (c f) -> p c f", c=C)).then_inc(tr_used, 1)

        with dve.Fori(0, KT // 2 - 1) as j:
            for u in range(2):
                gating(j * 2 + u)
        dve.wait_ge(row_mm, 1)
        for g in range(KT):
            ins = STT(out=rg[:, g, :], in0=wkb[:, g * P:(g + 1) * P], scalar=V("sg_b", g), in1=rg[:, g, :],
                      op0=ALU.mult, op1=ALU.add)
        ins.then_inc(rg_done, 1)
        gating(KT - 2)
        gating(KT - 1)
        dve.wait_ge(tr_used, KT)
        with dve.Fori(0, KT // 2) as j:
            link.enter(j, 2)
            for u in range(2):
                i = j * 2 + u
                dve.wait_ge(z_mm, i + 1)
                dve.wait_ge(z_dve, i)
                dve.wait_ge(cu_mm, i)
                dve.wait_ge(z_act, i * 3 + 1)
                link(TS(gm_[:], wk[:, 0, :], 0.0, None, ALU.min))
                dve.wait_ge(z_act, i * 3 + 3)
                TT(out=gm_[:], in0=gm_[:], in1=gl_[:], op=ALU.subtract).then_inc(z_dve, 1)
                for h in range(2):
                    ins = nc.vector.bn_stats(row(bnst, i * 2 + h), av[:, ds(i, 1), h * HALF:(h + 1) * HALF].rearrange("p a f -> p (a f)"))
                ins.then_inc(bn_done, 1)
        link.leave(KT // 2)
        dve.wait_ge(bn_done, C)
        for c in range(C):
            ins = nc.vector.bn_aggr(bnag[:, c, :], bnst[:, 2 * c:2 * c + 2, :].rearrange("p h s -> p (h s)"))
        link(ins)
        link(TS(sm[:, 8:16], bnag[:, :, 1], EPS2, None, ALU.add))
        rsqrt(sm[:, 0:8], sm[:, 8:16], sm[:, 16:24], rstd_done)
        dve.wait_ge(rstd_done, 6)
        link(STT(out=sm[:, 24:32], in0=bnag[:, :, 0], scalar=-1.0, in1=sm[:, 0:8], op0=ALU.mult, op1=ALU.mult))
        for c in range(C):
            TS(av[:, c, :], av[:, c, :], sm[:, c:c + 1], sm[:, 24 + c:25 + c], ALU.mult, ALU.add).then_inc(av_done, 1)
        def value(i):
            dve.wait_ge(tr_done, i + (KT + 1))
            if i >= 2:
                dve.wait_ge(v_put[i % 2], 16 * (i // 2))
            nc.vector.tensor_copy(vb[:, i % 2, :, :], wka.rearrange("p (c f) -> p c f", c=C)).then_inc(tr_used, 1)

        def mixed(g):
            dve.wait_ge(mix_mm, g + 1)
            STT(out=mix[:, g, :].rearrange("p (c t) -> p c t", c=C), in0=wkb.rearrange("p (c t) -> p c t", c=C),
                scalar=V("sg_g", g), in1=rg[:, g, :].unsqueeze(1).to_broadcast([P, C, P]), op0=ALU.mult,
                op1=ALU.add).then_inc(mix_done, 1)

        for i in range(KT - 1):
            value(i)
            mixed(i)
        mixed(KT - 1)

        link(nc.vector.memset(gst[:], 0.0))
        link(nc.vector.memset(sc[:], 0.0))
        link(nc.vector.memset(kp[:], 0.0))
        nc.vector.memset(qc[:], 0.0).then_inc(gst_done, 1)
        value(KT - 1)

        def second(ap, m):
            return ap.rearrange("p h (b two r) -> p (h b) two r", two=2, r=m)[:, :, 1, :]

        def first(ap, m):
            return ap.rearrange("p h (b two r) -> p (h b) two r", two=2, r=m)[:, :, 0, :]

        with dve.Fori(0, C // 2) as j:
            link.enter(j, 2 * GLA_LINKS)
            for u in range(2):
                i = j * 2 + u
                N = N_G + j * 6 + 3 * u
                q_, k_, c_ = qkc[:, 0, :, :], qkc[:, 1, :, :], qkc[:, 2, :, :]
                slots = [(u + n) % 2 for n in range(3)]

                def args(n):
                    m = LEVELS[n]
                    ref = c_.rearrange("p h (b two r) -> p (h b) two r", two=2, r=m)[:, :, 0, m - 1:m]
                    ref = ref.to_broadcast([P, 256 // m, m])
                    if n >= 2:
                        dve.wait_ge(lev_ready, i * 7 + n - 1)
                    d = darg[:, n % 2, :, :].rearrange("p a (b r) -> p a b r", r=m)
                    TT(out=d[:, 0], in0=second(c_, m), in1=ref, op=ALU.subtract)
                    TT(out=d[:, 1], in0=ref, in1=first(c_, m), op=ALU.subtract).then_inc(arg_done, 1)

                def scale(n, picked):
                    m = LEVELS[n]
                    dve.wait_ge(lev_exp, i * 7 + n + 1)
                    if n >= 2:
                        dve.wait_ge(lev_mm, i * 7 + n - 1)
                    if picked:
                        dve.wait_ge(lev_used, i * 7 + picked)
                    d = darg[:, n % 2, :, :].rearrange("p a (b r) -> p a b r", r=m)
                    TT(out=qc[:, n % 2, :, :].rearrange("p h (b r) -> p (h b) r", r=m), in0=second(q_, m), in1=d[:, 0], op=ALU.mult)
                    TT(out=first(kp[:, n % 2, :, :], m), in0=first(k_, m), in1=d[:, 1], op=ALU.mult).then_inc(lev_ready, 1)

                def pick(n):
                    m = LEVELS[n]
                    nb = 64 // m
                    dve.wait_ge(cst, 1 + len(LEVELS))
                    dve.wait_ge(lev_mm, i * 7 + n + 1)
                    out = sc[:].rearrange("p h (b two r) -> p h b two r", two=2, r=m)[:, :, :, 1, :]
                    mask = lmask[:, n, :].rearrange("p (b r) -> p b r", r=m).unsqueeze(1).to_broadcast([P, GH, nb, m])
                    src = wk[:, n % 2, 0:256].rearrange("p (h b r) -> p h b r", h=GH, r=m)
                    nc.vector.copy_predicated(out, mask, src).then_inc(lev_used, 1)

                dve.wait_ge(ch_in, i * 32 + 32)
                dve.wait_ge(lev_ready, i * 7)
                args(0)
                args(1)
                scale(0, 0)
                TT(out=kd[:], in0=c_[:, :, P - 1:P].to_broadcast([P, GH, P]), in1=c_, op=ALU.subtract).then_inc(end_arg, 1)
                dve.wait_ge(dg_mm, i + 1)
                args(2)
                dmask = ident[:].bitcast(u32).unsqueeze(1).to_broadcast([P, GH, P])
                nc.vector.copy_predicated(sc[:], dmask, wk[:, 2, :].rearrange("p (h t) -> p h t", h=GH)).then_inc(sc_done, 1)
                dve.wait_ge(sc_done, i + 1)
                scale(1, 0)
                pick(0)
                for n in range(2, 7):
                    if n + 1 < 7:
                        args(n + 1)
                    scale(n, n - 1)
                    pick(n - 1)
                    if n == 3:
                        dve.wait_ge(end_exp, i * 3 + 3)
                        TT(out=qe[:], in0=qe[:], in1=q_, op=ALU.mult)
                        TT(out=kd[:], in0=kd[:], in1=k_, op=ALU.mult).then_inc(kd_done, 1)
                dve.wait_ge(evac_done, N + 1)
                dve.wait_ge(lev_used, i * 7 + 6)
                STT(out=row(mix, i), in0=ea[:], scalar=1.0, in1=row(mix, i), op0=ALU.add, op1=ALU.mult).then_inc(ga_done, 1)
                pick(6)
                dve.wait_ge(evac_done, N + 2)
                STT(out=row(gbuf, i), in0=ec[:], scalar=1.0, in1=eb[:], op0=ALU.add, op1=ALU.mult).then_inc(r_done, 1)
                dve.wait_ge(su_mm, i + 1)
                for h in range(GH):
                    ins = STT(out=gst[:, h, :], in0=gst[:, h, :], scalar=etot[:, h:h + 1],
                              in1=wk[:, 2 + h // 2, (h % 2) * GV:(h % 2 + 1) * GV], op0=ALU.mult, op1=ALU.add)
                ins.then_inc(gst_done, 1)
                dve.wait_ge(o_act, i + 1)
                pairs = osq[:].rearrange("p (h w) t -> p h w t", w=2)
                TT(out=pairs[:, :, 0, :], in0=pairs[:, :, 0, :], in1=pairs[:, :, 1, :], op=ALU.add).then_inc(o_sum, 1)
                dve.wait_ge(o_stat, i + 1)
                link(TS(sm[:, 4:8], wk[:, 0, 0:GH], 1.0 / GV, EPS2, ALU.mult, ALU.add))
                rsqrt(sm[:, 0:4], sm[:, 4:8], sm[:, 8:12], o_rstd)
                dve.wait_ge(evac_done, N + 3)
                dve.wait_ge(r_done, i + 1)
                STT(out=row(gbuf, i), in0=ea[:], scalar=1.0, in1=row(gbuf, i), op0=ALU.add, op1=ALU.mult).then_inc(gb_done, 1)
                dve.wait_ge(o_spread, i + 1)
                TT(out=oc[:].rearrange("p (h w) t -> p h w t", w=2), in0=oc[:].rearrange("p (h w) t -> p h w t", w=2),
                   in1=wk[:, 1, :].rearrange("p (h t) -> p h t", h=GH).unsqueeze(2).to_broadcast([P, GH, 2, P]),
                   op=ALU.mult).then_inc(on_done, 1)
        link.leave(C // 2)

        with dve.Fori(0, KT // 2) as j:
            link.enter(j, 4)
            for u in range(2):
                i = j * 2 + u
                dve.wait_ge(o_in, i * 16 + 16)
                link(TT(out=eb[:], in0=eb[:], in1=row(gbuf, i), op=ALU.mult))
                dve.wait_ge(evac_done, N_U + i + 1)
                link(TT(out=ea[:], in0=ea[:], in1=row(mix, i), op=ALU.mult))
                TT(out=ea[:], in0=ea[:], in1=eb[:], op=ALU.add).then_inc(m_done, 1)
                dve.wait_ge(m_done, i + 1)
                dve.wait_ge(hi_done, 5 * KT + i + 1)
                STT(out=row(ml, i), in0=ea[:], scalar=0.5, in1=row(mh, i).bitcast(f32), op0=ALU.mult,
                    op1=ALU.subtract).then_inc(lo_done, 1)
        link.leave(KT // 2)

        link(nc.vector.memset(acc_a[:], 0.0))
        link(nc.vector.memset(acc_b[:], 0.0))
        with dve.Fori(0, KT // 2 - 1) as j:
            link.enter(j, 2)
            for u in range(2):
                n = j * 2 + u
                dve.wait_ge(evac_done, N_OUT2 + n + 1)
                link(STT(out=ea[:], in0=row(h2, n).bitcast(f32), scalar=ALPHA, in1=ea[:], op0=ALU.mult, op1=ALU.add))
                STT(out=row(yr, n), in0=row(l2, n).bitcast(f32), scalar=ALPHA, in1=ea[:], op0=ALU.mult,
                    op1=ALU.add).then_inc(y_done, 1)
                dve.wait_ge(y_done, n + 1)
                dve.wait_ge(a_used, n)
                TT(out=acc_a[:], in0=acc_a[:], in1=row(yr, n), op=ALU.add)
                dve.wait_ge(sq_done, 2 * KT + n + 1)
                TT(out=acc_b[:], in0=acc_b[:], in1=eb[:], op=ALU.add).then_inc(a_used, 1)
        link.leave(KT // 2 - 1)

        def add_up(h, u, ready, before, squares, sq):
            n, c = KT - 2 + u, cols(h)
            dve.wait_ge(*ready)
            dve.wait_ge(*before)
            TT(out=acc_a[:, c], in0=acc_a[:, c], in1=yr[:, n, c], op=ALU.add)
            dve.wait_ge(*squares)
            TT(out=acc_b[:, c], in0=acc_b[:, c], in1=sq[:, cols(u)], op=ALU.add).then_inc((half_acc, a_used)[h], 1)

        def sums_before(h, u, used, halves):
            if h == 0:
                return (a_used, used) if u == 0 else (half_acc, halves)
            return (a_used, used + u)

        def last_y(h, u):
            n, c, b = KT - 2 + u, cols(h), cols(u)
            dve.wait_ge((half_ev, evac_done)[h], (2 + u, N_OUT2 + n + 1)[h])
            link(STT(out=ea[:, b], in0=h2[:, n, c].bitcast(f32), scalar=ALPHA, in1=ea[:, b], op0=ALU.mult, op1=ALU.add))
            STT(out=yr[:, n, c], in0=l2[:, n, c].bitcast(f32), scalar=ALPHA, in1=ea[:, b], op0=ALU.mult,
                op1=ALU.add).then_inc((half_y, y_done)[h], 1)
            add_up(h, u, ((half_y, 1 + u), (y_done, n + 1))[h], sums_before(h, u, KT - 2, 2),
                   ((half_sq, 1 + u), (sq_done, 2 * KT + n + 1))[h], eb)

        def ln_scale(h, stats):
            dve.wait_ge(stat_done, stats + h)
            a = 4 * h
            mean, var, r = sm[:, 24 + a:28 + a], sm[:, 16 + a:20 + a], sm[:, a:4 + a]
            link(TS(mean, wk[:, 3, a:4 + a], 1.0 / D, None, ALU.mult))
            link(TT(out=var, in0=mean, in1=mean, op=ALU.mult))
            link(STT(out=var, in0=wk[:, 3, 8 + a:12 + a], scalar=1.0 / D, in1=var, op0=ALU.mult, op1=ALU.subtract))
            link(TS(var, var, 0.0, EPS2, ALU.max, ALU.add))
            rsqrt(r, var, sm[:, 32 + a:36 + a])
            STT(out=sm[:, 8 + a:12 + a], in0=mean, scalar=-1.0, in1=r, op0=ALU.mult, op1=ALU.mult).then_inc(rstd_done, 1)

        def normalise(q, buf, count, stats):
            h, k = divmod(q, KT)
            dve.wait_ge(spread_done, stats + h)
            if q >= 2:
                dve.wait_ge(h_done, count + q - 1)
            link(TT(out=buf[:, q % 2, :], in0=yr[:, k, cols(h)], in1=wka[:, cols(h)], op=ALU.mult))
            TT(out=buf[:, q % 2, :], in0=buf[:, q % 2, :], in1=wkb[:, cols(h)], op=ALU.add).then_inc(ln_done, 1)

        last_y(0, 0)
        last_y(0, 1)
        ln_scale(0, 6)
        last_y(1, 0)
        normalise(0, nrm, 0, 6)
        normalise(1, nrm, 0, 6)
        last_y(1, 1)
        weight_low(S_FF)
        normalise(2, nrm, 0, 6)
        normalise(3, nrm, 0, 6)
        ln_scale(1, 6)
        for q in range(4, 2 * KT):
            normalise(q, nrm, 0, 6)
        for k in range(KT):
            dve.wait_ge(lo_done, 6 * KT + k + 1)
            TS(yr[:, k, :], yr[:, k, :], ALPHA, None, ALU.mult).then_inc(f_acc, 1)

        def ff1(b):
            with dve.Fori(0, KT // 2) as j:
                for u in range(2):
                    i = b * KT + j * 2 + u
                    dve.wait_ge(evac_done, N_FF + b * 16 + j * 2 + u + 1)
                    TT(out=ebuf[:, u, :], in0=ebuf[:, u, :], in1=ebuf[:, u, :], op=ALU.mult).then_inc(f_sq, 1)
                    dve.wait_ge(f_sq, i + 1)
                    dve.wait_ge(f_hi, i + 1)
                    TT(out=row(fl, j * 2 + u), in0=ebuf[:, u, :], in1=row(fh, j * 2 + u).bitcast(f32),
                       op=ALU.subtract).then_inc(f_lo, 1)
            nc.vector.memset(acc_a[:], 0.0).then_inc(f_zero, 1)
            nc.vector.memset(acc_b[:], 0.0).then_inc(f_zero, 1)

        def ff2(b, pairs):
            with dve.Fori(0, pairs) as j:
                for u in range(2):
                    i = b * KT + j * 2 + u
                    yn = row(yr, j * 2 + u)
                    dve.wait_ge(evac_done, N_FF + b * 16 + 8 + j * 2 + u + 1)
                    dve.wait_ge(f_acc, i + KT)
                    TT(out=yn, in0=yn, in1=ebuf[:, u, :], op=ALU.add).then_inc(f_acc, 1)
                    dve.wait_ge(f_acc, i + KT + 1)
                    dve.wait_ge(a_used, i + KT)
                    dve.wait_ge(f_zero, b * 2 + 2)
                    TT(out=acc_a[:], in0=acc_a[:], in1=yn, op=ALU.add)
                    dve.wait_ge(sq_done, i + 3 * KT + 1)
                    TT(out=acc_b[:], in0=acc_b[:], in1=ec[:], op=ALU.add).then_inc(a_used, 1)

        with dve.Fori(0, FF_BLOCKS - 1) as b:
            ff1(b)
            ff2(b, KT // 2)
        ff1(FF_BLOCKS - 1)
        ff2(FF_BLOCKS - 1, KT // 2 - 1)

        def last_f(h, u):
            n, c, done = KT - 2 + u, cols(h), KT * FF_BLOCKS
            dve.wait_ge((half_ev, evac_done)[h], (4 + u, N_FF + 16 * FF_BLOCKS - 1 + u)[h])
            dve.wait_ge(f_acc, done + KT - 2)
            TT(out=yr[:, n, c], in0=yr[:, n, c], in1=ebuf[:, u, c], op=ALU.add).then_inc((half_y, f_acc)[h], 1)
            add_up(h, u, ((half_y, 3 + u), (f_acc, done + n + 1))[h], sums_before(h, u, done + KT - 2, 4),
                   ((half_sq, 3 + u), (sq_done, done + 2 * KT + n + 1))[h], ec)

        last_f(0, 0)
        last_f(0, 1)
        ln_scale(0, 8)
        last_f(1, 0)
        normalise(0, nrm2, 2 * KT, 8)
        normalise(1, nrm2, 2 * KT, 8)
        last_f(1, 1)
        normalise(2, nrm2, 2 * KT, 8)
        normalise(3, nrm2, 2 * KT, 8)
        ln_scale(1, 8)
        for q in range(4, 2 * KT):
            normalise(q, nrm2, 2 * KT, 8)

    @block.tensor
    def _(pe):
        MM = nc.tensor.matmul

        def project(S, N, w, slot, xs, k_ready=None, first=True, last=True, between=None):
            xhi, xlo = xs
            pe.wait_ge(w_split, S + 1)
            if first and N is not None:
                pe.wait_ge(evac_done, N)
            for k in range(KT):
                if k_ready is not None:
                    pe.wait_ge(k_ready[0], k_ready[1] + k + 1)
                for n, (wt, x) in enumerate(((w_hi, xhi), (w_hi, xlo), (w_lo, xhi))):
                    for h in range(2):
                        ins = MM(pt[:, slot, h * HALF:(h + 1) * HALF], wt[:, w, k * P:(k + 1) * P],
                                 x[:, k, h * HALF:(h + 1) * HALF], start=first and k == 0 and n == 0,
                                 stop=last and k == KT - 1 and n == 2)
                if k == KT - 1:
                    ins.then_inc(mm_done, 1)
                if between is not None:
                    between(k)

        def pair(j, S, N, xs, k_ready=None):
            for u in range(2):
                project(j * 2 + (S + u), j * 2 + (N + u - 1), u, u, xs, k_ready)

        def project_half(w, slot, xs, h, first=True, last=True, between=None):
            for k in range(KT):
                for n, (wt, x) in enumerate(((w_hi, xs[0]), (w_hi, xs[1]), (w_lo, xs[0]))):
                    ins = MM(pt[:, slot, cols(h)], wt[:, w, k * P:(k + 1) * P], x[:, k, cols(h)],
                             start=first and k == 0 and n == 0, stop=last and k == KT - 1 and n == 2)
                if between is not None and k < KT - 1:
                    between(k)
            return ins

        def pair_by_half(S, N, xs, half_base, base, between, tile_first=False):
            def step(h, k, u):
                pe.wait_ge(w_split, S + 1 + u)
                pe.wait_ge(evac_done, N - 1 + u)
                pe.wait_ge((half_lo, lo_done)[h], (half_base, base)[h] + k + 1)
                for n, (wt, x) in enumerate(((w_hi, xs[0]), (w_hi, xs[1]), (w_lo, xs[0]))):
                    ins = MM(pt[:, u, cols(h)], wt[:, u, k * P:(k + 1) * P], x[:, k, cols(h)],
                             start=k == 0 and n == 0, stop=k == KT - 1 and n == 2)
                if h == 1 and k == KT - 1:
                    ins.then_inc(mm_done, 1)

            order = [(k, u) for u in range(2) for k in range(KT)] if tile_first else [(k, u) for k in range(KT) for u in range(2)]
            for n, (k, u) in enumerate(order):
                step(0, k, u)
                between(n)
            for k in range(KT):
                for u in range(2):
                    step(1, k, u)

        def sums(acc, col):
            for c in range(C):
                ins = MM(wk[:, 3, col + c:col + c + 1], acc[:, c * P:(c + 1) * P], ones[:, 0:1], start=True, stop=True)
            return ins

        def narrow(bank, w, xs):
            for k in range(KT):
                for n, x in enumerate(xs):
                    for q in range(4):
                        ins = MM(wk[32 * q:32 * q + 16, bank, 0:QUARTER], w[:, k, :],
                                 x[:, k, q * QUARTER:(q + 1) * QUARTER].bitcast(f32),
                                 start=k == 0 and n == 0, stop=k == KT - 1 and n == 1, tile_position=(0, 32 * q))
            return ins

        def half_sums(acc, col, h):
            for c in range(4 * h, 4 * h + 4):
                ins = MM(wk[:, 3, col + c:col + c + 1], acc[:, c * P:(c + 1) * P], ones[:, 0:1], start=True, stop=True)
            return ins

        def half_spread(dst, col, h):
            for c in range(4 * h, 4 * h + 4):
                ins = MM(dst[:, c * P:(c + 1) * P], sm[:, col + c:col + c + 1].to_broadcast([P, P]), ident[:], start=True, stop=True)
            return ins

        def spread(dst, col):
            for c in range(C):
                ins = MM(dst[:, c * P:(c + 1) * P], sm[:, col + c:col + c + 1].to_broadcast([P, P]), ident[:], start=True, stop=True)
            return ins

        pe.wait_ge(cst, 1)
        def first_sums(h):
            pe.wait_ge((first_acc, sq_used)[h], KT)
            half_sums(acc_a, 0, h).then_inc(stat_done, 1)

        def first_spread(h):
            pe.wait_ge(rstd_done, 1 + h)
            half_spread(wka, 0, h).then_inc(spread_done, 1)

        pe.wait_ge(p_lo_done, 2)
        for n in range(KT):
            w, nt = n // 4, n % 4
            pe.wait_ge(w_split, S_PLE + w + 1)
            if n >= 2:
                pe.wait_ge(evac_done, n - 1)
            for k in range(2):
                for m, (wt, x) in enumerate(((w_hi, p_hi), (w_hi, p_lo), (w_lo, p_hi))):
                    for h in range(2):
                        lhs = wt[:, w, (nt * 2 + k) * P:(nt * 2 + k + 1) * P]
                        ins = MM(pt[:, n % 2, h * HALF:(h + 1) * HALF], lhs, x[:, k, h * HALF:(h + 1) * HALF],
                                 start=k == 0 and m == 0, stop=k == 1 and m == 2)
            ins.then_inc(ple_done, 1)
            if nt == 3:
                pe.wait_ge(ple_done, n + 1)
                pe.sem_inc(mm_done, 1)
            if n == 2:
                first_sums(0)
            if n == 4:
                first_spread(0)

        def in_xbc(n):
            if n == 3:
                first_sums(1)
            if n == 11:
                first_spread(1)

        pair_by_half(S_XBC, N_XBC, (xh, xl), 0, 0, in_xbc, tile_first=True)
        pe.wait_ge(sml_in, 48)
        narrow(0, wdt_raw, (xh, xl)).then_inc(dt_mm, 1)
        pair(1, S_XBC, N_XBC, (xh, xl))
        pe.wait_ge(dt_sb, 1)
        for c in range(C):
            ins = nc.tensor.transpose(wk[:, 3, c * HEADS:(c + 1) * HEADS], dtf[0:HEADS, c * P:(c + 1) * P], ident[0:HEADS, 0:HEADS])
        ins.then_inc(dt_mm, 1)
        with pe.Fori(2, XBC_T // 2 - 1) as j:
            pair(j, S_XBC, N_XBC, (xh, xl))
        pe.wait_ge(adt_done, 1)
        flat = adt[:].rearrange("p c h -> p (c h)")
        MM(wk[:, 3, 0:P], tri[:], flat, start=True, stop=True)
        MM(wk[:, 3, P:2 * P], ones[:, 0:1].to_broadcast([P, P]), flat, start=True, stop=True)
        MM(wk[:, 3, 2 * P:3 * P], flat, tri[:], start=True, stop=True).then_inc(acs_mm, 1)
        pair(XBC_T // 2 - 1, S_XBC, N_XBC, (xh, xl))
        pe.wait_ge(dec_done, 3)
        pe.wait_ge(dec_arg, 1)
        with pe.Fori(0, C) as j:
            S, N = j * 4 + S_SC, j * 4 + N_SC
            project(S, N - 1, 0, 0, (xh, xl))
            pe.wait_ge(stage_done, j + 1)
            pe.wait_ge(s_ready, j)
            pe.wait_ge(y_evac, j)
            for i in range(KT):
                nc.tensor.transpose(wka[:, i * P:(i + 1) * P], st[:, i, :], ident[:])
            nc.tensor.transpose(wk[:, 2, 0:P], st[:, KT, :], ident[:])
            for g in range(GROUPS):
                r = slice(g * 64, g * 64 + 64)
                ins = MM(wk[:, 2, P:2 * P] if g == 0 else wk[:, 3, 0:P], st[r, KT, :], st[r, KT + 1, :], start=True, stop=True)
            ins.then_inc(ssd_a, 1)
            project(S + 1, N, 1, 1, (xh, xl))
            pe.wait_ge(m_ready, j + 1)
            pe.wait_ge(xdd_done, j + 1)
            pe.wait_ge(ce_done, j + 1)
            pe.wait_ge(s_ready, j)
            pe.wait_ge(bt_done, j + 1)
            for h in range(HEADS):
                o = wka[(h % 2) * 64:(h % 2) * 64 + 64, (h // 2) * P:(h // 2 + 1) * P]
                MM(o, xd[:, h, :], rowb[:, h, :], start=True, stop=False)
                MM(o, state[:, h, :], ce[:, h % HG, :], start=False, stop=True)
            for g in range(GROUPS):
                ins = MM(wk[g * 64:g * 64 + 64, 3, :], bt[:, g * 64:g * 64 + 64],
                         xdd[:, g * HG:(g + 1) * HG, :].rearrange("p h q -> p (h q)"), start=True, stop=True)
            ins.then_inc(ssd_b, 1)
            project(S + 2, N + 1, 0, 0, (xh, xl))
            project(S + 3, N + 2, 1, 1, (xh, xl))

        pair(0, S_SB, N_SB, (xh, xl))
        pair(1, S_SB, N_SB, (xh, xl))
        pe.wait_ge(sq_used, 2 * KT)
        pe.wait_ge(s_ready, C)
        pe.wait_ge(y_evac, C)
        sums(acc_g[:, 0, :], 0)
        sums(acc_g[:, 1, :], 8).then_inc(stat_done, 1)
        pair(2, S_SB, N_SB, (xh, xl))
        pe.wait_ge(rstd_done, 3)
        spread(wka, 0)
        spread(wkb, 8).then_inc(spread_done, 1)
        pair(3, S_SB, N_SB, (xh, xl))
        def mixer(j, u):
            project(j * 4 + (S_OUT + 2 * u), j * 2 + (N_OUT + u - 1), 0, u, (sh, sl), (lo_done, KT), last=False)
            project(j * 4 + (S_OUT + 2 * u + 1), None, 1, u, (yh, yl), (lo_done, 2 * KT), first=False)

        with pe.Fori(0, KT // 2 - 1) as j:
            for u in range(2):
                mixer(j, u)
        mixer(KT // 2 - 1, 0)

        def mixer_sums(h, ready):
            pe.wait_ge(*ready)
            half_sums(acc_a, 0, h).then_inc(stat_done, 1)

        def mixer_spread(h):
            pe.wait_ge(rstd_done, 4 + h)
            half_spread(wka, 0, h).then_inc(spread_done, 1)

        pe.wait_ge(w_split, S_OUT + 2 * KT - 1)
        pe.wait_ge(evac_done, N_OUT + KT - 2)
        project_half(0, 1, (sh, sl), 0, last=False)
        pe.wait_ge(w_split, S_OUT + 2 * KT)
        project_half(1, 1, (yh, yl), 0, first=False).then_inc(half_mm, 1)
        project_half(0, 1, (sh, sl), 1, last=False,
                     between=lambda k: mixer_sums(0, (half_acc, 1)) if k == 6 else None).then_inc(mm_done, 1)
        project_half(1, 1, (yh, yl), 1, first=False, between=lambda k: mixer_spread(0) if k == 2 else None).then_inc(mm_done, 1)

        def in_gate(n):
            if n == 0:
                mixer_sums(1, (sq_used, 3 * KT))
            if n == 8:
                mixer_spread(1)

        pair_by_half(S_GATE, N_GATE, (xh, xl), KT, 3 * KT, in_gate)
        with pe.Fori(1, KT // 2) as j:
            pair(j, S_GATE, N_GATE, (xh, xl))
        x2 = (h2, l2)
        def turn(u, used):
            pe.wait_ge(tr_used, used)
            for c in range(C):
                ins = nc.tensor.transpose(wka[:, c * P:(c + 1) * P], ebuf[:, u, c * P:(c + 1) * P], ident[:])
            ins.then_inc(tr_done, 1)

        project(S_AV, N_AV - 1, 0, 0, x2, (lo_done, 4 * KT))
        with pe.Fori(0, KT // 2 - 1) as j:
            project(j * 2 + (S_AV + 1), j * 2 + N_AV, 1, 1, x2)
            pe.wait_ge(evac_done, j * 2 + (N_AV + 1))
            turn(0, j * 2)
            project(j * 2 + (S_AV + 2), j * 2 + (N_AV + 1), 0, 0, x2)
            pe.wait_ge(evac_done, j * 2 + (N_AV + 2))
            turn(1, j * 2 + 1)
        pe.wait_ge(ws_done, 1)
        for h in range(2):
            ins = MM(wk[:, 2 + h, :], ones[:, 0:1].to_broadcast([P, P]),
                     wst[:, 4 * h:4 * h + 4, :].rearrange("p g t -> p (g t)"), start=True, stop=True)
        ins.then_inc(row_mm, 1)
        project(S_AV + KT - 1, N_AV + KT - 2, 1, 1, x2)
        pe.wait_ge(evac_done, N_AV + KT - 1)
        turn(0, KT - 2)
        pe.wait_ge(b2_in, 96)
        pe.wait_ge(rg_done, 1)
        narrow(2, wl_raw, x2).then_inc(low_mm, 1)
        pe.wait_ge(evac_done, N_AV + KT)
        turn(1, KT - 1)
        pe.wait_ge(tr_used, KT)
        with pe.Fori(0, KT // 2) as j:
            for u in range(2):
                i = j * 2 + u
                pe.wait_ge(alc_done, i + 1)
                pe.wait_ge(z_dve, i)
                MM(wk[:, 0, :], alc[0:RANK + 1, u, :], wg2[0:RANK + 1, :], start=True, stop=True).then_inc(z_mm, 1)
                project(j * 2 + (S_QK + u), j * 2 + (N_QK + u - 1), u, u, x2)
                pe.wait_ge(z_dve, i + 1)
                pe.wait_ge(cu_done, i)
                for h in range(GH):
                    ins = MM(wk[:, 1, h * P:(h + 1) * P], gm_[:, h * P:(h + 1) * P], tri[:], start=True, stop=True)
                ins.then_inc(cu_mm, 1)
        pe.wait_ge(cu_done, C)

        def mix_tokens(g):
            pe.wait_ge(av_done, C)
            if g:
                pe.wait_ge(mix_done, g)
            for c in range(C):
                ins = MM(wkb[:, c * P:(c + 1) * P], av[:, c, g * P:(g + 1) * P], wst[:, g, :], start=True, stop=True)
            ins.then_inc(mix_mm, 1)

        for i in range(KT):
            project(S_VAL + i, N_VAL + i - 1, i % 2, i % 2, x2)
            if i:
                pe.wait_ge(evac_done, N_VAL + i)
                turn((i - 1) % 2, KT + i - 1)
                mix_tokens(i - 1)
        mix_tokens(KT - 1)
        pe.wait_ge(evac_done, N_VAL + KT)
        turn(1, 2 * KT - 1)
        with pe.Fori(0, C // 2) as j:
            for u in range(2):
                i = j * 2 + u
                S, N = j * 6 + (S_G + 3 * u), j * 6 + (N_G + 3 * u)
                slots = [(u + n) % 2 for n in range(3)]

                def level(n):
                    pe.wait_ge(lev_ready, i * 7 + n + 1)
                    if n >= 2:
                        pe.wait_ge(lev_used, i * 7 + n - 1)
                    m = LEVELS[n]
                    width = min(max(2 * m, 32), 64)
                    groups = 1 if m == 64 else P // width
                    for h in range(GH):
                        for g in range(groups):
                            t = slice(g * 64 // groups, (g + 1) * 64 // groups)
                            ins = MM(wk[g * width:(g + 1) * width, n % 2, h * 64 + t.start:h * 64 + t.stop],
                                     kp[:, n % 2, h, g * width:(g + 1) * width], qc[:, n % 2, h, t], start=True, stop=True,
                                     tile_position=(0, g * width))
                    ins.then_inc(lev_mm, 1)

                def in_ga(k):
                    if k == 0:
                        pe.wait_ge(ch_in, i * 32 + 32)
                        pe.wait_ge(gst_done, i + 1)
                        for h in range(GH):
                            ins = MM(wk[:, 2, h * P:(h + 1) * P], qkc[:, 1, h, :], qkc[:, 0, h, :], start=True, stop=True)
                        ins.then_inc(dg_mm, 1)
                    if k == 1:
                        pe.wait_ge(on_done, i)
                    if k in (3, 5, 7):
                        level((k - 3) // 2)

                def in_r(k):
                    if k in (1, 3, 5, 7):
                        level(3 + (k - 1) // 2)
                    if k == 6:
                        pe.wait_ge(kd_done, i + 1)
                        for h in range(GH):
                            ins = nc.tensor.transpose(wk[:, 3, h * P:(h + 1) * P], kd[:, h, :], ident[:])
                        ins.then_inc(kdt_mm, 1)

                def in_gb(k):
                    if k == 1:
                        pe.wait_ge(lev_used, i * 7 + 7)
                        pe.wait_ge(sc_done, i + 1)
                        pe.wait_ge(vc_in, i * 16 + 16)
                        for v in range(8):
                            h = v // 2
                            o = wka[:, v * P:(v + 1) * P]
                            MM(o, vc[:, v * P:(v + 1) * P], sc[:, h, :], start=True, stop=False)
                            ins = MM(o, gst[:, h, (v % 2) * P:(v % 2 + 1) * P], qe[:, h, :], start=False, stop=True)
                        ins.then_inc(o_mm, 1)
                        pe.wait_ge(kdt_done, i + 1)
                        for h in range(GH):
                            ins = MM(wk[:, 2 + h // 2, (h % 2) * GV:(h % 2 + 1) * GV], kdt[:, h, :], vc[:, h * GV:(h + 1) * GV],
                                     start=True, stop=True)
                        ins.then_inc(su_mm, 1)
                    if k == 4:
                        pe.wait_ge(o_sum, i + 1)
                        for h in range(GH):
                            ins = MM(wk[:, 0, h:h + 1], osq[:, 2 * h, :], ones[:, 0:1], start=True, stop=True)
                        ins.then_inc(o_stat, 1)
                    if k == 7:
                        pe.wait_ge(o_rstd, i + 1)
                        for h in range(GH):
                            ins = MM(wk[:, 1, h * P:(h + 1) * P], sm[:, h:h + 1].to_broadcast([P, P]), ident[:], start=True, stop=True)
                        ins.then_inc(o_spread, 1)

                project(S, N - 1, u, slots[0], x2, between=in_ga)
                project(S + 1, N, 1 - u, slots[1], x2, between=in_r)
                project(S + 2, N + 1, u, slots[2], x2, between=in_gb)
        with pe.Fori(0, KT // 2) as j:
            pair(j, S_U, N_U, x2)
        def ln_sums(h, ready):
            pe.wait_ge(*ready)
            half_sums(acc_a, 0, h)
            half_sums(acc_b, 8, h).then_inc(stat_done, 1)

        def ln_spread(h, n):
            pe.wait_ge(rstd_done, n)
            half_spread(wka, 0, h)
            half_spread(wkb, 8, h).then_inc(spread_done, 1)

        def last_pair(S, N, xs, halves, n, k_ready=None):
            pe.wait_ge(w_split, S + 1)
            pe.wait_ge(evac_done, N - 1)
            if k_ready is not None:
                pe.wait_ge(*k_ready)
            project_half(0, 0, xs, 0).then_inc(half_mm, 1)
            pe.wait_ge(w_split, S + 2)
            pe.wait_ge(evac_done, N)
            project_half(1, 1, xs, 0).then_inc(half_mm, 1)
            project_half(0, 0, xs, 1, between=lambda k: ln_sums(0, (half_acc, halves)) if k == 6 else None).then_inc(mm_done, 1)
            project_half(1, 1, xs, 1, between=lambda k: ln_spread(0, n) if k == 2 else None).then_inc(mm_done, 1)

        with pe.Fori(0, KT // 2 - 1) as j:
            pair(j, S_OUT2, N_OUT2, (mh, ml), (lo_done, 5 * KT))
        last_pair(S_OUT2 + KT - 2, N_OUT2 + KT - 2, (mh, ml), 3, 7)

        def in_ff(n):
            if n == 0:
                ln_sums(1, (a_used, KT))
            if n == 8:
                ln_spread(1, 8)

        def ff2(b, pairs):
            with pe.Fori(0, pairs) as j:
                for u in range(2):
                    project(b * 16 + j * 2 + (S_FF + 8 + u), b * 16 + j * 2 + (N_FF + 8 + u - 1), u, u, (fh, fl),
                            (f_lo, b * KT))

        def ff1(b, first=0):
            with pe.Fori(first, KT // 2) as j:
                for u in range(2):
                    project(b * 16 + j * 2 + (S_FF + u), b * 16 + j * 2 + (N_FF + u - 1), u, u, x2)

        pair_by_half(S_FF, N_FF, x2, 2 * KT, 6 * KT, in_ff)
        ff1(0, 1)
        ff2(0, KT // 2)
        with pe.Fori(1, FF_BLOCKS - 1) as b:
            ff1(b)
            ff2(b, KT // 2)
        ff1(FF_BLOCKS - 1)
        ff2(FF_BLOCKS - 1, KT // 2 - 1)
        last_pair(S_ALL - 2, N_FF + 16 * FF_BLOCKS - 2, (fh, fl), 5, 9)
        ln_sums(1, (a_used, KT + FF_BLOCKS * KT))
        ln_spread(1, 10)
    ctx.close()


def kernel(**inputs):
    import numpy as _np
    import concourse.bacc as _bacc
    from concourse import mybir as _mybir
    from concourse.bass_utils import run_bass_kernel_spmd as _run

    a = {k: _np.asarray(v) for k, v in inputs.items()}
    w_in, w_in2 = a["w_in"][0], a["w_in_2"][0]

    def tiles(w):
        k, n = w.shape
        return w.reshape(k // 1024, 8, P, n // P, P).transpose(3, 0, 2, 1, 4).reshape(-1, P, 1024)

    def mixed(*ws):
        t = [tiles(w) for w in ws]
        return _np.stack(t, 1).reshape(-1, P, 1024)

    o = XBC_T * P + HEADS
    z, sc_h, sc_b, sc_c, z_sc = (w_in[:, o + i * D:o + (i + 1) * D] for i in range(5))
    u_, v_, qk_, val_, r_ = (w_in2[:, i * D:(i + 1) * D] for i in range(5))
    o2 = 5 * D + RANK
    g_a, g_b = w_in2[:, o2:o2 + D], w_in2[:, o2 + D:o2 + 2 * D]
    w_out = a["w_out"][0]
    w_ple = a["w_ple_proj"][0].reshape(2, P, 2, 4, P).transpose(2, 1, 3, 0, 4).reshape(2, P, 1024)
    ff1 = tiles(a["w_ff1_2"][0]).reshape(FF_BLOCKS, 8, P, 1024)
    ff2 = tiles(a["w_ff2_2"][0]).reshape(8, FF_BLOCKS, P, 1024).transpose(1, 0, 2, 3)
    stream = _np.concatenate([
        w_ple, tiles(w_in[:, 0:XBC_T * P]), mixed(z, sc_c, sc_h, z_sc), tiles(sc_b),
        mixed(w_out[D:], w_out[:D]), tiles(a["w_ple_gate"][0]), tiles(v_), tiles(qk_), tiles(val_),
        mixed(g_a, r_, g_b), tiles(u_), tiles(a["w_out_2"][0]),
        _np.concatenate([ff1, ff2], 1).reshape(-1, P, 1024)])
    b_in = a["b_in_2"][0]
    cols = {"norm_pre": a["norm_pre"], "norm_post": a["norm_post"], "conv_w": a["ssd_conv_w"][0], "conv_b": a["ssd_conv_b"],
            "d_skip": _np.repeat(a["d_skip"][0], HP), "ssd_norm": a["ssd_norm"], "sc_w": a["sc_conv_w"][0],
            "b_u": b_in[0:D], "b_v": b_in[D:2 * D], "b_qk": b_in[2 * D:3 * D], "b_val": b_in[3 * D:4 * D],
            "b_r": b_in[4 * D:5 * D], "b_ga": b_in[o2:o2 + D], "b_gb": b_in[o2 + D:o2 + 2 * D],
            "sg_g": a["sg_ln_g_2"], "sg_b": a["sg_ln_b_2"], "gn": a["gla_norm_g_2"], "ln1_g": a["ln1_g_2"],
            "ln1_b": a["ln1_b_2"], "ln2_g": a["ln2_g_2"], "ln2_b": a["ln2_b_2"]}
    vecs = _np.concatenate([cols[n].reshape(-1, P).T for n, _ in VCOLS], 1)
    arrays = {
        "xT": a["x"][0].T, "pT": a["p"][0, 0].T, "ws": stream, "w_dt": w_in[:, XBC_T * P:o],
        "w_low": w_in2[:, 5 * D:o2], "vecs": vecs, "dt_bias": a["dt_bias"], "a_log": a["a_log"],
        "b_low": b_in[5 * D:o2].reshape(RANK, 1), "w_gate2": a["gla_w_gate2_2"][0], "b_gate": a["gla_b_gate_2"],
        "sg_w": a["sg_w_s_2"][0].transpose(2, 0, 1), "sg_bs": a["sg_b_s_2"].reshape(1, D)}
    nc = _bacc.Bacc("TRN2", target_bir_lowering=False, num_devices=1)
    ins, args = {}, []
    for name, x in arrays.items():
        ins[name + "_d"] = _np.ascontiguousarray(x)
        args.append(nc.dram_tensor(name + "_d", x.shape, _mybir.dt.float32, kind="ExternalInput").ap())
    args.append(nc.dram_tensor("outT_d", (D, T), _mybir.dt.float32, kind="ExternalOutput").ap())
    two_blocks_kernel(nc, *args)
    r = _run(nc, [ins], core_ids=[0])
    return _np.ascontiguousarray(r.results[0]["outT_d"].T).reshape(1, T, D)
```
